# Optimizing a Trainium2 kernel written in Bass

```python
import jax, jax.numpy as jnp
from jax import lax
import numpy as np

D_MODEL = 1024
BATCH = 1
SEQ = 1024
DEPTH = 1

POOL_WIDTH = D_MODEL // 2
POOL_GROUPS = 4
POOL_GROUP_DIM = POOL_WIDTH // POOL_GROUPS
POOL_WINDOWS = (2, 4, 8, 16)
N_HEADS = 8
HEAD_DIM = 64
ATTN_WIDTH = N_HEADS * HEAD_DIM
KV_DIM = HEAD_DIM
IDX_HEADS = 8
IDX_DIM = 64
TOPK_MAX = 256
ROPE_THETA = 500000.0
ROT_DIM = HEAD_DIM // 4
Q_BLOCK = 128
EPS = 1e-6

IN_SIZES = (
    POOL_WIDTH,
    POOL_WIDTH,
    ATTN_WIDTH,
    KV_DIM,
    KV_DIM,
    ATTN_WIDTH,
    IDX_HEADS * IDX_DIM,
    IDX_DIM,
    IDX_HEADS,
    D_MODEL,
    D_MODEL,
)
IN_WIDTH = 2 * POOL_WIDTH + 2 * ATTN_WIDTH + 2 * KV_DIM + IDX_HEADS * IDX_DIM + IDX_DIM + IDX_HEADS + 2 * D_MODEL

kernel_name = "hybrid_pool_dsa_gated_block"

def rmsnorm(x, gain):
    xf = x.astype(jnp.float32)
    out = xf * lax.rsqrt(jnp.mean(xf * xf, axis=-1, keepdims=True) + EPS)
    return (out * gain.astype(jnp.float32)).astype(x.dtype)

def rope_tables(positions):
    inv_freq = ROPE_THETA ** (-jnp.arange(0, ROT_DIM, 2, dtype=jnp.float32) / ROT_DIM)
    ang = positions.astype(jnp.float32)[..., None] * inv_freq
    return jnp.cos(ang)[:, :, None, :], jnp.sin(ang)[:, :, None, :]

def apply_partial_rope(x, cos, sin):
    half = ROT_DIM // 2
    x1 = x[..., :half].astype(jnp.float32)
    x2 = x[..., half:ROT_DIM].astype(jnp.float32)
    rot = jnp.concatenate([x1 * cos - x2 * sin, x2 * cos + x1 * sin], axis=-1)
    return jnp.concatenate([rot.astype(x.dtype), x[..., ROT_DIM:]], axis=-1)

def multiscale_pool(u, w_group, scale):
    B, L, _ = u.shape
    ug = u.reshape(B, L, POOL_GROUPS, POOL_GROUP_DIM).astype(jnp.float32)
    cs = jnp.cumsum(ug, axis=1)
    cs_pad = jnp.concatenate([jnp.zeros_like(cs[:, :1]), cs], axis=1)
    t = jnp.arange(L)
    groups = []
    for g, w in enumerate(POOL_WINDOWS):
        start = jnp.maximum(t + 1 - w, 0)
        win_sum = cs[:, :, g] - cs_pad[:, start, g]
        count = (t + 1 - start).astype(jnp.float32)[None, :, None]
        groups.append(win_sum / count - ug[:, :, g])
    pooled = jnp.stack(groups, axis=2).astype(u.dtype)
    mixed = jnp.einsum('blgc,gcd->blgd', pooled, w_group)
    return mixed.reshape(B, L, POOL_WIDTH) * scale

def dsa_sparse_attention(q, k, v, q_idx, k_idx, w_idx):
    B, L = q.shape[0], q.shape[1]
    n_blk = L // Q_BLOCK
    top_k = min(TOPK_MAX, L // 4)
    attn_scale = HEAD_DIM ** -0.5
    key_pos = jnp.arange(L)
    k_idx_f = k_idx.astype(jnp.float32)

    def to_blocks(a):
        return a.reshape((B, n_blk, Q_BLOCK) + a.shape[2:]).swapaxes(0, 1)

    def block(args):
        qb, qib, wb, blk = args
        tq = blk * Q_BLOCK + jnp.arange(Q_BLOCK)
        s = jax.nn.relu(jnp.einsum('bqhd,bsd->bqhs', qib.astype(jnp.float32), k_idx_f))
        score = jnp.einsum('bqhs,bqh->bqs', s, wb.astype(jnp.float32))
        causal = key_pos[None, :] <= tq[:, None]
        score = jnp.where(causal[None], score, -jnp.inf)
        _, idx = lax.top_k(score, top_k)
        k_sel = jax.vmap(lambda kb, ib: kb[ib])(k, idx)
        v_sel = jax.vmap(lambda vb, ib: vb[ib])(v, idx)
        logits = jnp.einsum('bqhd,bqkd->bqhk', qb, k_sel).astype(jnp.float32) * attn_scale
        valid = idx <= tq[None, :, None]
        logits = jnp.where(valid[:, :, None, :], logits, -jnp.inf)
        p = jax.nn.softmax(logits, axis=-1).astype(v.dtype)
        return jnp.einsum('bqhk,bqkd->bqhd', p, v_sel)

    out = lax.map(block, (to_blocks(q), to_blocks(q_idx), to_blocks(w_idx), jnp.arange(n_blk)))
    return out.swapaxes(0, 1).reshape(B, L, N_HEADS * HEAD_DIM)

def setup_inputs(seed: int = 0) -> dict:
    key = jax.random.key(seed)
    ks = jax.random.split(key, 16)
    f32 = jnp.float32
    x = jax.random.normal(ks[0], (BATCH, SEQ, D_MODEL), f32)
    c = jax.random.normal(ks[1], (BATCH, D_MODEL), f32)
    offsets = jax.random.randint(ks[2], (BATCH, 1), 0, 1024, dtype=jnp.int32)
    positions = offsets + jnp.arange(SEQ, dtype=jnp.int32)[None, :]
    w_ada = jax.random.normal(ks[3], (DEPTH, D_MODEL, 3 * D_MODEL), f32) * (0.5 * D_MODEL ** -0.5)
    b_ada = jax.random.normal(ks[4], (DEPTH, 3 * D_MODEL), f32) * 0.02
    norm_gain = 1.0 + 0.02 * jax.random.normal(ks[5], (DEPTH, D_MODEL), f32)
    w_in = jax.random.normal(ks[6], (DEPTH, D_MODEL, IN_WIDTH), f32) * D_MODEL ** -0.5
    w_pool_group = jax.random.normal(ks[7], (DEPTH, POOL_GROUPS, POOL_GROUP_DIM, POOL_GROUP_DIM), f32) * POOL_GROUP_DIM ** -0.5
    pool_scale = 1.0 + 0.02 * jax.random.normal(ks[8], (DEPTH, POOL_WIDTH), f32)
    q_norm_gain = 1.0 + 0.02 * jax.random.normal(ks[9], (DEPTH, HEAD_DIM), f32)
    k_norm_gain = 1.0 + 0.02 * jax.random.normal(ks[10], (DEPTH, HEAD_DIM), f32)
    w_branch_a = jax.random.normal(ks[11], (DEPTH, POOL_WIDTH, D_MODEL), f32) * POOL_WIDTH ** -0.5
    w_branch_b = jax.random.normal(ks[12], (DEPTH, ATTN_WIDTH, D_MODEL), f32) * ATTN_WIDTH ** -0.5
    w_out = jax.random.normal(ks[13], (DEPTH, D_MODEL, D_MODEL), f32) * D_MODEL ** -0.5
    return {"x": x, "c": c, "positions": positions, "w_ada": w_ada, "b_ada": b_ada,
            "norm_gain": norm_gain, "w_in": w_in, "w_pool_group": w_pool_group,
            "pool_scale": pool_scale, "q_norm_gain": q_norm_gain, "k_norm_gain": k_norm_gain,
            "w_branch_a": w_branch_a, "w_branch_b": w_branch_b, "w_out": w_out}

def reference(x, c, positions, w_ada, b_ada, norm_gain, w_in, w_pool_group, pool_scale,
              q_norm_gain, k_norm_gain, w_branch_a, w_branch_b, w_out):
    B, L, _ = x.shape
    cos, sin = rope_tables(positions)
    split_points = tuple(int(s) for s in np.cumsum(IN_SIZES)[:-1])
    idx_w_scale = (IDX_HEADS ** -0.5) * (IDX_DIM ** -0.5)
    for layer in range(DEPTH):
        mod = jax.nn.silu(c) @ w_ada[layer] + b_ada[layer]
        shift, scale, gate = jnp.split(mod, 3, axis=-1)
        h = rmsnorm(x, norm_gain[layer]) * (1.0 + scale[:, None, :]) + shift[:, None, :]

        proj = h @ w_in[layer]
        (u_a, z_a, q, k, v, z_b, q_idx, k_idx, w_idx, g_a, g_b) = jnp.split(proj, split_points, axis=-1)

        y_a = multiscale_pool(u_a, w_pool_group[layer], pool_scale[layer]) * jax.nn.silu(z_a)

        q = apply_partial_rope(rmsnorm(q.reshape(B, L, N_HEADS, HEAD_DIM), q_norm_gain[layer]), cos, sin)
        k = apply_partial_rope(rmsnorm(k.reshape(B, L, 1, KV_DIM), k_norm_gain[layer]), cos, sin)[:, :, 0]
        q_idx = apply_partial_rope(q_idx.reshape(B, L, IDX_HEADS, IDX_DIM), cos, sin)
        k_idx = apply_partial_rope(k_idx.reshape(B, L, 1, IDX_DIM), cos, sin)[:, :, 0]
        attn = dsa_sparse_attention(q, k, v, q_idx, k_idx, w_idx * idx_w_scale)
        y_b = attn * jax.nn.silu(z_b)

        merged = jax.nn.sigmoid(g_a) * (y_a @ w_branch_a[layer]) + jax.nn.sigmoid(g_b) * (y_b @ w_branch_b[layer])
        x = x + gate[:, None, :] * (merged @ w_out[layer])
    return x


_drawn_inputs = setup_inputs


def setup_inputs(seed=0):
    import zlib

    import numpy as np

    out = dict(_drawn_inputs(seed))
    spreads = {}
    factors = {'b_ada': 6.435,
     'norm_gain': 8.0,
     'pool_scale': 8.0,
     'q_norm_gain': 8.0,
     'k_norm_gain': 8.0}
    for name, (base, spread) in spreads.items():
        noise = np.random.default_rng([zlib.crc32(name.encode()), seed]).standard_normal(out[name].shape)
        drawn = base * np.exp(spread * noise) if base else spread * noise
        out[name] = __import__('jax').numpy.asarray(drawn.astype(out[name].dtype))
    for name, factor in factors.items():
        out[name] = (out[name] * factor).astype(out[name].dtype)
    return out
```

```python
from contextlib import ExitStack

import numpy as np
import concourse.bass as bass
from concourse import mybir

F32, F32R, BF16, I32, U8 = (mybir.dt.float32, mybir.dt.float32r, mybir.dt.bfloat16, mybir.dt.int32, mybir.dt.uint8)
ACT, ALU, AX = mybir.ActivationFunctionType, mybir.AluOpType, mybir.AxisListType

P = 128
D = 1024
L = 1024
NT = L // P
KD = D // P
HALF = 512
H, HD = 8, 64
ROT = HD // 4
NF = ROT // 2
THETA = 500000.0
TOPK = min(256, L // 4)
FREE_BLOCKS = TOPK // P
NSEL = NT - FREE_BLOCKS
EPS = 1e-6
GROUPS = 4
KA = 512 // P
CW = 256
IDX_SCALE = float(H ** -0.5 * HD ** -0.5)
ATT_SCALE = float(HD ** -0.5)
MAGIC = 12582912.0
TWO_PI = (6.28125, 0.0019340515136718750, 1.2556416e-06)
MASKED = -3.0e38
NEG_BIAS = -1.0e30

O_UA, O_ZA, O_Q, O_K, O_V, O_ZB, O_QI, O_KI, O_WI, O_GA, O_GB = (
    0, 512, 1024, 1536, 1600, 1664, 2176, 2688, 2752, 2760, 3784)
KR_KI, KR_WI, KR_K, KR_V, KR_W = 0, 64, 72, 136, 200


def keys(b):
    return (b + 1) * P


def score_at(b):
    return P * sum(j + 1 for j in range(FREE_BLOCKS, b))


def bias_at(b):
    return P * sum(j + 1 for j in range(b))


def hybrid_layer(nc, x, c, positions, w_ada, b_ada, norm_gain, w_in, w_pool_group, pool_scale,
                 q_norm_gain, k_norm_gain, w_branch_a, w_branch_b, w_out, out):
    x, out = x[0], out[0]
    w_ada, w_in, w_group = w_ada[0], w_in[0], w_pool_group[0]
    w_branch_a, w_branch_b, w_out = w_branch_a[0], w_branch_b[0], w_out[0]

    def cols(src, first, kt=KD):
        return (kt, [(src, first, CW, 0)])
    chunks, name_of = [], {}

    def add(name, chunk):
        name_of[name] = len(chunks)
        chunks.append(chunk)
    for i in range(2):
        add(("qi", i), cols(w_in, O_QI + CW * i))
    add("kv", (KD, [(w_in, O_KI, KR_K, 0), (w_in, O_K, 2 * HD, KR_K)]))
    for i in range(2):
        add(("q", i), cols(w_in, O_Q + CW * i))
    for i in range(2):
        add(("zb", i), cols(w_in, O_ZB + CW * i))
    C_ORDER = [("ua", 0), ("gb", 0), ("gb", 1), ("ua", 1), ("gb", 2), ("gb", 3)]
    for kind, i in C_ORDER:
        add((kind, i), cols(w_in, (O_UA if kind == "ua" else O_GB) + CW * i))
    for i in range(2):
        add(("za", i), cols(w_in, O_ZA + CW * i))
    for i in range(4):
        add(("ga", i), cols(w_in, O_GA + CW * i))
        add(("wa", i), cols(w_branch_a, CW * i, KA))
    for i in range(4):
        add(("wb", i), cols(w_branch_b, CW * i, KA))
    for i in range(4):
        add(("wo", i), cols(w_out, CW * i))
    pieces = [(ci, p) for ci, (kt, _) in enumerate(chunks) for p in range(kt // 4)]
    pieces_through = [sum(k // 4 for k, _ in chunks[:ci + 1]) for ci in range(len(chunks))]
    RAW = 2
    raw_ready, got = [], [0] * RAW
    for n, (ci, _) in enumerate(pieces):
        got[n % RAW] += 16 * len(chunks[ci][1])
        raw_ready.append(got[n % RAW])

    pp_uses = []
    QI_TILES = [4, 5, 6, 7, 2, 3]
    ALL_TILES = [4, 5, 6, 7, 0, 1, 2, 3]
    for i in range(2):
        pp_uses += [("qi", i, t) for t in QI_TILES]
    pp_uses += [("kv", 0, t) for t in ALL_TILES]
    for i in range(2):
        pp_uses += [("q", i, t) for t in range(NT)]
    for i in range(2):
        pp_uses += [("zb", i, t) for t in range(NT)]
    UNITS = [(m, f) for m in range(2) for f in range(2)]
    for kind, i in C_ORDER:
        pp_uses += [(kind, i, u) for u in range(4)]
    for i in range(2):
        for m in range(2):
            pp_uses += [("za", i, 2 * m), ("za", i, 2 * m + 1), ("mix", i, 2 * m), ("mix", i, 2 * m + 1)]
    for i in range(4):
        pp_uses += [("ga", i, u) for u in range(4)] + [("wa", i, u) for u in range(4)]
    PP_ACT = len(pp_uses)
    for b in range(NT):
        pp_uses += [("pv", b, 0), ("pv", b, 1)]
    for i in range(4):
        pp_uses += [("wb", i, u) for u in range(4)]
    for i in range(4):
        pp_uses += [("wo", i, t) for t in range(NT)]
    pp_at = {use: n for n, use in enumerate(pp_uses)}

    def pp_value(n):
        return n + 1 if n < PP_ACT else n + 1 - 2 * NT

    def chunk_done(ci):
        name = [k for k, v in name_of.items() if v == ci][0]
        kind, i = name if isinstance(name, tuple) else (name, 0)
        return max(pp_value(n) for n, use in enumerate(pp_uses)
                   if use[:2] == (kind, i) or (kind == "za" and use[:2] == ("mix", i)))

    HEADS = NT * H
    MASK_UNIT = {12 + 3 * n: FREE_BLOCKS + n for n in range(NSEL)}
    GATE_ADD = {24 + 2 * k: (0, k) for k in range(KD)} | {46 + 2 * k: (1, k) for k in range(KD)}
    GATE_STEP = {40: 0, 62: 1}
    pt_uses = [("cols", "v"), ("gains", "v")]
    pt_uses += [(("h", n), "v") for n in range(2 * KD)]
    pt_uses += [(("ki", s, f), "a") for s in range(2) for f in range(2)]
    pt_uses += [(("k", s, f), "a") for s in range(2) for f in range(2)]
    pt_uses += [(("qi", b, g), "a") for b in range(FREE_BLOCKS, NT) for g in range(2)]
    pt_uses += [(("eqT", b), "a") for b in range(FREE_BLOCKS, NT)]
    pt_uses += [(("qT", 0, g), "a") for g in range(2)]
    for i in range(HEADS + 4):
        if 0 <= i - 2 < HEADS:
            for g in range((keys((i - 2) // H) // P + 3) // 4):
                pt_uses.append((("PT", i - 2, g), "av"))
        if i % H == 4 and i // H + 1 < NT:
            pt_uses += [(("qT", i // H + 1, g), "a") for g in range(2)]
        if i in GATE_STEP:
            pt_uses.append((("gate", GATE_STEP[i]), "a"))
        if i >= 11 and (i - 11) % H == 0:
            pt_uses.append((("yb", (i - 11) // H), "av"))
    pt_at, pt_done, na, nv = {}, [], 0, 0
    for n, (key, who) in enumerate(pt_uses):
        pt_at[key] = n
        na += "a" in who
        nv += "v" in who
        pt_done.append((na if "a" in who else 0, nv if "v" in who else 0))

    ps_uses = [("ada", "v")]
    ps_uses += [(("idx", b, h), "a") for b in range(FREE_BLOCKS, NT) for h in range(H)]
    ps_uses += [(("cum", b), "v") for b in range(FREE_BLOCKS, NT)]
    ps_uses += [(("S", i), "v") for i in range(HEADS)]
    ps_at, ps_done, na, nv = {}, [], 0, 0
    for n, (key, who) in enumerate(ps_uses):
        ps_at[key] = n
        na += who == "a"
        nv += who == "v"
        ps_done.append((na if who == "a" else 0, nv if who == "v" else 0))

    def ps_value(key):
        return ps_at[key] + 4

    with ExitStack() as ctx:
        def alloc(stack, name, shape, dt=F32):
            return stack.enter_context(nc.sbuf_tensor(name, shape, dt))

        def sb(name, shape, dt=F32):
            return alloc(ctx, name, shape, dt)

        def sem(name):
            return ctx.enter_context(nc.semaphore(name))

        ident = sb("ident", [P, P])
        ident_b = sb("ident_b", [P, P], BF16)
        prefix = sb("prefix", [P, L], BF16)
        diag_bias = sb("diag_bias", [P, P], BF16)
        ident_r = sb("ident_r", [P, P], F32R)
        ones = sb("ones", [P, P])
        col = sb("col", [P, 28])
        pos_col = sb("pos_col", [P, NT])
        gains = sb("gains", [P, 2 * HD])
        c_col = sb("c_col", [P, KD])
        c_silu = sb("c_silu", [P, KD])
        shift = sb("shift", [P, 2 * KD])
        gmul = sb("gmul", [P, KD])
        rot_c = sb("rot_c", [P, NT, ROT])
        rot_s = sb("rot_s", [P, NT, ROT])
        ssx, rx, nx = sb("ssx", [P, NT]), sb("rx", [P, NT]), sb("nx", [P, NT])
        ssq, rq, nq = sb("ssq", [P, NT * H]), sb("rq", [P, NT * H]), sb("nq", [P, NT * H])
        ssk, rk, nk = sb("ssk", [P, NT]), sb("rk", [P, NT]), sb("nk", [P, NT])
        w_idx = sb("w_idx", [P, NT, H])
        rope_a, rope_b = sb("rope_a", [P, H, ROT]), sb("rope_b", [P, H, ROT])
        recip_n = sb("recip_n", [P, 16])
        wg_hi, wg_lo = sb("wg_hi", [P, GROUPS, P], F32R), sb("wg_lo", [P, GROUPS, P], F32R)
        cnt, thr = sb("cnt", [P, NSEL]), sb("thr", [P, NSEL], I32)
        cand, accept = sb("cand", [P, NSEL], I32), sb("accept", [P, NSEL], I32)
        bit_i, bit_f = sb("bit_i", [P, 32], I32), sb("bit_f", [P, 32])
        need = sb("need", [P, 1])
        neg_max, row_sum, row_inv = sb("neg_max", [P, 2]), sb("row_sum", [P, 2 * H]), sb("row_inv", [P, 4])
        kT = sb("kT", [P, 2, L], F32R)
        v2 = sb("v2", [P, NT, 2 * HD], F32R)
        w_raw = sb("w_raw", [P, RAW, 4, CW])
        w_hi, w_lo = sb("w_hi", [P, 2, KD, CW], F32R), sb("w_lo", [P, 2, KD, CW], F32R)

        def zone(kib, *tenants):
            got = []
            for tenant in tenants:
                with ExitStack() as s:
                    got.append(tenant(s))
            sb(f"zone_{kib}".replace(".", "_"), [P, int(kib * 256)])
            return got

        ada_w, (hT_hi, hT_lo), att, (mT_hi, mT_lo) = zone(
            64,
            lambda s: alloc(s, "ada_w", [P, 4, KD, HALF]),
            lambda s: (alloc(s, "hT_hi", [P, KD, L], F32R), alloc(s, "hT_lo", [P, KD, L], F32R)),
            lambda s: dict(
                q_row=alloc(s, "q_row", [P, 2, H * HD]), z_row=alloc(s, "z_row", [P, 2, H * HD]),
                q_stk=alloc(s, "q_stk", [P, 2, H, 2 * HD], F32R), qT=alloc(s, "qT", [P, 2, H, P], F32R),
                logit=alloc(s, "logit", [P, 2, L]), prob=alloc(s, "prob", [P, 2, L]),
                pT_hi=alloc(s, "pT_hi", [P, 2, NT, P], F32R), pT_lo=alloc(s, "pT_lo", [P, 2, NT, P], F32R),
                o_lo=alloc(s, "o_lo", [P, 4, HD]), y_row=alloc(s, "y_row", [P, H * HD]),
                gate_acc=alloc(s, "gate_acc", [P, HALF])),
            lambda s: (alloc(s, "mT_hi", [P, KD, L], F32R), alloc(s, "mT_lo", [P, KD, L], F32R)))
        def tenants_start(s):
            return (alloc(s, "h_raw", [P, 4, HALF]), alloc(s, "wg_raw", [P, GROUPS, P]),
                    alloc(s, "col_rows", [28, P]),
                    alloc(s, "pos_i", [NT, P], I32), alloc(s, "pos_f", [NT, P]), alloc(s, "gain_row", [1, 2 * HD]),
                    alloc(s, "angle", [P, NT, NF]), alloc(s, "turns", [P, 2, NT * NF]),
                    alloc(s, "reduced", [P, 2, NT * NF]), alloc(s, "trig", [P, 2, NT * NF]))
        (h_raw, wg_raw, col_rows, pos_i, pos_f, gain_row, angle, turns, reduced, trig), score, gate_w, (x_row, o_row) = zone(
            16.5, tenants_start,
            lambda s: alloc(s, "score", [P, score_at(NT)]),
            lambda s: alloc(s, "gate_w", [P, KD, HALF]),
            lambda s: (alloc(s, "x_row", [P, 4, CW]), alloc(s, "o_row", [P, 4, CW])))

        def tenants_first(s):
            return alloc(s, "x_in", [P, NT, D])

        def tenants_a(s):
            q, qi = alloc(s, "q_all", [P, NT, H * HD]), alloc(s, "qi", [P, NSEL, H * HD])
            kiT = alloc(s, "kiT", [P, 2, L], F32R)
            qi_stk = alloc(s, "qi_stk", [P, H, 2 * HD], F32R)
            qiT = alloc(s, "qiT", [P, 2, H, P], F32R)
            with ExitStack() as k:
                kr, kst = alloc(k, "kr", [P, NT, KR_W]), alloc(k, "kst", [P, 2, NT, P], F32R)
            with ExitStack() as k:
                rel, zb_out = alloc(k, "rel", [P, 2, L]), alloc(k, "zb_out", [P, 4, CW])
            return q, qi, kiT, qi_stk, qiT, kr, kst, rel, zb_out

        def tenants_c(s):
            yT_hi, yT_lo = alloc(s, "yT_hi", [P, KA, L], F32R), alloc(s, "yT_lo", [P, KA, L], F32R)
            with ExitStack() as k:
                ua, win = alloc(k, "ua", [P, 2, L]), alloc(k, "win", [P, 2, L])
            with ExitStack() as k:
                z_silu, mixed = alloc(k, "z_silu", [P, 2, L]), alloc(k, "mixed", [P, 2, HALF])
            with ExitStack() as k:
                bias, a_out = alloc(k, "bias", [P, bias_at(NT)], BF16), alloc(k, "a_out", [P, 2, HALF])
            with ExitStack() as k:
                e_in = alloc(k, "e_in", [P, 2, 4, HALF])
            alloc(s, "zone_c", [P, 16 * 256])
            with ExitStack() as k:
                stage = alloc(k, "stage", [P, 4, HALF])
            with ExitStack() as k:
                m_raw = alloc(k, "m_raw", [P, 4, HALF])
            alloc(s, "zone_s", [P, 8 * 256])
            with ExitStack() as k:
                junk = alloc(k, "junk", [P, 2, L], U8)
            with ExitStack() as k:
                gt, eq, eqT = (alloc(k, n, [P, L], BF16) for n in ("gt", "eq", "eqT"))
            with ExitStack() as k:
                gate = alloc(k, "gate", [P, D])
            alloc(s, "zone_m", [P, 6 * 256])
            return yT_hi, yT_lo, ua, win, z_silu, mixed, bias, a_out, e_in, stage, gt, eq, eqT, m_raw, junk, gate

        x_in, ta, tc = zone(62.5, tenants_first, tenants_a, tenants_c)
        q_all, qi, kiT, qi_stk, qiT, kr, kst, rel, zb_out = ta
        yT_hi, yT_lo, ua, win, z_silu, mixed, bias, a_out, e_in, stage, gt, eq, eqT, m_raw, junk, gate = tc
        q_row, z_row, q_stk, qT = att["q_row"], att["z_row"], att["q_stk"], att["qT"]
        logit, prob, pT_hi, pT_lo = att["logit"], att["prob"], att["pT_hi"], att["pT_lo"]
        o_lo, y_row, gate_acc = att["o_lo"], att["y_row"], att["gate_acc"]

        pp = [ctx.enter_context(nc.psum_tensor(f"pp{i}", [P, 512], F32)) for i in range(2)]
        pt = [ctx.enter_context(nc.psum_tensor(f"pt{i}", [P, 512], F32)) for i in range(2)]
        ps = [ctx.enter_context(nc.psum_tensor(f"ps{i}", [P, 1024], F32)) for i in range(2)]

        q_dram = nc.dram_tensor("q_spill", [L, H * HD], F32).ap()
        zb_dram = nc.dram_tensor("zb_spill", [L, H * HD], F32).ap()
        sgb_dram = nc.dram_tensor("sgb_spill", [D, L], F32).ap()
        ma_dram = nc.dram_tensor("ma_spill", [D, L], F32).ap()

        c_in, cols_in, rows_in, group_in = sem("c_in"), sem("cols_in"), sem("rows_in"), sem("group_in")
        x_tile_in = [sem(f"x_tile_in{t}") for t in range(NT)]
        ada_in = [sem(f"ada_in{i}") for i in range(4)]
        raw_in = [sem(f"raw_in{i}") for i in range(RAW)]
        consts = sem("consts")
        dve_ready = sem("dve_ready")
        w_hi_done, w_lo_done = sem("w_hi_done"), sem("w_lo_done")
        pp_full, pp_free_a, pp_free_v = sem("pp_full"), sem("pp_free_a"), sem("pp_free_v")
        pt_full, pt_free_a, pt_free_v = sem("pt_full"), sem("pt_free_a"), sem("pt_free_v")
        ps_full, ps_free_a, ps_free_v = sem("ps_full"), sem("ps_free_a"), sem("ps_free_v")
        c_silu_done, ssx_done, sqrt_done, trig_done = sem("c_silu_done"), sem("ssx_done"), sem("sqrt_done"), sem("trig_done")
        xn_done, h_raw_done = sem("xn_done"), sem("h_raw_done")
        hT_hi_done, hT_lo_v, hT_lo_p = sem("hT_hi_done"), sem("hT_lo_v"), sem("hT_lo_p")
        wg_hi_done, wg_lo_done = sem("wg_hi_done"), sem("wg_lo_done")
        qi_roped, kst_ready = sem("qi_roped"), sem("kst_ready")
        var_ready = sem("var_ready")
        q_scaled, q_roped = sem("q_scaled"), sem("q_roped")
        q_spilled, zb_spilled = sem("q_spilled"), [sem(f"zb_spilled{i}") for i in range(4)]
        qi_hi, qi_lo = sem("qi_hi"), sem("qi_lo")
        rel_used, block_scored, masked = sem("rel_used"), sem("block_scored"), sem("masked")
        silu_b = sem("silu_b")
        sel_done, bisected = sem("sel_done"), sem("bisected")
        pooled, pooled_hi, ua_used, mixed_used = sem("pooled"), sem("pooled_hi"), sem("ua_used"), sem("mixed_used")
        ya_hi, ya_lo, ya_done = sem("ya_hi"), sem("ya_lo"), sem("ya_done")
        stage_full, ma_full = sem("stage_full"), sem("ma_full")
        sgb_out, ma_out = [sem(f"sgb_out{i}") for i in range(4)], [sem(f"ma_out{i}") for i in range(4)]
        q_in, z_in = [sem(f"q_in{i}") for i in range(2)], [sem(f"z_in{i}") for i in range(2)]
        stk_hi, stk_lo = sem("stk_hi"), sem("stk_lo")
        gate_sum, gate_in = sem("gate_sum"), sem("gate_in")
        eq_ready, bias_ready = sem("eq_ready"), sem("bias_ready")
        logit_done, prob_done = sem("logit_done"), sem("prob_done")
        pT_read, pv_done = sem("pT_read"), sem("pv_done")
        o_lo_done, o_sum, y_done = sem("o_lo_done"), sem("o_sum"), sem("y_done")
        e_loaded = [sem(f"e_loaded{i}") for i in range(4)]
        m_raw_done, mT_hi_done, mT_lo_done = sem("m_raw_done"), sem("mT_hi_done"), sem("mT_lo_done")
        x_row_in, o_row_done = [sem(f"x_row_in{i}") for i in range(4)], sem("o_row_done")
        stored = [sem(f"stored{i}") for i in range(4)]
        block = ctx.enter_context(nc.Block())

        def wait_done(eng, done, sem_a, sem_v):
            if done[0]:
                eng.wait_ge(sem_a, done[0])
            if done[1]:
                eng.wait_ge(sem_v, done[1])

        V_POS, V_COL, V_SIN, V_MEAN, V_GAIN, V_MOD, V_BIAS = 1, 2, 3, 4, 5, 6, 7

        @block.sync
        def _(sp):
            sp.dma_start(c_col[:], c.rearrange("a (p k) -> p (a k)", k=KD)).then_inc(c_in, 16)
            sp.dma_start(col_rows[0:8, :], norm_gain.rearrange("a (r p) -> (a r) p", p=P)).then_inc(cols_in, 16)
            sp.dma_start(col_rows[8:12, :], pool_scale.rearrange("a (r p) -> (a r) p", p=P)).then_inc(cols_in, 16)
            sp.dma_start(col_rows[12:28, :], b_ada[:, 0:2 * D].rearrange("a (r p) -> (a r) p", p=P)).then_inc(cols_in, 16)
            sp.dma_start(pos_i[:], positions.rearrange("a (r p) -> (a r) p", p=P)).then_inc(cols_in, 16)
            sp.dma_start(gain_row[:, 0:HD], q_norm_gain).then_inc(rows_in, 16)
            sp.dma_start(gain_row[:, HD:2 * HD], k_norm_gain).then_inc(rows_in, 16)
            ada = w_ada.rearrange("(p k) n -> p k n", k=KD)
            for i in range(4):
                sp.dma_start(ada_w[:, i], ada[:, :, i * HALF:(i + 1) * HALF]).then_inc(ada_in[i], 16)
            sp.dma_start(wg_raw[:], w_group.rearrange("g c d -> c g d")).then_inc(group_in, 16)
            for n, (ci, p) in enumerate(pieces):
                if n >= RAW:
                    sp.wait_ge(w_lo_done, n - RAW + 1)
                for src, first, width, to in chunks[ci][1]:
                    view = src.rearrange("(k p) n -> p k n", p=P)
                    sp.dma_start(w_raw[:, n % RAW, :, to:to + width],
                                 view[:, 4 * p:4 * p + 4, first:first + width]).then_inc(raw_in[n % RAW], 16)

        def split_chunk_hi(act, ci):
            if ci >= len(chunks):
                return
            if ci >= 2:
                act.wait_ge(pp_full, chunk_done(ci - 2))
            for n, (cj, p) in enumerate(pieces):
                if cj == ci:
                    width = sum(w for _, _, w, _ in chunks[ci][1])
                    act.wait_ge(raw_in[n % RAW], raw_ready[n])
                    nc.scalar.activation(w_hi[:, ci % 2, 4 * p:4 * p + 4, 0:width], w_raw[:, n % RAW, :, 0:width],
                                         ACT.Copy).then_inc(w_hi_done, 1)

        def split_chunk_lo(pool, ci):
            if ci >= len(chunks):
                return
            for n, (cj, p) in enumerate(pieces):
                if cj == ci:
                    width = sum(w for _, _, w, _ in chunks[ci][1])
                    pool.wait_ge(w_hi_done, n + 1)
                    nc.gpsimd.tensor_tensor(w_lo[:, ci % 2, 4 * p:4 * p + 4, 0:width], w_raw[:, n % RAW, :, 0:width],
                                            w_hi[:, ci % 2, 4 * p:4 * p + 4, 0:width].bitcast(F32),
                                            ALU.subtract).then_inc(w_lo_done, 1)

        SCALED = {b: {1: 2 * n, 4: 2 * n + 1} if n < 2 else {1: 2 + n} for n, b in enumerate(range(FREE_BLOCKS, NT))}

        POOLED_ROUND = {("gb", 1, 0): 0, ("ua", 1, 1): 1, ("gb", 2, 1): 2, ("gb", 3, 1): 3}

        zb_after = {(b, h): 1 if b == FREE_BLOCKS else 3 for b in range(FREE_BLOCKS, NT) for h in range(H)}
        assert sum(zb_after.values()) == 2 * NT * KD

        @block.tensor
        def _(pe):
            def pp_claim(use):
                n = pp_at[use]
                if n >= 2:
                    if n - 2 < PP_ACT:
                        pe.wait_ge(pp_free_a, n - 1)
                    else:
                        pe.wait_ge(pp_free_v, n - 1 - PP_ACT)
                return pp[n % 2]

            def pt_claim(key):
                n = pt_at[key]
                if n >= 2:
                    wait_done(pe, pt_done[n - 2], pt_free_a, pt_free_v)
                return pt[n % 2]

            def ps_claim(key):
                n = ps_at[key]
                if n >= 2:
                    wait_done(pe, ps_done[n - 2], ps_free_a, ps_free_v)
                return ps[n % 2]

            def product(o, a_hi, a_lo, b_hi, b_lo, first, last):
                nc.tensor.matmul(o, a_hi, b_hi, start=first, stop=False)
                nc.tensor.matmul(o, a_hi, b_lo, start=False, stop=False)
                return nc.tensor.matmul(o, a_lo, b_hi, start=False, stop=last)

            def rows_step(o, t, ci, k, width):
                s, tok = ci % 2, slice(t * P, (t + 1) * P)
                return product(o[:, 0:width], hT_hi[:, k, tok], hT_lo[:, k, tok],
                               w_hi[:, s, k, 0:width], w_lo[:, s, k, 0:width], k == 0, k == KD - 1)

            def channels(use, ci, m, f, act_hi, act_lo, kt):
                o = pp_claim(use)
                s, tok, ch = ci % 2, slice(f * HALF, (f + 1) * HALF), slice(m * P, (m + 1) * P)
                for k in range(kt):
                    last = product(o[:], w_hi[:, s, k, ch], w_lo[:, s, k, ch], act_hi[:, k, tok], act_lo[:, k, tok],
                                   k == 0, k == kt - 1)
                last.then_inc(pp_full, 1)

            def yb_transposes(b):
                pe.wait_ge(y_done, 2 * b + 2)
                o = pt_claim(("yb", b))
                for j in range(4):
                    last = nc.tensor.transpose(o[:, j * P:(j + 1) * P], y_row[:, j * P:(j + 1) * P], ident[:])
                last.then_inc(pt_full, 1)

            pe.wait_ge(consts, 1)
            pe.wait_ge(dve_ready, V_POS)
            o = pt_claim("cols")
            nc.tensor.transpose(o[:, 0:28], col_rows[:], ident[0:28, 0:28])
            nc.tensor.transpose(o[:, 32:32 + NT], pos_f[:], ident[0:NT, 0:NT]).then_inc(pt_full, 1)
            pe.wait_ge(rows_in, 32)
            o = pt_claim("gains")
            nc.tensor.matmul(o[:, 0:2 * HD], ones[0:1, :], gain_row[:], start=True, stop=True).then_inc(pt_full, 1)
            pe.wait_ge(c_silu_done, 1)
            o = ps_claim("ada")
            for i in range(4):
                pe.wait_ge(ada_in[i], 16)
                for j in range(4):
                    for k in range(KD):
                        last = nc.tensor.matmul(o[:, 4 * i + j:4 * i + j + 1], ada_w[:, i, k, j * P:(j + 1) * P],
                                                c_silu[:, k:k + 1], start=(k == 0), stop=(k == KD - 1))
                last.then_inc(ps_full, 1)
            for n in range(2 * KD):
                f, k = 1 - n // KD, n % KD
                if k == 0:
                    pe.wait_ge(xn_done, NT if f == 0 else NT // 2)
                o = pt_claim(("h", n))
                for j in range(4):
                    last = nc.tensor.transpose(o[:, j * P:(j + 1) * P], x_in[:, 4 * f + j, k * P:(k + 1) * P], ident[:])
                last.then_inc(pt_full, 1)

            def rows_chunk(kind, i, tiles, width):
                ci = name_of[(kind, i)] if kind != "kv" else name_of["kv"]
                pe.wait_ge(w_lo_done, pieces_through[ci])
                for t in tiles:
                    o = pp_claim((kind, i, t))
                    for k in range(KD):
                        last = rows_step(o, t, ci, k, width)
                    last.then_inc(pp_full, 1)
            pe.wait_ge(hT_hi_done, KD)
            pe.wait_ge(hT_lo_v, KD // 2)
            pe.wait_ge(hT_lo_p, KD // 2)
            ci = name_of[("qi", 0)]
            pe.wait_ge(w_lo_done, pieces_through[ci])
            for n, t in enumerate(QI_TILES):
                if n == 4:
                    pe.wait_ge(hT_hi_done, 2 * KD)
                    pe.wait_ge(hT_lo_v, KD)
                    pe.wait_ge(hT_lo_p, KD)
                o = pp_claim(("qi", 0, t))
                for k in range(KD):
                    last = rows_step(o, t, ci, k, CW)
                last.then_inc(pp_full, 1)
            rows_chunk("qi", 1, QI_TILES, CW)
            rows_chunk("kv", 0, ALL_TILES, KR_W)

            def key_transposes(kind, done):
                for s in range(2):
                    for f in range(2):
                        pe.wait_ge(kst_ready, done)
                        o = pt_claim((kind, s, f))
                        for j in range(4):
                            last = nc.tensor.transpose(o[:, j * P:(j + 1) * P].bitcast(F32R), kst[:, s, 4 * f + j, :],
                                                       ident_r[:])
                        last.then_inc(pt_full, 1)
            rows_chunk("q", 0, range(NT), CW)
            key_transposes("ki", 1)
            rows_chunk("q", 1, range(NT), CW)
            key_transposes("k", 2)

            def qi_transposes(b):
                n = b - FREE_BLOCKS
                pe.wait_ge(qi_hi, n + 1)
                pe.wait_ge(qi_lo, n + 1)
                for g in range(2):
                    o = pt_claim(("qi", b, g))
                    for j in range(4):
                        last = nc.tensor.transpose(o[:, j * P:(j + 1) * P].bitcast(F32R), qi_stk[:, 4 * g + j, :],
                                                   ident_r[:])
                    last.then_inc(pt_full, 1)

            def two_pass(o, q, kt_, n):
                for a in range(0, n, 512):
                    z = min(a + 512, n)
                    nc.tensor.matmul(o[:, a:z], q, kt_[:, 0, a:z], start=True, stop=False)
                    last = nc.tensor.matmul(o[:, a:z], q, kt_[:, 1, a:z], start=False, stop=True)
                return last

            def zb_step(n):
                i, t, k = n // (NT * KD), n // KD % NT, n % KD
                ci = name_of[("zb", i)]
                if t == 0 and k == 0:
                    pe.wait_ge(w_lo_done, pieces_through[ci])
                o = pp_claim(("zb", i, t)) if k == 0 else pp[pp_at[("zb", i, t)] % 2]
                last = rows_step(o, t, ci, k, CW)
                if k == KD - 1:
                    last.then_inc(pp_full, 1)
            qi_transposes(FREE_BLOCKS)
            step = 0
            for b in range(FREE_BLOCKS, NT):
                pe.wait_ge(pt_free_a, pt_done[pt_at[("qi", b, 1)]][0])
                if b == FREE_BLOCKS:
                    pe.wait_ge(pt_free_a, pt_done[pt_at[("k", 1, 1)]][0])
                for h in range(H):
                    o = ps_claim(("idx", b, h))
                    two_pass(o, qiT[:, b % 2, h, :], kiT, keys(b)).then_inc(ps_full, 1)
                    if h == 3 and b + 1 < NT:
                        qi_transposes(b + 1)
                    for _ in range(zb_after[(b, h)]):
                        zb_step(step)
                        step += 1

            def channel_chunk(kind, i):
                ci = name_of[(kind, i)]
                pe.wait_ge(w_lo_done, pieces_through[ci])
                for u, (m, f) in enumerate(UNITS):
                    channels((kind, i, u), ci, m, f, hT_hi, hT_lo, KD)
            for kind, i in C_ORDER:
                channel_chunk(kind, i)
            pe.wait_ge(wg_lo_done, 1)
            for i in range(2):
                ci = name_of[("za", i)]
                pe.wait_ge(w_lo_done, pieces_through[ci])
                for m in range(2):
                    g = 2 * i + m
                    for f in range(2):
                        channels(("za", i, 2 * m + f), ci, m, f, hT_hi, hT_lo, KD)
                    pe.wait_ge(pooled_hi, g + 1)
                    pe.wait_ge(pooled, g + 1)
                    for f in range(2):
                        tok = slice(f * HALF, (f + 1) * HALF)
                        o = pp_claim(("mix", i, 2 * m + f))
                        product(o[:], wg_hi[:, g, :], wg_lo[:, g, :], yT_hi[:, g, tok], yT_lo[:, g, tok],
                                True, True).then_inc(pp_full, 1)

            def mask_steps(u):
                if u in MASK_UNIT:
                    b = MASK_UNIT[u]
                    pe.wait_ge(eq_ready, b - FREE_BLOCKS + 1)
                    o = pt_claim(("eqT", b))[:].bitcast(BF16)
                    for j in range(b + 1):
                        last = nc.tensor.transpose(o[:, j * P:(j + 1) * P], eq[:, j * P:(j + 1) * P], ident_b[:])
                    last.then_inc(pt_full, 1)
                if u - 1 in MASK_UNIT:
                    b = MASK_UNIT[u - 1]
                    pe.wait_ge(pt_free_a, pt_done[pt_at[("eqT", b)]][0])
                    o = ps_claim(("cum", b))
                    n = keys(b)
                    for j in range(b + 1):
                        for a in range(0, n, 512):
                            z, lo = min(a + 512, n), max(a, j * P)
                            if lo < z:
                                last = nc.tensor.matmul(o[:, lo:z], eqT[:, j * P:(j + 1) * P],
                                                        prefix[:, lo - j * P:z - j * P], start=(j == 0),
                                                        stop=(j == min(b, z // P - 1)))
                    last.then_inc(ps_full, 1)
            for i in range(4):
                ci = name_of[("ga", i)]
                pe.wait_ge(w_lo_done, pieces_through[ci])
                for u, (m, f) in enumerate(UNITS):
                    channels(("ga", i, u), ci, m, f, hT_hi, hT_lo, KD)
                    mask_steps(8 * i + u)
                ci = name_of[("wa", i)]
                pe.wait_ge(w_lo_done, pieces_through[ci])
                if i == 0:
                    pe.wait_ge(ya_hi, 2 * GROUPS)
                    pe.wait_ge(ya_lo, 2 * GROUPS)
                for u, (m, f) in enumerate(UNITS):
                    channels(("wa", i, u), ci, m, f, yT_hi, yT_lo, KA)
                    mask_steps(8 * i + 4 + u)

            def q_transposes(b):
                pe.wait_ge(stk_hi, b + 1)
                pe.wait_ge(stk_lo, b + 1)
                for g in range(2):
                    o = pt_claim(("qT", b, g))
                    for j in range(4):
                        last = nc.tensor.transpose(o[:, j * P:(j + 1) * P].bitcast(F32R), q_stk[:, b % 2, 4 * g + j, :],
                                                   ident_r[:])
                    last.then_inc(pt_full, 1)
            q_transposes(0)
            for i in range(HEADS + 4):
                if i < HEADS:
                    b, h = i // H, i % H
                    if h == 0:
                        pe.wait_ge(pt_free_a, pt_done[pt_at[("qT", b, 1)]][0])
                    o = ps_claim(("S", i))
                    two_pass(o, qT[:, b % 2, h, :], kT, keys(b)).then_inc(ps_full, 1)
                if 0 <= i - 2 < HEADS:
                    j, b = i - 2, (i - 2) // H
                    pe.wait_ge(prob_done, j + 1)
                    for g in range((b + 4) // 4):
                        o = pt_claim(("PT", j, g))
                        for t in range(4 * g, min(4 * g + 4, b + 1)):
                            last = nc.tensor.transpose(o[:, (t % 4) * P:(t % 4 + 1) * P], prob[:, j % 2, t * P:(t + 1) * P],
                                                       ident[:])
                        last.then_inc(pt_full, 1)
                if 0 <= i - 3 < HEADS:
                    j, b, h = i - 3, (i - 3) // H, (i - 3) % H
                    wait_done(pe, pt_done[pt_at[("PT", j, b // 4)]], pt_free_a, pt_free_v)
                    o = pp_claim(("pv", b, h // 4)) if h % 4 == 0 else pp[pp_at[("pv", b, h // 4)] % 2]
                    o = o[:, (h % 4) * P:(h % 4 + 1) * P]
                    for t in range(b + 1):
                        nc.tensor.matmul(o, pT_hi[:, j % 2, t, :], v2[:, t, :], start=(t == 0), stop=False)
                        last = nc.tensor.matmul(o, pT_lo[:, j % 2, t, :], v2[:, t, :], start=False, stop=(t == b))
                    last.then_inc(pv_done, 1)
                if i % H == 4 and i // H + 1 < NT:
                    q_transposes(i // H + 1)
                if i in GATE_STEP:
                    g = GATE_STEP[i]
                    pe.wait_ge(gate_in, 32 * (g + 1))
                    pe.wait_ge(gate_sum, g + 1)
                    o = pt_claim(("gate", g))
                    nc.tensor.matmul(o[:], ones[:], gate_acc[:], start=True, stop=False)
                    nc.tensor.matmul(o[:], ones[0:1, :], gate[0:1, g * HALF:(g + 1) * HALF],
                                     start=False, stop=True).then_inc(pt_full, 1)
                if i >= 11 and (i - 11) % H == 0:
                    yb_transposes((i - 11) // H)

            wait_done(pe, pt_done[pt_at[("yb", NT - 1)]], pt_free_a, pt_free_v)
            for i in range(4):
                ci = name_of[("wb", i)]
                pe.wait_ge(w_lo_done, pieces_through[ci])
                for u, (m, f) in enumerate(UNITS):
                    channels(("wb", i, u), ci, m, f, yT_hi, yT_lo, KA)
            pe.wait_ge(mT_hi_done, 16)
            pe.wait_ge(mT_lo_done, 16)
            for i in range(4):
                ci = name_of[("wo", i)]
                pe.wait_ge(w_lo_done, pieces_through[ci])
                for t in range(NT):
                    o = pp_claim(("wo", i, t))
                    tok = slice(t * P, (t + 1) * P)
                    for k in range(KD):
                        last = product(o[:, 0:CW], mT_hi[:, k, tok], mT_lo[:, k, tok], w_hi[:, ci % 2, k, :],
                                       w_lo[:, ci % 2, k, :], k == 0, k == KD - 1)
                    last.then_inc(pp_full, 1)

        @block.scalar
        def _(act):
            for t in [4, 5, 6, 7, 0, 1, 2, 3]:
                act.dma_start(x_in[:, t, :], x[t * P:(t + 1) * P, :]).then_inc(x_tile_in[t], 16)
            act.wait_ge(consts, 1)
            nc.scalar.activation(ident_r[:], ident[:], ACT.Copy)
            act.wait_ge(c_in, 16)
            nc.scalar.activation(c_silu[:], c_col[:], ACT.Silu).then_inc(c_silu_done, 1)
            for t in [4, 5, 6, 7, 0, 1, 2, 3]:
                act.wait_ge(x_tile_in[t], 16)
                nc.scalar.activation(ps[1][:], x_in[:, t, :], ACT.Square, accum_out=ssx[:, t:t + 1]).then_inc(ssx_done, 1)
                act.drain()
            act.wait_ge(dve_ready, V_MEAN)
            nc.scalar.activation(rx[:], ssx[:], ACT.Sqrt).then_inc(sqrt_done, 1)
            act.wait_ge(dve_ready, V_SIN)
            nc.scalar.activation(trig[:], reduced[:], ACT.Sin).then_inc(trig_done, 1)
            act.wait_ge(group_in, 16)
            nc.scalar.activation(wg_hi[:], wg_raw[:], ACT.Copy).then_inc(wg_hi_done, 1)

            def ht_hi(n):
                f, k = 1 - n // KD, n % KD
                act.wait_ge(h_raw_done, n + 1)
                nc.scalar.activation(hT_hi[:, k, f * HALF:(f + 1) * HALF], h_raw[:, n % 4, :],
                                     ACT.Copy).then_inc(hT_hi_done, 1)
            for n in range(KD):
                ht_hi(n)
            split_chunk_hi(act, 0)
            for n in range(KD, 2 * KD):
                ht_hi(n)
            split_chunk_hi(act, 1)

            def pp_take(use):
                act.wait_ge(pp_full, pp_at[use] + 1)
                return pp[pp_at[use] % 2]

            def pt_take(key):
                act.wait_ge(pt_full, pt_at[key] + 1)
                return pt[pt_at[key] % 2]

            def pooled_round(g):
                act.wait_ge(ua_used, g + 1)
                nc.scalar.activation(yT_hi[:, g, :], win[:, 0, :], ACT.Copy).then_inc(pooled_hi, 1)

            def yb_hi(b):
                o = pt_take(("yb", b))
                nc.scalar.activation(yT_hi[:, :, b * P:(b + 1) * P], o[:].rearrange("p (k q) -> p k q", q=P),
                                     ACT.Copy).then_inc(pt_free_a, 1)

            act.wait_ge(xn_done, NT)
            act.wait_ge(pt_full, pt_at[("h", 2 * KD - 1)] + 1)
            for i in range(2):
                for t in QI_TILES:
                    o = pp_take(("qi", i, t))
                    nc.scalar.activation(qi[:, t - FREE_BLOCKS, i * CW:(i + 1) * CW], o[:, 0:CW],
                                         ACT.Copy).then_inc(pp_free_a, 1)
                split_chunk_hi(act, name_of[("qi", i)] + 2)
            for t in ALL_TILES:
                o = pp_take(("kv", 0, t))
                nc.scalar.activation(kr[:, t, :], o[:, 0:KR_W], ACT.Copy).then_inc(pp_free_a, 1)
            split_chunk_hi(act, name_of["kv"] + 2)

            def q_tile(i, t):
                o = pp_take(("q", i, t))
                nc.scalar.activation(q_all[:, t, i * CW:(i + 1) * CW], o[:, 0:CW], ACT.Copy).then_inc(pp_free_a, 1)

            def key_copies(kind, to):
                for s in range(2):
                    for f in range(2):
                        o = pt_take((kind, s, f))
                        nc.scalar.activation(to[:, s, f * HALF:(f + 1) * HALF], o[:], ACT.Copy).then_inc(pt_free_a, 1)
            for t in range(NT):
                q_tile(0, t)
            split_chunk_hi(act, name_of[("q", 0)] + 2)
            act.wait_ge(var_ready, 1)
            nc.scalar.activation(rk[:], ssk[:], ACT.Sqrt).then_inc(sqrt_done, 1)
            key_copies("ki", kiT)
            for t in range(NT):
                q_tile(1, t)
            split_chunk_hi(act, name_of[("q", 1)] + 2)
            key_copies("k", kT)
            act.wait_ge(var_ready, 2)
            nc.scalar.activation(rq[:], ssq[:], ACT.Sqrt).then_inc(sqrt_done, 1)

            def qi_split_hi(b):
                n = b - FREE_BLOCKS
                act.wait_ge(qi_roped, n + 1)
                if n:
                    act.wait_ge(pt_full, pt_at[("qi", b - 1, 1)] + 1)
                nc.scalar.activation(qi_stk[:, :, 0:HD], qi[:, n, :].rearrange("p (h d) -> p h d", d=HD),
                                     ACT.Copy).then_inc(qi_hi, 1)

            def qi_copies(b):
                for g in range(2):
                    o = pt_take(("qi", b, g))
                    nc.scalar.activation(qiT[:, b % 2, 4 * g:4 * g + 4, :].rearrange("p h q -> p (h q)"), o[:],
                                         ACT.Copy).then_inc(pt_free_a, 1)

            def zb_tile(i, t):
                s = (i * NT + t) % 4
                if i * NT + t >= 4:
                    act.wait_ge(zb_spilled[s], 16 * ((i * NT + t) // 4))
                o = pp_take(("zb", i, t))
                nc.scalar.activation(zb_out[:, s, :], o[:, 0:CW], ACT.Silu).then_inc(pp_free_a, 1)
                act.wait_ge(pp_free_a, pp_at[("zb", i, t)] + 1)
                act.dma_start(zb_dram[t * P:(t + 1) * P, i * CW:(i + 1) * CW], zb_out[:, s, :]).then_inc(zb_spilled[s], 16)
            qi_split_hi(FREE_BLOCKS)
            qi_copies(FREE_BLOCKS)
            step = 0
            for b in range(FREE_BLOCKS, NT):
                for h in range(H):
                    n = (b - FREE_BLOCKS) * H + h
                    if h == 0 and b + 1 < NT:
                        qi_split_hi(b + 1)
                    act.wait_ge(ps_full, ps_value(("idx", b, h)))
                    if n >= 2:
                        act.wait_ge(rel_used, n - 1)
                    nc.scalar.activation(rel[:, n % 2, 0:keys(b)], ps[ps_at[("idx", b, h)] % 2][:, 0:keys(b)],
                                         ACT.Relu).then_inc(ps_free_a, 1)
                    if h == 3 and b + 1 < NT:
                        qi_copies(b + 1)
                    for _ in range(zb_after[(b, h)]):
                        step += 1
                        if step % KD == 0:
                            zb_tile((step // KD - 1) // NT, (step // KD - 1) % NT)
                            if step == NT * KD:
                                split_chunk_hi(act, name_of[("zb", 0)] + 2)
            split_chunk_hi(act, name_of[("zb", 1)] + 2)

            act.wait_ge(q_spilled, 16 * NT)
            act.wait_ge(rel_used, NSEL * H)
            for s in range(4):
                act.wait_ge(zb_spilled[s], 16 * 4)

            def stage_slot(n):
                if n >= 4:
                    act.wait_ge(sgb_out[n % 4], 16 * min(n // 4, 4))
                if n >= 20:
                    act.wait_ge(ma_out[n % 4], 16 * (n // 4 - 4))
                return n % 4
            for kind, i in C_ORDER:
                for u, (m, f) in enumerate(UNITS):
                    o = pp_take((kind, i, u))
                    if kind == "ua":
                        g = 2 * i + m
                        if g >= 2:
                            act.wait_ge(pooled, g - 1)
                        nc.scalar.activation(ua[:, g % 2, f * HALF:(f + 1) * HALF], o[:], ACT.Copy).then_inc(pp_free_a, 1)
                    else:
                        s = stage_slot(4 * i + u)
                        nc.scalar.activation(stage[:, s, :], o[:], ACT.Sigmoid).then_inc(pp_free_a, 1)
                        act.wait_ge(pp_free_a, pp_at[("gb", i, u)] + 1)
                        r = (2 * i + m) * P
                        act.dma_start(sgb_dram[r:r + P, f * HALF:(f + 1) * HALF], stage[:, s, :]).then_inc(sgb_out[s], 16)
                    if (kind, i, u) in POOLED_ROUND:
                        pooled_round(POOLED_ROUND[kind, i, u])
                split_chunk_hi(act, name_of[(kind, i)] + 2)

            def ya_round(n):
                g, f = n // 2, n % 2
                act.wait_ge(ya_done, n + 1)
                nc.scalar.activation(yT_hi[:, g, f * HALF:(f + 1) * HALF], z_silu[:, g % 2, f * HALF:(f + 1) * HALF],
                                     ACT.Copy).then_inc(ya_hi, 1)
            act.wait_ge(pooled, GROUPS)
            for i in range(2):
                for m in range(2):
                    g = 2 * i + m
                    if g >= 2:
                        ya_round(2 * (g - 2))
                        ya_round(2 * (g - 2) + 1)
                        act.wait_ge(ya_lo, 2 * (g - 1))
                        act.wait_ge(ya_hi, 2 * (g - 1))
                    for f in range(2):
                        o = pp_take(("za", i, 2 * m + f))
                        nc.scalar.activation(z_silu[:, g % 2, f * HALF:(f + 1) * HALF], o[:], ACT.Silu).then_inc(pp_free_a, 1)
                    for f in range(2):
                        n = 2 * g + f
                        if n >= 2:
                            act.wait_ge(ya_done, n - 1)
                        o = pp_take(("mix", i, 2 * m + f))
                        nc.scalar.activation(mixed[:, n % 2, :], o[:], ACT.Copy, scale=col[:, 8 + g:9 + g]).then_inc(pp_free_a, 1)
                split_chunk_hi(act, name_of[("za", i)] + 2)
            for n in range(4, 8):
                ya_round(n)

            def mask_copy(u):
                if u in MASK_UNIT:
                    b = MASK_UNIT[u]
                    o = pt_take(("eqT", b))[:].bitcast(BF16)
                    nc.scalar.activation(eqT[:, 0:keys(b)], o[:, 0:keys(b)], ACT.Copy).then_inc(pt_free_a, 1)
            for i in range(4):
                for u, (m, f) in enumerate(UNITS):
                    s = stage_slot(16 + 4 * i + u)
                    o = pp_take(("ga", i, u))
                    nc.scalar.activation(stage[:, s, :], o[:], ACT.Sigmoid).then_inc(pp_free_a, 1)
                    mask_copy(8 * i + u)
                split_chunk_hi(act, name_of[("ga", i)] + 2)
                for u, (m, f) in enumerate(UNITS):
                    n = 4 * i + u
                    if n == 0:
                        act.wait_ge(ya_lo, 8)
                        act.wait_ge(ya_hi, 8)
                    if n >= 2:
                        act.wait_ge(ma_full, n - 1)
                    o = pp_take(("wa", i, u))
                    nc.scalar.activation(a_out[:, n % 2, :], o[:], ACT.Copy).then_inc(pp_free_a, 1)
                    mask_copy(8 * i + 4 + u)
                split_chunk_hi(act, name_of[("wa", i)] + 2)

            def load_q(b):
                if b >= 2:
                    act.wait_ge(stk_lo, b - 1)
                act.dma_start(q_row[:, b % 2, :], q_dram[b * P:(b + 1) * P, :]).then_inc(q_in[b % 2], 16)

            def load_z(b):
                if b >= 2:
                    act.wait_ge(y_done, 2 * (b - 1))
                act.dma_start(z_row[:, b % 2, :], zb_dram[b * P:(b + 1) * P, :]).then_inc(z_in[b % 2], 16)

            def q_split_hi(b):
                act.wait_ge(q_in[b % 2], 16 * (b // 2 + 1))
                if b >= 2:
                    act.wait_ge(pt_full, pt_at[("qT", b - 2, 1)] + 1)
                nc.scalar.activation(q_stk[:, b % 2, :, 0:HD], q_row[:, b % 2, :].rearrange("p (h d) -> p h d", d=HD),
                                     ACT.Copy).then_inc(stk_hi, 1)

            def q_copies(b):
                for g in range(2):
                    o = pt_take(("qT", b, g))
                    nc.scalar.activation(qT[:, b % 2, 4 * g:4 * g + 4, :].rearrange("p h q -> p (h q)"), o[:],
                                         ACT.Copy).then_inc(pt_free_a, 1)

            def load_gate(g):
                if g:
                    act.wait_ge(gate_sum, g)
                else:
                    act.wait_ge(eq_ready, NSEL)
                    act.wait_ge(bias_ready, NSEL + 1)
                act.dma_start(gate_w[:], w_ada.rearrange("(p k) n -> p k n", k=KD)[
                    :, :, 2 * D + g * HALF:2 * D + (g + 1) * HALF]).then_inc(gate_in, 16)
                act.dma_start(gate[0:1, g * HALF:(g + 1) * HALF],
                              b_ada[:, 2 * D + g * HALF:2 * D + (g + 1) * HALF]).then_inc(gate_in, 16)
            act.wait_ge(pp_full, PP_ACT)
            for b in range(2):
                load_q(b)
                load_z(b)
            q_split_hi(0)
            q_copies(0)
            for i in range(HEADS + 4):
                if 0 <= i - 1 < HEADS:
                    j, b, h = i - 1, (i - 1) // H, (i - 1) % H
                    act.wait_ge(logit_done, j + 1)
                    if j >= 2:
                        act.wait_ge(pt_full, pt_at[("PT", j - 2, (j - 2) // H // 4)] + 1)
                    if h % 4 == 0 and b >= 2:
                        act.wait_ge(o_sum, 2 * (b - 1))
                    r = (b % 2) * H + h
                    nc.scalar.activation(prob[:, j % 2, 0:keys(b)], logit[:, j % 2, 0:keys(b)], ACT.Exp, scale=-1.0,
                                         bias=neg_max[:, j % 2:j % 2 + 1],
                                         accum_out=row_sum[:, r:r + 1]).then_inc(prob_done, 1)
                if 0 <= i - 2 < HEADS:
                    j, b = i - 2, (i - 2) // H
                    if j >= 2:
                        act.wait_ge(pv_done, j - 1)
                    for g in range((b + 4) // 4):
                        t0, t1 = 4 * g, min(4 * g + 4, b + 1)
                        o = pt_take(("PT", j, g))
                        nc.scalar.activation(pT_hi[:, j % 2, t0:t1, :].rearrange("p t q -> p (t q)"), o[:, 0:(t1 - t0) * P],
                                             ACT.Copy).then_inc(pt_free_a, 1)
                if i % H == 2 and i // H + 1 < NT:
                    q_split_hi(i // H + 1)
                if i % H == 4 and i // H + 1 < NT:
                    q_copies(i // H + 1)
                if i % H == 5 and i // H + 2 < NT:
                    load_q(i // H + 2)
                if i == 10:
                    load_gate(0)
                if i == 40:
                    load_gate(1)
                if i in GATE_STEP:
                    g = GATE_STEP[i]
                    o = pt_take(("gate", g))
                    nc.scalar.activation(gate[:, g * HALF:(g + 1) * HALF], o[:], ACT.Copy).then_inc(pt_free_a, 1)
                if 0 <= i - 3 < HEADS and (i - 3) % 4 == 3:
                    n = (i - 3) // 4
                    if n >= 1:
                        act.wait_ge(o_sum, n)
                    act.wait_ge(pv_done, 4 * (n + 1))
                    o = pp[(PP_ACT + n) % 2][:].rearrange("p (h s d) -> p h s d", s=2, d=HD)
                    nc.scalar.activation(o_lo[:], o[:, :, 1, :], ACT.Copy).then_inc(o_lo_done, 1)
                if i >= 11 and (i - 11) % H == 0:
                    yb_hi((i - 11) // H)
                    b = (i - 11) // H + 2
                    if b < NT:
                        load_z(b)

            def load_e(n):
                i, u = n // 4, n % 4
                m, f = UNITS[u]
                r = (2 * i + m) * P
                if n >= 4:
                    act.wait_ge(m_raw_done, n - 3)
                act.dma_start(e_in[:, 0, n % 4, :], sgb_dram[r:r + P, f * HALF:(f + 1) * HALF]).then_inc(e_loaded[n % 4], 16)
                act.dma_start(e_in[:, 1, n % 4, :], ma_dram[r:r + P, f * HALF:(f + 1) * HALF]).then_inc(e_loaded[n % 4], 16)
            act.wait_ge(logit_done, HEADS)
            for n in range(4):
                load_e(n)
            act.wait_ge(pt_full, len(pt_uses))
            act.wait_ge(pt_free_v, pt_done[-1][1])
            act.wait_ge(y_done, 2 * NT)
            for n in range(16):
                i, u = n // 4, n % 4
                m, f = UNITS[u]
                act.wait_ge(m_raw_done, n + 1)
                nc.scalar.activation(mT_hi[:, 2 * i + m, f * HALF:(f + 1) * HALF], m_raw[:, n % 4, :],
                                     ACT.Copy).then_inc(mT_hi_done, 1)
                if n + 4 < 16:
                    load_e(n + 4)
                if u == 3:
                    split_chunk_hi(act, name_of[("wb", i)] + 2)

            def load_x(n):
                i, t = n // NT, n % NT
                if n >= 4:
                    act.wait_ge(o_row_done, n - 3)
                act.dma_start(x_row[:, n % 4, :], x[t * P:(t + 1) * P, i * CW:(i + 1) * CW]).then_inc(x_row_in[n % 4], 16)
            for n in range(4):
                load_x(n)
            for n in range(4 * NT):
                i, t = n // NT, n % NT
                act.wait_ge(o_row_done, n + 1)
                act.dma_start(out[t * P:(t + 1) * P, i * CW:(i + 1) * CW], o_row[:, n % 4, :]).then_inc(stored[n % 4], 16)
                if n + 4 < 4 * NT:
                    load_x(n + 4)
                if t == NT - 1:
                    split_chunk_hi(act, name_of[("wo", i)] + 2)
            for s in range(4):
                act.wait_ge(stored[s], 16 * NT)

        @block.gpsimd
        def _(pool):
            gp = nc.gpsimd
            gp.memset(ident[:], 0.0)
            gp.memset(ident_b[:], 0.0)
            gp.memset(prefix[:], 1.0)
            gp.memset(diag_bias[:], 0.0)
            gp.memset(ones[:], 1.0)
            for n in range(16):
                gp.memset(recip_n[:, n:n + 1], 1.0 / (n + 1))
            pool.drain()
            for m in (ident, ident_b):
                gp.affine_select(out=m[:], in_=m[:], compare_op=ALU.not_equal, fill=1.0, base=0,
                                 pattern=[[-1, P]], channel_multiplier=1)
            gp.affine_select(out=prefix[:, 0:P], in_=prefix[:, 0:P], compare_op=ALU.is_ge, fill=0.0, base=0,
                             pattern=[[1, P]], channel_multiplier=-1)
            gp.affine_select(out=diag_bias[:], in_=diag_bias[:], compare_op=ALU.is_ge, fill=NEG_BIAS, base=0,
                             pattern=[[-1, P]], channel_multiplier=1)
            pool.drain()
            gp.memset(rope_a[:], 0.0).then_inc(consts, 1)

            pool.wait_ge(wg_hi_done, 1)
            gp.tensor_tensor(wg_lo[:], wg_raw[:], wg_hi[:].bitcast(F32), ALU.subtract).then_inc(wg_lo_done, 1)

            def ht_lo(n):
                f, k = 1 - n // KD, n % KD
                pool.wait_ge(hT_hi_done, n + 1)
                tok = slice(f * HALF, (f + 1) * HALF)
                gp.tensor_tensor(hT_lo[:, k, tok], h_raw[:, n % 4, :], hT_hi[:, k, tok].bitcast(F32),
                                 ALU.subtract).then_inc(hT_lo_p, 1)
            for n in range(1, KD, 2):
                ht_lo(n)
            split_chunk_lo(pool, 0)
            for n in range(KD + 1, 2 * KD, 2):
                ht_lo(n)
            split_chunk_lo(pool, 1)

            def rope(v, t):
                cc = rot_c[:, t, :].unsqueeze(1).to_broadcast([P, H, ROT])
                ss = rot_s[:, t, :].unsqueeze(1).to_broadcast([P, H, ROT])
                gp.tensor_tensor(rope_a[:], v[:, :, 0:ROT], cc, ALU.mult)
                gp.tensor_tensor(rope_b[:, :, 0:NF], v[:, :, NF:ROT], ss[:, :, 0:NF], ALU.mult)
                gp.tensor_tensor(rope_b[:, :, NF:ROT], v[:, :, 0:NF], ss[:, :, NF:ROT], ALU.mult)
                pool.drain()
                return gp.tensor_tensor(v[:, :, 0:ROT], rope_a[:], rope_b[:], ALU.add)

            def qi_split_lo(b):
                n = b - FREE_BLOCKS
                pool.wait_ge(qi_hi, n + 1)
                nc.gpsimd.tensor_tensor(qi_stk[:, :, HD:2 * HD], qi[:, n, :].rearrange("p (h d) -> p h d", d=HD),
                                        qi_stk[:, :, 0:HD].bitcast(F32), ALU.subtract).then_inc(qi_lo, 1)

            def ya_rest(n):
                g, f = n // 2, n % 2
                tok = slice(f * HALF, (f + 1) * HALF)
                pool.wait_ge(ya_hi, n + 1)
                nc.gpsimd.tensor_tensor(yT_lo[:, g, tok], z_silu[:, g % 2, tok], yT_hi[:, g, tok].bitcast(F32),
                                        ALU.subtract).then_inc(ya_lo, 1)

            pool.wait_ge(pp_free_a, pp_at[("qi", 0, QI_TILES[-1])] + 1)
            split_chunk_lo(pool, 2)
            pool.wait_ge(trig_done, 2)
            for n in range(NSEL):
                t = n + FREE_BLOCKS
                pool.wait_ge(pp_free_a, pp_at[("qi", 1, 3)] + 1)
                rope(qi[:, n, :].rearrange("p (h d) -> p h d", d=HD), t).then_inc(qi_roped, 1)
                pool.wait_ge(qi_roped, n + 1)
                if n == 0:
                    split_chunk_lo(pool, 3)
            split_chunk_lo(pool, 4)
            split_chunk_lo(pool, 5)
            qi_split_lo(FREE_BLOCKS)

            def finish_query(t):
                pool.wait_ge(q_scaled, t + 1)
                rope(q_all[:, t, :].rearrange("p (h d) -> p h d", d=HD), t).then_inc(q_roped, 1)
                pool.wait_ge(q_roped, t + 1)
                pool.dma_start(q_dram[t * P:(t + 1) * P, :], q_all[:, t, :]).then_inc(q_spilled, 16)

            def causal_scores(b):
                pool.wait_ge(block_scored, b - FREE_BLOCKS + 1)
                own = slice(score_at(b) + b * P, score_at(b) + (b + 1) * P)
                gp.affine_select(out=score[:, own], in_=score[:, own], compare_op=ALU.is_ge, fill=MASKED, base=0,
                                 pattern=[[-1, P]], channel_multiplier=1).then_inc(masked, 1)
            for b in range(FREE_BLOCKS, NT):
                if b + 1 < NT:
                    qi_split_lo(b + 1)
                for t in SCALED[b].values():
                    finish_query(t)
                if b == FREE_BLOCKS:
                    split_chunk_lo(pool, 6)
                if b > FREE_BLOCKS:
                    causal_scores(b - 1)
                if b == 5:
                    split_chunk_lo(pool, 7)
            causal_scores(NT - 1)
            split_chunk_lo(pool, 8)

            pool.wait_ge(q_spilled, 16 * NT)
            for s in range(4):
                pool.wait_ge(zb_spilled[s], 16 * 4)

            def window_mean(g):
                w = 2 << g
                pool.wait_ge(pp_free_a, pp_at[("ua", g // 2, 2 * (g % 2) + 1)] + 1)
                if g:
                    pool.wait_ge(pooled, g)
                cur, s, side = ua[:, g % 2, :], 1, 0
                while s < w:
                    nxt = win[:, side, :]
                    gp.tensor_copy(nxt[:, 0:s], cur[:, 0:s])
                    gp.tensor_tensor(nxt[:, s:L], cur[:, s:L], cur[:, 0:L - s], ALU.add)
                    pool.drain()
                    cur, s, side = nxt, 2 * s, 1 - side
                other = win[:, side, :]
                gp.tensor_scalar(other[:, w:L], cur[:, w:L], 1.0 / w, None, ALU.mult)
                gp.tensor_tensor(other[:, 0:w], cur[:, 0:w], recip_n[:, 0:w], ALU.mult)
                pool.drain()
                gp.tensor_tensor(win[:, 0, :], other, ua[:, g % 2, :], ALU.subtract).then_inc(ua_used, 1)

            def pooled_low(g):
                pool.wait_ge(pooled_hi, g + 1)
                gp.tensor_tensor(yT_lo[:, g, :], win[:, 0, :], yT_hi[:, g, :].bitcast(F32), ALU.subtract).then_inc(pooled, 1)
            split_chunk_lo(pool, name_of["ua", 0] + 2)
            window_mean(0)
            split_chunk_lo(pool, name_of["gb", 0] + 2)
            pooled_low(0)
            window_mean(1)
            split_chunk_lo(pool, name_of["gb", 1] + 2)
            pooled_low(1)
            window_mean(2)
            split_chunk_lo(pool, name_of["ua", 1] + 2)
            pooled_low(2)
            window_mean(3)
            split_chunk_lo(pool, name_of["gb", 2] + 2)
            pooled_low(3)
            split_chunk_lo(pool, name_of["gb", 3] + 2)
            for n in range(2 * GROUPS):
                g, f = n // 2, n % 2
                tok = slice(f * HALF, (f + 1) * HALF)
                pool.wait_ge(pp_free_a, pp_at[("mix", g // 2, 2 * (g % 2) + f)] + 1)
                gp.tensor_tensor(z_silu[:, g % 2, tok], mixed[:, n % 2, :], z_silu[:, g % 2, tok], ALU.mult).then_inc(ya_done, 1)
                if n >= 2:
                    ya_rest(n - 2)
                if n % 4 == 3:
                    split_chunk_lo(pool, name_of[("za", n // 4)] + 2)
            ya_rest(2 * GROUPS - 2)
            ya_rest(2 * GROUPS - 1)
            for i in range(4):
                split_chunk_lo(pool, name_of[("ga", i)] + 2)
                for u, (m, f) in enumerate(UNITS):
                    n = 4 * i + u
                    r = (2 * i + m) * P
                    pool.wait_ge(pp_free_a, pp_at[("wa", i, u)] + 1)
                    gp.tensor_tensor(stage[:, n % 4, :], a_out[:, n % 2, :], stage[:, n % 4, :], ALU.mult).then_inc(ma_full, 1)
                    pool.wait_ge(ma_full, n + 1)
                    pool.dma_start(ma_dram[r:r + P, f * HALF:(f + 1) * HALF], stage[:, n % 4, :]).then_inc(ma_out[n % 4], 16)
                split_chunk_lo(pool, name_of[("wa", i)] + 2)

            pool.wait_ge(pp_full, PP_ACT)

            def q_split_lo(b):
                pool.wait_ge(stk_hi, b + 1)
                gp.tensor_tensor(q_stk[:, b % 2, :, HD:2 * HD], q_row[:, b % 2, :].rearrange("p (h d) -> p h d", d=HD),
                                 q_stk[:, b % 2, :, 0:HD].bitcast(F32), ALU.subtract).then_inc(stk_lo, 1)
            q_split_lo(0)
            for b in range(NT):
                for f in range(2):
                    n = 2 * b + f
                    if f == 0 and b + 1 < NT:
                        q_split_lo(b + 1)
                    if f == 0 and b >= 1:
                        pool.wait_ge(pt_full, pt_at[("yb", b - 1)] + 1)
                    pool.wait_ge(o_sum, n + 1)
                    pool.wait_ge(z_in[b % 2], 16 * (b // 2 + 1))
                    y = y_row[:, 4 * f * HD:4 * (f + 1) * HD]
                    gp.tensor_tensor(y, y, z_row[:, b % 2, 4 * f * HD:4 * (f + 1) * HD], ALU.mult).then_inc(y_done, 1)
            pool.wait_ge(pt_full, len(pt_uses))
            pool.wait_ge(pt_free_v, pt_done[-1][1])
            for n in range(16):
                i, u = n // 4, n % 4
                m, f = UNITS[u]
                tok = slice(f * HALF, (f + 1) * HALF)
                pool.wait_ge(mT_hi_done, n + 1)
                gp.tensor_tensor(mT_lo[:, 2 * i + m, tok], m_raw[:, n % 4, :], mT_hi[:, 2 * i + m, tok].bitcast(F32),
                                 ALU.subtract).then_inc(mT_lo_done, 1)
                if u == 3:
                    split_chunk_lo(pool, name_of[("wb", i)] + 2)
            for i in range(4):
                split_chunk_lo(pool, name_of[("wo", i)] + 2)

        @block.vector
        def _(dve):
            v = nc.vector
            for k in range(31):
                v.memset(bit_i[:, k:k + 1], 1 << (30 - k))
                v.memset(bit_f[:, k:k + 1], float(1 << (30 - k)))
            v.memset(bit_i[:, 31:32], 0)
            v.memset(bit_f[:, 31:32], 0.0)
            dve.wait_ge(cols_in, 64)
            v.tensor_copy(pos_f[:], pos_i[:]).then_inc(dve_ready, 1)
            dve.wait_ge(pt_full, pt_at["cols"] + 1)
            v.tensor_copy(col[:], pt[0][:, 0:28])
            v.tensor_copy(pos_col[:], pt[0][:, 32:32 + NT]).then_inc(pt_free_v, 1)
            dve.wait_ge(pt_full, pt_at["gains"] + 1)
            v.tensor_copy(gains[:], pt[1][:, 0:2 * HD]).then_inc(pt_free_v, 1)
            dve.drain()
            v.tensor_scalar(nx[:], pos_col[:], 0.0, None, ALU.add).then_inc(dve_ready, 1)
            for k in range(NF):
                v.tensor_scalar(angle[:, :, k], pos_col[:], float(np.float32(THETA ** (-2.0 * k / ROT))), None, ALU.mult)
            dve.drain()
            ang = angle[:].rearrange("p t f -> p (t f)")
            v.tensor_scalar(turns[:, 0, :], ang, float(1 / (2 * np.pi)), MAGIC, ALU.mult, ALU.add)
            v.tensor_scalar(turns[:, 1, :], ang, float(1 / (2 * np.pi)), 0.25, ALU.mult, ALU.add)
            dve.drain()
            v.tensor_scalar(turns[:, 1, :], turns[:, 1, :], MAGIC, None, ALU.add)
            dve.drain()
            v.tensor_scalar(turns[:], turns[:], MAGIC, None, ALU.subtract)
            dve.drain()
            for s in range(2):
                v.scalar_tensor_tensor(reduced[:, s, :], turns[:, s, :], -TWO_PI[0], ang, ALU.mult, ALU.add)
            for part in TWO_PI[1:]:
                dve.drain()
                v.scalar_tensor_tensor(reduced[:], turns[:], -part, reduced[:], ALU.mult, ALU.add)
            dve.drain()
            v.tensor_scalar(reduced[:, 1, :], reduced[:, 1, :], float(np.pi / 2), None, ALU.add)
            dve.drain()
            v.tensor_scalar(reduced[:], reduced[:], 3.1415925, -3.1415925, ALU.min, ALU.max).then_inc(dve_ready, 1)

            def rsqrt_step(y, mean, tmp):
                v.reciprocal(y, y)
                dve.drain()
                v.tensor_tensor(tmp, y, y, ALU.mult)
                dve.drain()
                v.tensor_tensor(tmp, tmp, mean, ALU.mult)
                dve.drain()
                v.tensor_scalar(tmp, tmp, -0.5, 1.5, ALU.mult, ALU.add)
                dve.drain()
                v.tensor_tensor(y, y, tmp, ALU.mult)
                dve.drain()

            dve.wait_ge(ssx_done, NT)
            v.tensor_scalar(ssx[:], ssx[:], 1.0 / D, EPS, ALU.mult, ALU.add).then_inc(dve_ready, 1)
            dve.wait_ge(sqrt_done, 1)
            rsqrt_step(rx[:], ssx[:], nx[:])
            for t in [4, 5, 6, 7, 0, 1, 2, 3]:
                v.tensor_scalar(x_in[:, t, :], x_in[:, t, :], rx[:, t:t + 1], None, ALU.mult).then_inc(xn_done, 1)
            dve.wait_ge(trig_done, 1)
            sin, cos = (trig[:, s, :].rearrange("p (t f) -> p t f", f=NF) for s in range(2))
            v.tensor_copy(rot_c[:, :, 0:NF], cos)
            v.tensor_copy(rot_c[:, :, NF:ROT], cos)
            v.tensor_scalar(rot_s[:, :, 0:NF], sin, -1.0, None, ALU.mult)
            v.tensor_copy(rot_s[:, :, NF:ROT], sin)
            dve.drain()
            v.tensor_copy(nq[:, 0:1], rx[:, 0:1]).then_inc(trig_done, 1)
            dve.wait_ge(ps_full, 4)
            v.tensor_tensor(shift[:], ps[0][:, 0:2 * KD], col[:, 12:28], ALU.add).then_inc(ps_free_v, 1)
            dve.drain()
            v.tensor_scalar(gmul[:], shift[:, KD:2 * KD], 1.0, None, ALU.add)
            dve.drain()
            v.tensor_tensor(gmul[:], gmul[:], col[:, 0:KD], ALU.mult)
            dve.drain()
            for n in range(2 * KD + 2):
                if n < 2 * KD:
                    k = n % KD
                    dve.wait_ge(pt_full, pt_at[("h", n)] + 1)
                    if n == 0:
                        dve.wait_ge(wg_lo_done, 1)
                    if n >= 4:
                        if n % 2 == 0:
                            dve.wait_ge(hT_lo_v, (n - 4) // 2 + 1)
                        else:
                            dve.wait_ge(hT_lo_p, (n - 5) // 2 + 1)
                    v.tensor_scalar(h_raw[:, n % 4, :], pt[pt_at[("h", n)] % 2][:], gmul[:, k:k + 1], shift[:, k:k + 1],
                                    ALU.mult, ALU.add).then_inc(h_raw_done, 1)
                    dve.wait_ge(h_raw_done, n + 1)
                    dve.sem_inc(pt_free_v, 1)
                if n >= 2 and n % 2 == 0:
                    j = n - 2
                    f, k = 1 - j // KD, j % KD
                    tok = slice(f * HALF, (f + 1) * HALF)
                    dve.wait_ge(hT_hi_done, j + 1)
                    v.tensor_tensor(hT_lo[:, k, tok], h_raw[:, j % 4, :], hT_hi[:, k, tok].bitcast(F32),
                                    ALU.subtract).then_inc(hT_lo_v, 1)

            dve.wait_ge(pp_free_a, pp_at[("kv", 0, 3)] + 1)
            ki, kk, vv = kr[:, :, KR_KI:KR_KI + HD], kr[:, :, KR_K:KR_K + HD], kr[:, :, KR_V:KR_V + HD]
            tmp_a = score[:, 0:NT * ROT].rearrange("p (t r) -> p t r", r=ROT)
            tmp_b = score[:, NT * ROT:2 * NT * ROT].rearrange("p (t r) -> p t r", r=ROT)

            def rope_keys(u):
                v.tensor_tensor(tmp_a, u[:, :, 0:ROT], rot_c[:], ALU.mult)
                v.tensor_tensor(tmp_b[:, :, 0:NF], u[:, :, NF:ROT], rot_s[:, :, 0:NF], ALU.mult)
                v.tensor_tensor(tmp_b[:, :, NF:ROT], u[:, :, 0:NF], rot_s[:, :, NF:ROT], ALU.mult)
                dve.drain()
                v.tensor_tensor(u[:, :, 0:ROT], tmp_a, tmp_b, ALU.add)
                dve.drain()

            def stack_keys(u):
                for s in range(2):
                    v.tensor_copy(kst[:, 0, :, s * HD:(s + 1) * HD], u)
                dve.drain()
                v.tensor_tensor(kst[:, 1, :, 0:HD], u, kst[:, 0, :, 0:HD].bitcast(F32), ALU.subtract)
                v.tensor_tensor(kst[:, 1, :, HD:2 * HD], u, kst[:, 0, :, HD:2 * HD].bitcast(F32),
                                ALU.subtract).then_inc(kst_ready, 1)
            rope_keys(ki)
            stack_keys(ki)
            v.tensor_scalar(w_idx[:], kr[:, :, KR_WI:KR_WI + H], IDX_SCALE, None, ALU.mult)
            v.tensor_copy(v2[:, :, 0:HD], vv)
            dve.drain()
            v.tensor_tensor(v2[:, :, HD:2 * HD], vv, v2[:, :, 0:HD].bitcast(F32), ALU.subtract)
            sq = score[:, 512:512 + NT * HD].rearrange("p (t d) -> p t d", d=HD)
            v.tensor_tensor(sq, kk, kk, ALU.mult)
            dve.drain()
            v.tensor_reduce(ssk[:], sq, AX.X, ALU.add)
            dve.drain()
            v.tensor_scalar(ssk[:], ssk[:], 1.0 / HD, EPS, ALU.mult, ALU.add).then_inc(var_ready, 1)
            dve.wait_ge(sqrt_done, 2)
            rsqrt_step(rk[:], ssk[:], nk[:])
            v.tensor_tensor(kk, kk, rk[:].unsqueeze(2).to_broadcast([P, NT, HD]), ALU.mult)
            dve.drain()
            v.tensor_tensor(kk, kk, gains[:, HD:2 * HD].unsqueeze(1).to_broadcast([P, NT, HD]), ALU.mult)
            dve.drain()
            rope_keys(kk)
            dve.wait_ge(pt_full, pt_at[("ki", 1, 1)] + 1)
            stack_keys(kk)
            for t in range(NT):
                dve.wait_ge(pp_free_a, pp_at[("q", 1, t)] + 1)
                sq = score[:, 512 * (1 + t % 2):512 * (2 + t % 2)]
                v.tensor_tensor(sq, q_all[:, t, :], q_all[:, t, :], ALU.mult)
                dve.drain()
                v.tensor_reduce(ssq[:, t * H:(t + 1) * H], sq.rearrange("p (h d) -> p h d", d=HD), AX.X, ALU.add)
            dve.drain()
            v.tensor_scalar(ssq[:], ssq[:], 1.0 / HD, EPS, ALU.mult, ALU.add).then_inc(var_ready, 1)
            dve.wait_ge(sqrt_done, 3)
            rsqrt_step(rq[:], ssq[:], nq[:])

            def scale_query(t):
                qv = q_all[:, t, :].rearrange("p (h d) -> p h d", d=HD)
                v.tensor_tensor(qv, qv, rq[:, t * H:(t + 1) * H].unsqueeze(2).to_broadcast([P, H, HD]), ALU.mult)
                dve.drain()
                v.tensor_tensor(qv, qv, gains[:, 0:HD].unsqueeze(1).to_broadcast([P, H, HD]), ALU.mult).then_inc(q_scaled, 1)
            for b in range(FREE_BLOCKS, NT):
                s = score[:, score_at(b):score_at(b + 1)]
                for h in range(H):
                    n = (b - FREE_BLOCKS) * H + h
                    dve.wait_ge(ps_free_a, n + 1)
                    w = w_idx[:, b, h:h + 1]
                    if h == 0:
                        ins = v.tensor_scalar(s, rel[:, n % 2, 0:keys(b)], w, None, ALU.mult)
                    else:
                        dve.wait_ge(rel_used, n)
                        ins = v.scalar_tensor_tensor(s, rel[:, n % 2, 0:keys(b)], w, s, ALU.mult, ALU.add)
                    ins.then_inc(rel_used, 1)
                    if h in SCALED[b]:
                        scale_query(SCALED[b][h])
                dve.wait_ge(rel_used, (b - FREE_BLOCKS + 1) * H)
                dve.sem_inc(block_scored, 1)

            dve.wait_ge(masked, NSEL)
            dve.wait_ge(pt_free_a, pt_done[pt_at[("qi", NT - 1, 1)]][0])
            for s in range(4):
                dve.wait_ge(zb_spilled[s], 16 * 4)

            def count(at_least):
                for n in range(NSEL):
                    b = n + FREE_BLOCKS
                    least = at_least if at_least is not None else cand[:, n:n + 1].bitcast(F32)
                    if n and n % 2 == 0:
                        dve.drain()
                    v.tensor_scalar(junk[:, n % 2, 0:keys(b)], score[:, score_at(b):score_at(b + 1)], least, None,
                                    ALU.is_ge, ALU.add, accum_out=cnt[:, n:n + 1])
                dve.drain()
            count(0.0)
            v.tensor_scalar(thr[:], cnt[:], TOPK - 0.5, -1.0, ALU.is_lt, ALU.mult)
            dve.drain()
            v.tensor_scalar(cand[:], thr[:], bit_i[:, 0:1], None, ALU.bitwise_xor)
            dve.drain()
            with dve.Fori(0, 31) as k:
                count(None)
                v.tensor_scalar(accept[:], cnt[:], TOPK - 0.5, bit_f[:, bass.ds(k, 1)], ALU.is_ge, ALU.mult)
                dve.drain()
                v.scalar_tensor_tensor(cand[:], accept[:], bit_i[:, bass.ds(k + 1, 1)], thr[:],
                                       ALU.bitwise_xor, ALU.bitwise_xor)
                v.tensor_tensor(thr[:], thr[:], accept[:], ALU.bitwise_xor)
                dve.drain()

            dve.wait_ge(ya_hi, 2 * GROUPS)
            dve.wait_ge(ya_lo, 2 * GROUPS)
            for b in range(FREE_BLOCKS):
                if b:
                    v.memset(bias[:, bias_at(b):bias_at(b) + b * P], 0.0)
                v.tensor_copy(bias[:, bias_at(b) + b * P:bias_at(b + 1)], diag_bias[:])
            dve.drain()
            dve.sem_inc(bias_ready, 1)

            def mask_begin(b):
                n = b - FREE_BLOCKS
                t = thr[:, n:n + 1].bitcast(F32)
                s = score[:, score_at(b):score_at(b + 1)]
                v.tensor_scalar(gt[:, 0:keys(b)], s, t, None, ALU.is_gt, ALU.add, accum_out=cnt[:, n:n + 1])
                v.tensor_scalar(eq[:, 0:keys(b)], s, t, None, ALU.is_equal).then_inc(eq_ready, 1)
                dve.drain()
                v.tensor_scalar(need[:], cnt[:, n:n + 1], -1.0, float(TOPK), ALU.mult, ALU.add)
                dve.drain()

            def mask_end(b):
                dve.wait_ge(ps_full, ps_value(("cum", b)))
                o = ps[ps_at[("cum", b)] % 2]
                v.scalar_tensor_tensor(eq[:, 0:keys(b)], o[:, 0:keys(b)], need[:], eq[:, 0:keys(b)],
                                       ALU.is_le, ALU.mult).then_inc(ps_free_v, 1)
                dve.drain()
                v.tensor_tensor(gt[:, 0:keys(b)], gt[:, 0:keys(b)], eq[:, 0:keys(b)], ALU.add)
                dve.drain()
                v.tensor_scalar(bias[:, bias_at(b):bias_at(b + 1)], gt[:, 0:keys(b)], 1.0, -NEG_BIAS,
                                ALU.subtract, ALU.mult).then_inc(bias_ready, 1)
                dve.drain()

            def pT_low(j):
                b = j // H
                if j >= 2:
                    dve.wait_ge(pv_done, j - 1)
                for g in range((b + 4) // 4):
                    t0, t1 = 4 * g, min(4 * g + 4, b + 1)
                    n = pt_at[("PT", j, g)]
                    dve.wait_ge(pt_free_a, pt_done[n][0])
                    v.tensor_tensor(pT_lo[:, j % 2, t0:t1, :].rearrange("p t q -> p (t q)"), pt[n % 2][:, 0:(t1 - t0) * P],
                                    pT_hi[:, j % 2, t0:t1, :].rearrange("p t q -> p (t q)").bitcast(F32),
                                    ALU.subtract).then_inc(pt_free_v, 1)

            def outputs(n):
                b, f = n // 2, n % 2
                r = (b % 2) * H + 4 * f
                if f == 0 and b >= 1:
                    dve.wait_ge(pt_full, pt_at[("yb", b - 1)] + 1)
                v.reciprocal(row_inv[:], row_sum[:, r:r + 4])
                dve.wait_ge(o_lo_done, n + 1)
                y = y_row[:, 4 * f * HD:4 * (f + 1) * HD].rearrange("p (h d) -> p h d", d=HD)
                o = pp[(PP_ACT + n) % 2][:].rearrange("p (h s d) -> p h s d", s=2, d=HD)
                v.tensor_tensor(y, o[:, :, 0, :], o_lo[:], ALU.add).then_inc(pp_free_v, 1)
                dve.drain()
                v.tensor_tensor(y, y, row_inv[:].unsqueeze(2).to_broadcast([P, 4, HD]), ALU.mult).then_inc(o_sum, 1)

            def yb_low(b):
                n = pt_at[("yb", b)]
                dve.wait_ge(pt_free_a, pt_done[n][0])
                v.tensor_tensor(yT_lo[:, :, b * P:(b + 1) * P], pt[n % 2][:].rearrange("p (k q) -> p k q", q=P),
                                yT_hi[:, :, b * P:(b + 1) * P].bitcast(F32), ALU.subtract).then_inc(pt_free_v, 1)
            for b in range(FREE_BLOCKS, NT):
                mask_begin(b)
                mask_end(b)
            dve.wait_ge(pp_full, PP_ACT)
            for i in range(HEADS + 4):
                if i < HEADS:
                    b = i // H
                    dve.wait_ge(ps_full, ps_value(("S", i)))
                    if i >= 2:
                        dve.wait_ge(prob_done, i - 1)
                    v.tensor_tensor_reduce(logit[:, i % 2, 0:keys(b)], ps[ps_at[("S", i)] % 2][:, 0:keys(b)],
                                           bias[:, bias_at(b):bias_at(b + 1)], -ATT_SCALE, 3.0e38, ALU.add, ALU.min,
                                           neg_max[:, i % 2:i % 2 + 1]).then_inc(logit_done, 1)
                    dve.wait_ge(logit_done, i + 1)
                    dve.sem_inc(ps_free_v, 1)
                if 0 <= i - 2 < HEADS:
                    pT_low(i - 2)
                if i in GATE_ADD:
                    g, k = GATE_ADD[i]
                    c = c_silu[:, k:k + 1]
                    if k == 0:
                        dve.wait_ge(gate_in, 32 * (g + 1))
                        if g:
                            dve.wait_ge(pt_full, pt_at[("gate", g - 1)] + 1)
                        ins = v.tensor_scalar(gate_acc[:], gate_w[:, k, :], c, None, ALU.mult)
                    else:
                        dve.drain()
                        ins = v.scalar_tensor_tensor(gate_acc[:], gate_w[:, k, :], c, gate_acc[:], ALU.mult, ALU.add)
                    if k == KD - 1:
                        ins.then_inc(gate_sum, 1)
                if 0 <= i - 3 < HEADS and (i - 3) % 4 == 3:
                    outputs((i - 3) // 4)
                if i >= 11 and (i - 11) % H == 0:
                    yb_low((i - 11) // H)
            for s in range(4):
                dve.wait_ge(ma_out[s], 16 * 4)

            for n in range(16):
                u = PP_ACT + 2 * NT + n
                dve.wait_ge(pp_full, pp_value(u))
                dve.wait_ge(e_loaded[n % 4], 32 * (n // 4 + 1))
                if n >= 4:
                    dve.wait_ge(mT_lo_done, n - 3)
                v.tensor_tensor(m_raw[:, n % 4, :], pp[u % 2][:], e_in[:, 0, n % 4, :], ALU.mult).then_inc(pp_free_v, 1)
                dve.drain()
                v.tensor_tensor(m_raw[:, n % 4, :], m_raw[:, n % 4, :], e_in[:, 1, n % 4, :], ALU.add).then_inc(m_raw_done, 1)
            for n in range(4 * NT):
                i = n // NT
                u = PP_ACT + 2 * NT + 16 + n
                dve.wait_ge(pp_full, pp_value(u))
                dve.wait_ge(x_row_in[n % 4], 16 * (n // 4 + 1))
                if n >= 4:
                    dve.wait_ge(stored[n % 4], 16 * (n // 4))
                v.tensor_tensor(o_row[:, n % 4, :], pp[u % 2][:, 0:CW], gate[:, i * CW:(i + 1) * CW],
                                ALU.mult).then_inc(pp_free_v, 1)
                dve.drain()
                v.tensor_tensor(o_row[:, n % 4, :], o_row[:, n % 4, :], x_row[:, n % 4, :], ALU.add).then_inc(o_row_done, 1)


_INS = ["x", "c", "positions", "w_ada", "b_ada", "norm_gain", "w_in", "w_pool_group", "pool_scale",
        "q_norm_gain", "k_norm_gain", "w_branch_a", "w_branch_b", "w_out"]


def kernel(**inputs):
    import concourse.bacc as bacc
    from concourse.bass_utils import run_bass_kernel_spmd

    nc = bacc.Bacc("TRN2", target_bir_lowering=False, num_devices=1)
    arrays, args = {}, []
    for name in _INS:
        a = np.ascontiguousarray(inputs[name])
        arrays[f"in_{name}"] = a
        args.append(nc.dram_tensor(f"in_{name}", a.shape, mybir.dt.from_np(a.dtype), kind="ExternalInput").ap())
    args.append(nc.dram_tensor("out", (1, L, D), F32, kind="ExternalOutput").ap())
    hybrid_layer(nc, *args)
    r = run_bass_kernel_spmd(nc, [arrays], core_ids=[0])
    return r.results[0]["out"]
```

```python
from contextlib import ExitStack

import numpy as np
import concourse.bass as bass
from concourse import mybir

F32, F32R, BF16, I32, U8 = (mybir.dt.float32, mybir.dt.float32r, mybir.dt.bfloat16, mybir.dt.int32, mybir.dt.uint8)
ACT, ALU, AX = mybir.ActivationFunctionType, mybir.AluOpType, mybir.AxisListType

P = 128
D = 1024
L = 1024
NT = L // P
KD = D // P
HALF = 512
H, HD = 8, 64
ROT = HD // 4
NF = ROT // 2
THETA = 500000.0
TOPK = min(256, L // 4)
FREE_BLOCKS = TOPK // P
NSEL = NT - FREE_BLOCKS
EPS = 1e-6
GROUPS = 4
KA = 512 // P
CW = 256
IDX_SCALE = float(H ** -0.5 * HD ** -0.5)
ATT_SCALE = float(HD ** -0.5)
MAGIC = 12582912.0
TWO_PI = (6.28125, 0.0019340515136718750, 1.2556416e-06)
MASKED = -3.0e38
NEG_BIAS = -1.0e30

O_UA, O_ZA, O_Q, O_K, O_V, O_ZB, O_QI, O_KI, O_WI, O_GA, O_GB = (
    0, 512, 1024, 1536, 1600, 1664, 2176, 2688, 2752, 2760, 3784)
KR_KI, KR_WI, KR_K, KR_V, KR_W = 0, 64, 72, 136, 200


def keys(b):
    return (b + 1) * P


def score_at(b):
    return P * sum(j + 1 for j in range(FREE_BLOCKS, b))


def bias_at(b):
    return P * sum(j + 1 for j in range(b))


def hybrid_layer(nc, x, c, positions, w_ada, b_ada, norm_gain, w_in, w_pool_group, pool_scale,
                 q_norm_gain, k_norm_gain, w_branch_a, w_branch_b, w_out, out):
    x, out = x[0], out[0]
    w_ada, w_in, w_group = w_ada[0], w_in[0], w_pool_group[0]
    w_branch_a, w_branch_b, w_out = w_branch_a[0], w_branch_b[0], w_out[0]

    def cols(src, first, kt=KD):
        return (kt, [(src, first, CW, 0)])
    chunks, name_of = [], {}

    def add(name, chunk):
        name_of[name] = len(chunks)
        chunks.append(chunk)
    for i in range(2):
        add(("qi", i), cols(w_in, O_QI + CW * i))
    add("kv", (KD, [(w_in, O_KI, KR_K, 0), (w_in, O_K, 2 * HD, KR_K)]))
    for i in range(2):
        add(("q", i), cols(w_in, O_Q + CW * i))
    for i in range(2):
        add(("zb", i), cols(w_in, O_ZB + CW * i))
    C_ORDER = [("ua", 0), ("gb", 0), ("gb", 1), ("ua", 1), ("gb", 2), ("gb", 3)]
    for kind, i in C_ORDER:
        add((kind, i), cols(w_in, (O_UA if kind == "ua" else O_GB) + CW * i))
    for i in range(2):
        add(("za", i), cols(w_in, O_ZA + CW * i))
    for i in range(4):
        add(("ga", i), cols(w_in, O_GA + CW * i))
    for i in range(4):
        add(("wa", i), cols(w_branch_a, CW * i, KA))
    for i in range(4):
        add(("wb", i), cols(w_branch_b, CW * i, KA))
    for i in range(4):
        add(("wo", i), cols(w_out, CW * i))
    pieces = [(ci, p) for ci, (kt, _) in enumerate(chunks) for p in range(kt // 4)]
    pieces_through = [sum(k // 4 for k, _ in chunks[:ci + 1]) for ci in range(len(chunks))]
    RAW = 2
    raw_ready, got = [], [0] * RAW
    for n, (ci, _) in enumerate(pieces):
        got[n % RAW] += 16 * len(chunks[ci][1])
        raw_ready.append(got[n % RAW])

    pp_uses = []
    QI_TILES = [4, 5, 6, 7, 2, 3]
    ALL_TILES = [4, 5, 6, 7, 0, 1, 2, 3]
    for i in range(2):
        pp_uses += [("qi", i, t) for t in QI_TILES]
    pp_uses += [("kv", 0, t) for t in ALL_TILES]
    for i in range(2):
        pp_uses += [("q", i, t) for t in range(NT)]
    for i in range(2):
        pp_uses += [("zb", i, t) for t in range(NT)]
    UNITS = [(m, f) for m in range(2) for f in range(2)]
    for kind, i in C_ORDER:
        pp_uses += [(kind, i, u) for u in range(4)]
    for i in range(2):
        for m in range(2):
            pp_uses += [("za", i, 2 * m), ("za", i, 2 * m + 1), ("mix", i, 2 * m), ("mix", i, 2 * m + 1)]
    for i in range(4):
        pp_uses += [("ga", i, u) for u in range(4)]
    PP_HT = len(pp_uses)
    pp_bank = [n % 2 for n in range(PP_HT)]
    pp_uses += [("wa", i, u) for i in range(4) for u in range(4)]
    pp_bank += [1] * 16
    pp_uses += [("pv", b, f) for b in range(NT) for f in range(2)]
    pp_bank += [0] * (2 * NT)
    for i in range(4):
        pp_uses += [("wb", i, u) for u in range(4)]
    for i in range(4):
        pp_uses += [("wo", i, t) for t in range(NT)]
    pp_bank += [(n + 1) % 2 for n in range(len(pp_uses) - len(pp_bank))]
    pp_at = {use: n for n, use in enumerate(pp_uses)}
    pp_prev, pp_done, pp_sig = [], [], []
    last_in, na, nv, full = {}, 0, 0, 0
    for n, use in enumerate(pp_uses):
        pp_prev.append(last_in.get(pp_bank[n]))
        last_in[pp_bank[n]] = n
        by_act = n < PP_HT or use[0] == "wa"
        na, nv, full = na + by_act, nv + (not by_act), full + (use[0] != "pv")
        pp_done.append((na, 0) if by_act else (0, nv))
        pp_sig.append(full)

    def chunk_done(ci):
        name = [k for k, v in name_of.items() if v == ci][0]
        kind, i = name if isinstance(name, tuple) else (name, 0)
        return max(pp_sig[n] for n, use in enumerate(pp_uses)
                   if use[:2] == (kind, i) or (kind == "za" and use[:2] == ("mix", i)))

    HEADS = NT * H
    MASK_UNIT = {12: FREE_BLOCKS, 14: FREE_BLOCKS + 1}
    MASK_STEP = {4 * n: FREE_BLOCKS + 2 + n for n in range(NSEL - 2)}
    WA_FIRST = 2
    WA_STEP = {4 * (n - WA_FIRST) + 3: n for n in range(WA_FIRST, 16)}
    YB_STEP = {max(57 + b, 8 * b + 11): b for b in range(NT)}
    assert len(YB_STEP) == NT and max(WA_STEP) < min(YB_STEP)
    pt_uses = [("cols", "v"), ("gains", "v")]
    pt_uses += [(("h", n), "v") for n in range(2 * KD)]
    Q_EXTRA = {0: [("ki", 0, 0)], 1: [("ki", 0, 1)], 2: [("ki", 1, 0)], 3: [("ki", 1, 1)],
               4: [("qi", FREE_BLOCKS, 0)], 5: [("qi", FREE_BLOCKS, 1)],
               7: [("k", 0, 0)], 8: [("k", 0, 1), ("k", 1, 0), ("k", 1, 1)]}
    for t in Q_EXTRA:
        pt_uses += [(key, "a") for key in Q_EXTRA[t]]
    pt_uses += [(("qi", b, g), "a") for b in range(FREE_BLOCKS + 1, NT) for g in range(2)]
    pt_uses += [(("eqT", b), "a") for b in MASK_UNIT.values()]
    pt_uses += [(("qT", 0, g), "a") for g in range(2)]
    for i in range(HEADS + 4):
        if i - 1 in MASK_STEP:
            pt_uses.append((("eqT", MASK_STEP[i - 1]), "a"))
        if 0 <= i - 2 < HEADS:
            for g in range((keys((i - 2) // H) // P + 3) // 4):
                pt_uses.append((("PT", i - 2, g), "av"))
        if i % H == 4 and i // H + 1 < NT:
            pt_uses += [(("qT", i // H + 1, g), "a") for g in range(2)]
        if i in YB_STEP:
            pt_uses.append((("yb", YB_STEP[i]), "av"))
    pt_uses += [(("gate", g), "a") for g in range(2)]
    pt_at, pt_done, na, nv = {}, [], 0, 0
    for n, (key, who) in enumerate(pt_uses):
        pt_at[key] = n
        na += "a" in who
        nv += "v" in who
        pt_done.append((na if "a" in who else 0, nv if "v" in who else 0))

    ps_uses = [("ada", "v")]
    ps_uses += [(("idx", b, h), "a") for b in range(FREE_BLOCKS, NT) for h in range(H)]
    ps_uses += [(("cum", b), "v") for b in MASK_UNIT.values()]
    for i in range(HEADS):
        if i - 2 in MASK_STEP:
            ps_uses.append((("cum", MASK_STEP[i - 2]), "v"))
        ps_uses.append((("S", i), "v"))
    ps_at, ps_done, na, nv = {}, [], 0, 0
    for n, (key, who) in enumerate(ps_uses):
        ps_at[key] = n
        na += who == "a"
        nv += who == "v"
        ps_done.append((na if who == "a" else 0, nv if who == "v" else 0))

    def ps_value(key):
        return ps_at[key] + 4

    with ExitStack() as ctx:
        def alloc(stack, name, shape, dt=F32):
            return stack.enter_context(nc.sbuf_tensor(name, shape, dt))

        def sb(name, shape, dt=F32):
            return alloc(ctx, name, shape, dt)

        def sem(name):
            return ctx.enter_context(nc.semaphore(name))

        ident = sb("ident", [P, P])
        ident_b = sb("ident_b", [P, P], BF16)
        prefix = sb("prefix", [P, L], BF16)
        diag_bias = sb("diag_bias", [P, P], BF16)
        ident_r = sb("ident_r", [P, P], F32R)
        ones = sb("ones", [P, P])
        col = sb("col", [P, 28])
        pos_col = sb("pos_col", [P, NT])
        gains = sb("gains", [P, 2 * HD])
        c_col = sb("c_col", [P, KD])
        c_silu = sb("c_silu", [P, KD])
        shift = sb("shift", [P, 2 * KD])
        gmul = sb("gmul", [P, KD])
        rot_c = sb("rot_c", [P, NT, ROT])
        rot_s = sb("rot_s", [P, NT, ROT])
        ssx, rx, nx = sb("ssx", [P, NT]), sb("rx", [P, NT]), sb("nx", [P, NT])
        ssq, rq, nq = sb("ssq", [P, NT * H]), sb("rq", [P, NT * H]), sb("nq", [P, NT * H])
        ssk, rk, nk = sb("ssk", [P, NT]), sb("rk", [P, NT]), sb("nk", [P, NT])
        w_idx = sb("w_idx", [P, NT, H])
        rope_a, rope_b = sb("rope_a", [P, H, ROT]), sb("rope_b", [P, H, ROT])
        recip_n = sb("recip_n", [P, 16])
        wg_hi, wg_lo = sb("wg_hi", [P, GROUPS, P], F32R), sb("wg_lo", [P, GROUPS, P], F32R)
        cnt, thr = sb("cnt", [P, NSEL]), sb("thr", [P, NSEL], I32)
        cand, accept = sb("cand", [P, NSEL], I32), sb("accept", [P, NSEL], I32)
        bit_i, bit_f = sb("bit_i", [P, 32], I32), sb("bit_f", [P, 32])
        need = sb("need", [P, 1])
        neg_max, row_sum, row_inv = sb("neg_max", [P, 2]), sb("row_sum", [P, 2 * H]), sb("row_inv", [P, 4])
        kT = sb("kT", [P, 2, L], F32R)
        v2 = sb("v2", [P, NT, 2 * HD], F32R)
        w_raw = sb("w_raw", [P, RAW, 4, CW])
        w_hi, w_lo = sb("w_hi", [P, 2, KD, CW], F32R), sb("w_lo", [P, 2, KD, CW], F32R)

        def zone(kib, *tenants):
            got = []
            for tenant in tenants:
                with ExitStack() as s:
                    got.append(tenant(s))
            sb(f"zone_{kib}".replace(".", "_"), [P, int(kib * 256)])
            return got

        ada_w, (hT_hi, hT_lo), att, (mT_hi, mT_lo) = zone(
            64,
            lambda s: alloc(s, "ada_w", [P, 4, KD, HALF]),
            lambda s: (alloc(s, "hT_hi", [P, KD, L], F32R), alloc(s, "hT_lo", [P, KD, L], F32R)),
            lambda s: dict(
                q_row=alloc(s, "q_row", [P, 2, H * HD]), z_row=alloc(s, "z_row", [P, 2, H * HD]),
                q_stk=alloc(s, "q_stk", [P, 2, H, 2 * HD], F32R), qT=alloc(s, "qT", [P, 2, H, P], F32R),
                logit=alloc(s, "logit", [P, 2, L]), prob=alloc(s, "prob", [P, 2, L]),
                pT_hi=alloc(s, "pT_hi", [P, 2, NT, P], F32R), pT_lo=alloc(s, "pT_lo", [P, 2, NT, P], F32R),
                o_lo=alloc(s, "o_lo", [P, 4, HD])),
            lambda s: (alloc(s, "mT_hi", [P, KD, L], F32R), alloc(s, "mT_lo", [P, KD, L], F32R)))
        def tenants_start(s):
            return (alloc(s, "h_raw", [P, 4, HALF]), alloc(s, "wg_raw", [P, GROUPS, P]),
                    alloc(s, "col_rows", [28, P]),
                    alloc(s, "pos_i", [NT, P], I32), alloc(s, "pos_f", [NT, P]), alloc(s, "gain_row", [1, 2 * HD]),
                    alloc(s, "angle", [P, NT, NF]), alloc(s, "turns", [P, 2, NT * NF]),
                    alloc(s, "reduced", [P, 2, NT * NF]), alloc(s, "trig", [P, 2, NT * NF]))
        (h_raw, wg_raw, col_rows, pos_i, pos_f, gain_row, angle, turns, reduced, trig), score, y_row, gate_w = zone(
            16.5, tenants_start,
            lambda s: alloc(s, "score", [P, score_at(NT)]),
            lambda s: alloc(s, "y_row", [P, NT, H * HD]),
            lambda s: alloc(s, "gate_w", [P, KD, HALF]))

        def tenants_first(s):
            return alloc(s, "x_in", [P, NT, D]), alloc(s, "ada_acc", [P, 4, HALF])

        def tenants_a(s):
            q = alloc(s, "q_all", [P, NT, H * HD])
            kiT = alloc(s, "kiT", [P, 2, L], F32R)
            qi_stk = alloc(s, "qi_stk", [P, H, 2 * HD], F32R)
            qiT = alloc(s, "qiT", [P, 2, H, P], F32R)
            qi = alloc(s, "qi", [P, NSEL, H * HD])
            with ExitStack() as k:
                kr, kst = alloc(k, "kr", [P, NT, KR_W]), alloc(k, "kst", [P, 2, NT, P], F32R)
            with ExitStack() as k:
                rel, zb_out = alloc(k, "rel", [P, 2, L]), alloc(k, "zb_out", [P, 4, CW])
            return q, qi, kiT, qi_stk, qiT, kr, kst, rel, zb_out

        def tenants_c(s):
            yT_hi, yT_lo = alloc(s, "yT_hi", [P, KA, L], F32R), alloc(s, "yT_lo", [P, KA, L], F32R)
            with ExitStack() as k:
                ua, win = alloc(k, "ua", [P, 2, L]), alloc(k, "win", [P, 2, L])
            with ExitStack() as k:
                z_silu, mixed = alloc(k, "z_silu", [P, 2, L]), alloc(k, "mixed", [P, 2, HALF])
            with ExitStack() as k:
                bias, a_out = alloc(k, "bias", [P, bias_at(NT)], BF16), alloc(k, "a_out", [P, 2, HALF])
            with ExitStack() as k:
                e_in = alloc(k, "e_in", [P, 2, 4, HALF])
            with ExitStack() as k:
                x_row, o_row = alloc(k, "x_row", [P, 4, CW]), alloc(k, "o_row", [P, 4, CW])
            alloc(s, "zone_c", [P, 16 * 256])
            with ExitStack() as k:
                stage = alloc(k, "stage", [P, 4, HALF])
            with ExitStack() as k:
                m_raw = alloc(k, "m_raw", [P, 4, HALF])
            alloc(s, "zone_s", [P, 8 * 256])
            with ExitStack() as k:
                junk = alloc(k, "junk", [P, 2, L], U8)
            with ExitStack() as k:
                gt, eq, eqT = (alloc(k, n, [P, L], BF16) for n in ("gt", "eq", "eqT"))
            with ExitStack() as k:
                gate, gate_acc = alloc(k, "gate", [P, D]), alloc(k, "gate_acc", [P, HALF])
            alloc(s, "zone_m", [P, 6 * 256])
            return yT_hi, yT_lo, ua, win, z_silu, mixed, bias, a_out, e_in, stage, gt, eq, eqT, m_raw, junk, gate, gate_acc, x_row, o_row

        (x_in, ada_acc), ta, tc = zone(62.5, tenants_first, tenants_a, tenants_c)
        q_all, qi, kiT, qi_stk, qiT, kr, kst, rel, zb_out = ta
        yT_hi, yT_lo, ua, win, z_silu, mixed, bias, a_out, e_in, stage, gt, eq, eqT, m_raw, junk, gate, gate_acc, x_row, o_row = tc
        q_row, z_row, q_stk, qT = att["q_row"], att["z_row"], att["q_stk"], att["qT"]
        logit, prob, pT_hi, pT_lo = att["logit"], att["prob"], att["pT_hi"], att["pT_lo"]
        o_lo = att["o_lo"]

        pp = [ctx.enter_context(nc.psum_tensor(f"pp{i}", [P, 512], F32)) for i in range(2)]
        pt = [ctx.enter_context(nc.psum_tensor(f"pt{i}", [P, 512], F32)) for i in range(2)]
        ps = [ctx.enter_context(nc.psum_tensor(f"ps{i}", [P, 1024], F32)) for i in range(2)]

        q_dram = nc.dram_tensor("q_spill", [L, H * HD], F32).ap()
        zb_dram = nc.dram_tensor("zb_spill", [L, H * HD], F32).ap()
        sga_dram = nc.dram_tensor("sga_spill", [D, L], F32).ap()
        sgb_dram = nc.dram_tensor("sgb_spill", [D, L], F32).ap()
        ma_dram = nc.dram_tensor("ma_spill", [D, L], F32).ap()

        c_in, cols_in, rows_in, group_in = sem("c_in"), sem("cols_in"), sem("rows_in"), sem("group_in")
        x_tile_in = [sem(f"x_tile_in{t}") for t in range(NT)]
        ada_in = [sem(f"ada_in{i}") for i in range(8)]
        raw_in = [sem(f"raw_in{i}") for i in range(RAW)]
        consts = sem("consts")
        dve_ready = sem("dve_ready")
        w_hi_done, w_lo_done = sem("w_hi_done"), sem("w_lo_done")
        pp_full, pp_free_a, pp_free_v = sem("pp_full"), sem("pp_free_a"), sem("pp_free_v")
        pt_full, pt_free_a, pt_free_v = sem("pt_full"), sem("pt_free_a"), sem("pt_free_v")
        ps_full, ps_free_a, ps_free_v = sem("ps_full"), sem("ps_free_a"), sem("ps_free_v")
        ada_sum = sem("ada_sum")
        c_silu_done, ssx_done, sqrt_done, trig_done = sem("c_silu_done"), sem("ssx_done"), sem("sqrt_done"), sem("trig_done")
        xn_done, h_raw_done = sem("xn_done"), sem("h_raw_done")
        hT_hi_done, hT_lo_v, hT_lo_p = sem("hT_hi_done"), sem("hT_lo_v"), sem("hT_lo_p")
        wg_hi_done, wg_lo_done = sem("wg_hi_done"), sem("wg_lo_done")
        qi_roped, kst_ready = sem("qi_roped"), sem("kst_ready")
        var_ready = sem("var_ready")
        q_scaled, q_roped = sem("q_scaled"), sem("q_roped")
        q_spilled, zb_spilled = sem("q_spilled"), [sem(f"zb_spilled{i}") for i in range(4)]
        qi_hi, qi_lo = sem("qi_hi"), sem("qi_lo")
        rel_used, block_scored, masked = sem("rel_used"), sem("block_scored"), sem("masked")
        silu_b = sem("silu_b")
        sel_done, bisected = sem("sel_done"), sem("bisected")
        pooled, pooled_hi, ua_used, mixed_used = sem("pooled"), sem("pooled_hi"), sem("ua_used"), sem("mixed_used")
        ya_hi, ya_lo, ya_done = sem("ya_hi"), sem("ya_lo"), sem("ya_done")
        stage_full, ma_full = sem("stage_full"), sem("ma_full")
        sg_out, sga_in = [sem(f"sg_out{i}") for i in range(4)], [sem(f"sga_in{i}") for i in range(4)]
        ma_out = [sem(f"ma_out{i}") for i in range(4)]
        q_in, z_in = [sem(f"q_in{i}") for i in range(2)], [sem(f"z_in{i}") for i in range(2)]
        stk_hi, stk_lo = sem("stk_hi"), sem("stk_lo")
        gate_sum, gate_in = sem("gate_sum"), sem("gate_in")
        eq_ready, bias_ready = sem("eq_ready"), sem("bias_ready")
        logit_done, prob_done = sem("logit_done"), sem("prob_done")
        pT_read, pv_done = sem("pT_read"), sem("pv_done")
        o_lo_done, o_sum, y_done = sem("o_lo_done"), sem("o_sum"), sem("y_done")
        e_loaded = [sem(f"e_loaded{i}") for i in range(4)]
        m_raw_done, mT_hi_done, mT_lo_done = sem("m_raw_done"), sem("mT_hi_done"), sem("mT_lo_done")
        x_row_in, o_row_done = [sem(f"x_row_in{i}") for i in range(4)], sem("o_row_done")
        stored = [sem(f"stored{i}") for i in range(4)]
        block = ctx.enter_context(nc.Block())

        def wait_done(eng, done, sem_a, sem_v):
            if done[0]:
                eng.wait_ge(sem_a, done[0])
            if done[1]:
                eng.wait_ge(sem_v, done[1])

        V_POS, V_COL, V_SIN, V_MEAN, V_RSQRT = 1, 2, 3, 4, 5

        @block.sync
        def _(sp):
            sp.dma_start(c_col[:], c.rearrange("a (p k) -> p (a k)", k=KD)).then_inc(c_in, 16)
            sp.dma_start(col_rows[0:8, :], norm_gain.rearrange("a (r p) -> (a r) p", p=P)).then_inc(cols_in, 16)
            sp.dma_start(col_rows[8:12, :], pool_scale.rearrange("a (r p) -> (a r) p", p=P)).then_inc(cols_in, 16)
            sp.dma_start(col_rows[12:28, :], b_ada[:, 0:2 * D].rearrange("a (r p) -> (a r) p", p=P)).then_inc(cols_in, 16)
            sp.dma_start(pos_i[:], positions.rearrange("a (r p) -> (a r) p", p=P)).then_inc(cols_in, 16)
            sp.dma_start(gain_row[:, 0:HD], q_norm_gain).then_inc(rows_in, 16)
            sp.dma_start(gain_row[:, HD:2 * HD], k_norm_gain).then_inc(rows_in, 16)
            ada = w_ada.rearrange("(p k) n -> p k n", k=KD)
            for i in range(4):
                for j in range(2):
                    ks = slice(j * KD // 2, (j + 1) * KD // 2)
                    sp.dma_start(ada_w[:, i, ks], ada[:, ks, i * HALF:(i + 1) * HALF]).then_inc(ada_in[2 * i + j], 16)
            sp.dma_start(wg_raw[:], w_group.rearrange("g c d -> c g d")).then_inc(group_in, 16)
            for n, (ci, p) in enumerate(pieces):
                if n >= RAW:
                    sp.wait_ge(w_lo_done, n - RAW + 1)
                for src, first, width, to in chunks[ci][1]:
                    view = src.rearrange("(k p) n -> p k n", p=P)
                    sp.dma_start(w_raw[:, n % RAW, :, to:to + width],
                                 view[:, 4 * p:4 * p + 4, first:first + width]).then_inc(raw_in[n % RAW], 16)

        def split_chunk_hi(act, ci):
            if ci >= len(chunks):
                return
            if ci >= 2:
                act.wait_ge(pp_full, chunk_done(ci - 2))
            for n, (cj, p) in enumerate(pieces):
                if cj == ci:
                    width = sum(w for _, _, w, _ in chunks[ci][1])
                    act.wait_ge(raw_in[n % RAW], raw_ready[n])
                    nc.scalar.activation(w_hi[:, ci % 2, 4 * p:4 * p + 4, 0:width], w_raw[:, n % RAW, :, 0:width],
                                         ACT.Copy).then_inc(w_hi_done, 1)

        def split_chunk_lo(pool, ci):
            if ci >= len(chunks):
                return
            for n, (cj, p) in enumerate(pieces):
                if cj == ci:
                    width = sum(w for _, _, w, _ in chunks[ci][1])
                    pool.wait_ge(w_hi_done, n + 1)
                    nc.gpsimd.tensor_tensor(w_lo[:, ci % 2, 4 * p:4 * p + 4, 0:width], w_raw[:, n % RAW, :, 0:width],
                                            w_hi[:, ci % 2, 4 * p:4 * p + 4, 0:width].bitcast(F32),
                                            ALU.subtract).then_inc(w_lo_done, 1)

        SCALED = {b: {3: 2 * n, 6: 2 * n + 1} if n < 2 else {1: 2 + n} for n, b in enumerate(range(FREE_BLOCKS, NT))}

        POOLED_ROUND = {("gb", 1, 0): 0, ("ua", 1, 1): 1, ("gb", 2, 1): 2, ("gb", 3, 1): 3}

        GATE_UNIT = NT + 2

        zb_after = {(b, h): 1 if b == FREE_BLOCKS else 3 for b in range(FREE_BLOCKS, NT) for h in range(H)}
        assert sum(zb_after.values()) == 2 * NT * KD

        @block.tensor
        def _(pe):
            def pp_claim(use):
                n = pp_at[use]
                if pp_prev[n] is not None:
                    wait_done(pe, pp_done[pp_prev[n]], pp_free_a, pp_free_v)
                return pp[pp_bank[n]]

            def pt_claim(key):
                n = pt_at[key]
                if n >= 2:
                    wait_done(pe, pt_done[n - 2], pt_free_a, pt_free_v)
                return pt[n % 2]

            def ps_claim(key):
                n = ps_at[key]
                if n >= 2:
                    wait_done(pe, ps_done[n - 2], ps_free_a, ps_free_v)
                return ps[n % 2]

            def product(o, a_hi, a_lo, b_hi, b_lo, first, last):
                nc.tensor.matmul(o, a_hi, b_hi, start=first, stop=False)
                nc.tensor.matmul(o, a_hi, b_lo, start=False, stop=False)
                return nc.tensor.matmul(o, a_lo, b_hi, start=False, stop=last)

            def rows_step(o, t, ci, k, width):
                s, tok = ci % 2, slice(t * P, (t + 1) * P)
                return product(o[:, 0:width], hT_hi[:, k, tok], hT_lo[:, k, tok],
                               w_hi[:, s, k, 0:width], w_lo[:, s, k, 0:width], k == 0, k == KD - 1)

            def channels(use, ci, m, f, act_hi, act_lo, kt):
                o = pp_claim(use)
                s, tok, ch = ci % 2, slice(f * HALF, (f + 1) * HALF), slice(m * P, (m + 1) * P)
                for k in range(kt):
                    last = product(o[:], w_hi[:, s, k, ch], w_lo[:, s, k, ch], act_hi[:, k, tok], act_lo[:, k, tok],
                                   k == 0, k == kt - 1)
                last.then_inc(pp_full, 1)

            def yb_transposes(b):
                pe.wait_ge(y_done, 2 * b + 2)
                o = pt_claim(("yb", b))
                for j in range(4):
                    last = nc.tensor.transpose(o[:, j * P:(j + 1) * P], y_row[:, b, j * P:(j + 1) * P], ident[:])
                last.then_inc(pt_full, 1)

            pe.wait_ge(consts, 1)
            pe.wait_ge(dve_ready, V_POS)
            o = pt_claim("cols")
            nc.tensor.transpose(o[:, 0:28], col_rows[:], ident[0:28, 0:28])
            nc.tensor.transpose(o[:, 32:32 + NT], pos_f[:], ident[0:NT, 0:NT]).then_inc(pt_full, 1)
            pe.wait_ge(rows_in, 32)
            o = pt_claim("gains")
            nc.tensor.matmul(o[:, 0:2 * HD], ones[0:1, :], gain_row[:], start=True, stop=True).then_inc(pt_full, 1)
            def h_transposes(n):
                f, k = 1 - n // KD, n % KD
                if k == 0:
                    pe.wait_ge(xn_done, NT if f == 0 else NT // 2)
                o = pt_claim(("h", n))
                for j in range(4):
                    last = nc.tensor.transpose(o[:, j * P:(j + 1) * P], x_in[:, 4 * f + j, k * P:(k + 1) * P], ident[:])
                last.then_inc(pt_full, 1)
            for n in range(2):
                h_transposes(n)
            o = ps_claim("ada")
            for i in range(4):
                pe.wait_ge(ada_sum, i + 1)
                for j in range(4):
                    last = nc.tensor.matmul(o[:, 4 * i + j:4 * i + j + 1], ada_acc[:, i, j * P:(j + 1) * P],
                                            ones[:, 0:1], start=True, stop=True)
                last.then_inc(ps_full, 1)
            for n in range(2, KD):
                h_transposes(n)

            def rows_chunk(kind, i, tiles, width):
                ci = name_of[(kind, i)] if kind != "kv" else name_of["kv"]
                pe.wait_ge(w_lo_done, pieces_through[ci])
                for t in tiles:
                    o = pp_claim((kind, i, t))
                    for k in range(KD):
                        last = rows_step(o, t, ci, k, width)
                    last.then_inc(pp_full, 1)
            ci = name_of[("qi", 0)]
            pe.wait_ge(w_lo_done, pieces_through[ci])
            for n, t in enumerate(QI_TILES):
                if n == 4:
                    pe.wait_ge(hT_hi_done, 2 * KD)
                    pe.wait_ge(hT_lo_v, KD)
                    pe.wait_ge(hT_lo_p, KD)
                o = pp_claim(("qi", 0, t))
                for k in range(KD):
                    if n == 0:
                        pe.wait_ge(hT_hi_done, k + 1)
                        pe.wait_ge(hT_lo_v, k // 2 + 1)
                        if k:
                            pe.wait_ge(hT_lo_p, (k + 1) // 2)
                    last = rows_step(o, t, ci, k, CW)
                last.then_inc(pp_full, 1)
                if n < 4:
                    h_transposes(KD + 2 * n)
                    h_transposes(KD + 2 * n + 1)
            rows_chunk("qi", 1, QI_TILES, CW)
            rows_chunk("kv", 0, ALL_TILES, KR_W)

            def key_transposes(kind, s, f):
                pe.wait_ge(kst_ready, 1 if kind == "ki" else 2)
                o = pt_claim((kind, s, f))
                for j in range(4):
                    last = nc.tensor.transpose(o[:, j * P:(j + 1) * P].bitcast(F32R), kst[:, s, 4 * f + j, :],
                                               ident_r[:])
                last.then_inc(pt_full, 1)
            rows_chunk("q", 0, range(NT), CW)

            def qi_transposes(b, groups=range(2)):
                n = b - FREE_BLOCKS
                pe.wait_ge(qi_hi, n + 1)
                pe.wait_ge(qi_lo, n + 1)
                for g in groups:
                    o = pt_claim(("qi", b, g))
                    for j in range(4):
                        last = nc.tensor.transpose(o[:, j * P:(j + 1) * P].bitcast(F32R), qi_stk[:, 4 * g + j, :],
                                                   ident_r[:])
                    last.then_inc(pt_full, 1)

            def two_pass(o, q, kt_, n):
                for a in range(0, n, 512):
                    z = min(a + 512, n)
                    nc.tensor.matmul(o[:, a:z], q, kt_[:, 0, a:z], start=True, stop=False)
                    last = nc.tensor.matmul(o[:, a:z], q, kt_[:, 1, a:z], start=False, stop=True)
                return last

            def zb_step(n):
                i, t, k = n // (NT * KD), n // KD % NT, n % KD
                ci = name_of[("zb", i)]
                if t == 0 and k == 0:
                    pe.wait_ge(w_lo_done, pieces_through[ci])
                o = pp_claim(("zb", i, t)) if k == 0 else pp[pp_bank[pp_at[("zb", i, t)]]]
                last = rows_step(o, t, ci, k, CW)
                if k == KD - 1:
                    last.then_inc(pp_full, 1)
            ci = name_of[("q", 1)]
            pe.wait_ge(w_lo_done, pieces_through[ci])
            for t in range(NT + 1):
                for key in Q_EXTRA.get(t, []):
                    if key[0] == "qi":
                        qi_transposes(FREE_BLOCKS, [key[2]])
                    else:
                        key_transposes(*key)
                if t < NT:
                    o = pp_claim(("q", 1, t))
                    for k in range(KD):
                        last = rows_step(o, t, ci, k, CW)
                    last.then_inc(pp_full, 1)
            step = 0
            for b in range(FREE_BLOCKS, NT):
                pe.wait_ge(pt_free_a, pt_done[pt_at[("qi", b, 1)]][0])
                for h in range(H):
                    o = ps_claim(("idx", b, h))
                    two_pass(o, qiT[:, b % 2, h, :], kiT, keys(b)).then_inc(ps_full, 1)
                    if h == 5 and b + 1 < NT:
                        qi_transposes(b + 1)
                    for _ in range(zb_after[(b, h)]):
                        zb_step(step)
                        step += 1

            def channel_chunk(kind, i):
                ci = name_of[(kind, i)]
                pe.wait_ge(w_lo_done, pieces_through[ci])
                for u, (m, f) in enumerate(UNITS):
                    channels((kind, i, u), ci, m, f, hT_hi, hT_lo, KD)
            for kind, i in C_ORDER:
                channel_chunk(kind, i)
            pe.wait_ge(wg_lo_done, 1)
            for i in range(2):
                ci = name_of[("za", i)]
                pe.wait_ge(w_lo_done, pieces_through[ci])
                for m in range(2):
                    g = 2 * i + m
                    for f in range(2):
                        channels(("za", i, 2 * m + f), ci, m, f, hT_hi, hT_lo, KD)
                    pe.wait_ge(pooled_hi, g + 1)
                    pe.wait_ge(pooled, g + 1)
                    for f in range(2):
                        tok = slice(f * HALF, (f + 1) * HALF)
                        o = pp_claim(("mix", i, 2 * m + f))
                        product(o[:], wg_hi[:, g, :], wg_lo[:, g, :], yT_hi[:, g, tok], yT_lo[:, g, tok],
                                True, True).then_inc(pp_full, 1)

            def tie_transposes(b):
                pe.wait_ge(eq_ready, b - FREE_BLOCKS + 1)
                o = pt_claim(("eqT", b))[:].bitcast(BF16)
                for j in range(b + 1):
                    last = nc.tensor.transpose(o[:, j * P:(j + 1) * P], eq[:, j * P:(j + 1) * P], ident_b[:])
                last.then_inc(pt_full, 1)

            def tie_counts(b):
                pe.wait_ge(pt_free_a, pt_done[pt_at[("eqT", b)]][0])
                o = ps_claim(("cum", b))
                n = keys(b)
                for j in range(b + 1):
                    for a in range(0, n, 512):
                        z, lo = min(a + 512, n), max(a, j * P)
                        if lo < z:
                            last = nc.tensor.matmul(o[:, lo:z], eqT[:, j * P:(j + 1) * P],
                                                    prefix[:, lo - j * P:z - j * P], start=(j == 0),
                                                    stop=(j == min(b, z // P - 1)))
                last.then_inc(ps_full, 1)
            for i in range(4):
                ci = name_of[("ga", i)]
                pe.wait_ge(w_lo_done, pieces_through[ci])
                for u, (m, f) in enumerate(UNITS):
                    channels(("ga", i, u), ci, m, f, hT_hi, hT_lo, KD)
                    if 4 * i + u in MASK_UNIT:
                        tie_transposes(MASK_UNIT[4 * i + u])
                    if 4 * i + u - 1 in MASK_UNIT:
                        tie_counts(MASK_UNIT[4 * i + u - 1])

            def branch_a(q):
                n, k = q // KA, q % KA
                i, u = n // 4, n % 4
                m, f = UNITS[u]
                ci = name_of[("wa", i)]
                if u == 0 and k == 0:
                    pe.wait_ge(w_lo_done, pieces_through[ci])
                o = pp_claim(("wa", i, u)) if k == 0 else pp[1]
                s, tok, ch = ci % 2, slice(f * HALF, (f + 1) * HALF), slice(m * P, (m + 1) * P)
                last = product(o[:], w_hi[:, s, k, ch], w_lo[:, s, k, ch], yT_hi[:, k, tok], yT_lo[:, k, tok],
                               k == 0, k == KA - 1)
                if k == KA - 1:
                    last.then_inc(pp_full, 1)
            pe.wait_ge(ya_hi, 2 * GROUPS)
            pe.wait_ge(ya_lo, 2 * GROUPS)
            for q in range(KA * WA_FIRST):
                branch_a(q)

            def q_transposes(b):
                pe.wait_ge(stk_hi, b + 1)
                pe.wait_ge(stk_lo, b + 1)
                for g in range(2):
                    o = pt_claim(("qT", b, g))
                    for j in range(4):
                        last = nc.tensor.transpose(o[:, j * P:(j + 1) * P].bitcast(F32R), q_stk[:, b % 2, 4 * g + j, :],
                                                   ident_r[:])
                    last.then_inc(pt_full, 1)
            q_transposes(0)
            for i in range(HEADS + 4):
                if i - 1 in MASK_STEP:
                    tie_transposes(MASK_STEP[i - 1])
                if i - 2 in MASK_STEP:
                    tie_counts(MASK_STEP[i - 2])
                if i < HEADS:
                    b, h = i // H, i % H
                    if h == 0:
                        pe.wait_ge(pt_free_a, pt_done[pt_at[("qT", b, 1)]][0])
                    o = ps_claim(("S", i))
                    two_pass(o, qT[:, b % 2, h, :], kT, keys(b)).then_inc(ps_full, 1)
                if i < KA * (16 - WA_FIRST):
                    branch_a(KA * WA_FIRST + i)
                if 0 <= i - 2 < HEADS:
                    j, b = i - 2, (i - 2) // H
                    pe.wait_ge(prob_done, j + 1)
                    for g in range((b + 4) // 4):
                        o = pt_claim(("PT", j, g))
                        for t in range(4 * g, min(4 * g + 4, b + 1)):
                            last = nc.tensor.transpose(o[:, (t % 4) * P:(t % 4 + 1) * P], prob[:, j % 2, t * P:(t + 1) * P],
                                                       ident[:])
                        last.then_inc(pt_full, 1)
                if 0 <= i - 3 < HEADS:
                    j, b, h = i - 3, (i - 3) // H, (i - 3) % H
                    wait_done(pe, pt_done[pt_at[("PT", j, b // 4)]], pt_free_a, pt_free_v)
                    o = pp_claim(("pv", b, h // 4)) if h % 4 == 0 else pp[0]
                    o = o[:, (h % 4) * P:(h % 4 + 1) * P]
                    for t in range(b + 1):
                        nc.tensor.matmul(o, pT_hi[:, j % 2, t, :], v2[:, t, :], start=(t == 0), stop=False)
                        last = nc.tensor.matmul(o, pT_lo[:, j % 2, t, :], v2[:, t, :], start=False, stop=(t == b))
                    last.then_inc(pv_done, 1)
                if i % H == 4 and i // H + 1 < NT:
                    q_transposes(i // H + 1)
                if i in YB_STEP:
                    yb_transposes(YB_STEP[i])

            def gate_rows(g):
                pe.wait_ge(gate_in, 32 * (g + 1))
                pe.wait_ge(gate_sum, g + 1)
                o = pt_claim(("gate", g))
                nc.tensor.matmul(o[:], ones[:], gate_acc[:], start=True, stop=False)
                nc.tensor.matmul(o[:], ones[0:1, :], gate[0:1, g * HALF:(g + 1) * HALF],
                                 start=False, stop=True).then_inc(pt_full, 1)

            wait_done(pe, pt_done[pt_at[("yb", NT - 1)]], pt_free_a, pt_free_v)
            for i in range(4):
                ci = name_of[("wb", i)]
                pe.wait_ge(w_lo_done, pieces_through[ci])
                for u, (m, f) in enumerate(UNITS):
                    channels(("wb", i, u), ci, m, f, yT_hi, yT_lo, KA)
            gate_rows(0)
            pe.wait_ge(mT_hi_done, 16)
            pe.wait_ge(mT_lo_done, 16)
            for i in range(4):
                ci = name_of[("wo", i)]
                pe.wait_ge(w_lo_done, pieces_through[ci])
                for t in range(NT):
                    o = pp_claim(("wo", i, t))
                    tok = slice(t * P, (t + 1) * P)
                    for k in range(KD):
                        last = product(o[:, 0:CW], mT_hi[:, k, tok], mT_lo[:, k, tok], w_hi[:, ci % 2, k, :],
                                       w_lo[:, ci % 2, k, :], k == 0, k == KD - 1)
                    last.then_inc(pp_full, 1)
                    if NT * i + t == GATE_UNIT:
                        gate_rows(1)

        @block.scalar
        def _(act):
            for t in [4, 5, 6, 7, 0, 1, 2, 3]:
                act.dma_start(x_in[:, t, :], x[t * P:(t + 1) * P, :]).then_inc(x_tile_in[t], 16)
            act.wait_ge(consts, 1)
            nc.scalar.activation(ident_r[:], ident[:], ACT.Copy)
            act.wait_ge(c_in, 16)
            nc.scalar.activation(c_silu[:], c_col[:], ACT.Silu).then_inc(c_silu_done, 1)
            for t in [4, 5, 6, 7, 0, 1, 2, 3]:
                act.wait_ge(x_tile_in[t], 16)
                nc.scalar.activation(ps[1][:], x_in[:, t, :], ACT.Square, accum_out=ssx[:, t:t + 1]).then_inc(ssx_done, 1)
                act.drain()
            act.wait_ge(dve_ready, V_MEAN)
            nc.scalar.activation(rx[:], ssx[:], ACT.Sqrt).then_inc(sqrt_done, 1)
            act.wait_ge(dve_ready, V_RSQRT)
            for t in [4, 5, 6, 7, 0, 1, 2, 3]:
                nc.scalar.activation(x_in[:, t, :], x_in[:, t, :], ACT.Copy, scale=rx[:, t:t + 1]).then_inc(xn_done, 1)
            nc.scalar.activation(trig[:], reduced[:], ACT.Sin).then_inc(trig_done, 1)
            split_chunk_hi(act, 0)

            def ht_hi(n):
                f, k = 1 - n // KD, n % KD
                act.wait_ge(h_raw_done, n + 1)
                nc.scalar.activation(hT_hi[:, k, f * HALF:(f + 1) * HALF], h_raw[:, n % 4, :],
                                     ACT.Copy).then_inc(hT_hi_done, 1)
            for n in range(KD):
                ht_hi(n)

            def pp_take(use):
                act.wait_ge(pp_full, pp_sig[pp_at[use]])
                return pp[pp_bank[pp_at[use]]]

            def pt_take(key):
                act.wait_ge(pt_full, pt_at[key] + 1)
                return pt[pt_at[key] % 2]

            def pooled_round(g):
                act.wait_ge(ua_used, g + 1)
                nc.scalar.activation(yT_hi[:, g, :], win[:, 0, :], ACT.Copy).then_inc(pooled_hi, 1)

            def yb_hi(b):
                o = pt_take(("yb", b))
                nc.scalar.activation(yT_hi[:, :, b * P:(b + 1) * P], o[:].rearrange("p (k q) -> p k q", q=P),
                                     ACT.Copy).then_inc(pt_free_a, 1)

            for i in range(2):
                for n, t in enumerate(QI_TILES):
                    o = pp_take(("qi", i, t))
                    nc.scalar.activation(qi[:, t - FREE_BLOCKS, i * CW:(i + 1) * CW], o[:, 0:CW],
                                         ACT.Copy).then_inc(pp_free_a, 1)
                    if i == 0 and n < 4:
                        ht_hi(KD + 2 * n)
                        ht_hi(KD + 2 * n + 1)
                    if i == 0 and n == 0:
                        split_chunk_hi(act, 1)
                    if i == 0 and n == 4:
                        act.wait_ge(group_in, 16)
                        nc.scalar.activation(wg_hi[:], wg_raw[:], ACT.Copy).then_inc(wg_hi_done, 1)
                split_chunk_hi(act, name_of[("qi", i)] + 2)
            for t in ALL_TILES:
                o = pp_take(("kv", 0, t))
                nc.scalar.activation(kr[:, t, :], o[:, 0:KR_W], ACT.Copy).then_inc(pp_free_a, 1)
            split_chunk_hi(act, name_of["kv"] + 2)

            def q_tile(i, t):
                o = pp_take(("q", i, t))
                nc.scalar.activation(q_all[:, t, i * CW:(i + 1) * CW], o[:, 0:CW], ACT.Copy).then_inc(pp_free_a, 1)

            def key_copy(kind, s, f):
                to = kiT if kind == "ki" else kT
                o = pt_take((kind, s, f))
                nc.scalar.activation(to[:, s, f * HALF:(f + 1) * HALF], o[:], ACT.Copy).then_inc(pt_free_a, 1)
            for t in range(NT):
                q_tile(0, t)
            split_chunk_hi(act, name_of[("q", 0)] + 2)

            def qi_split_hi(b):
                n = b - FREE_BLOCKS
                act.wait_ge(qi_roped, n + 1)
                if n:
                    act.wait_ge(pt_full, pt_at[("qi", b - 1, 1)] + 1)
                nc.scalar.activation(qi_stk[:, :, 0:HD], qi[:, n, :].rearrange("p (h d) -> p h d", d=HD),
                                     ACT.Copy).then_inc(qi_hi, 1)

            def qi_copies(b, groups=range(2)):
                for g in groups:
                    o = pt_take(("qi", b, g))
                    nc.scalar.activation(qiT[:, b % 2, 4 * g:4 * g + 4, :].rearrange("p h q -> p (h q)"), o[:],
                                         ACT.Copy).then_inc(pt_free_a, 1)

            def zb_tile(i, t):
                s = (i * NT + t) % 4
                if i * NT + t >= 4:
                    act.wait_ge(zb_spilled[s], 16 * ((i * NT + t) // 4))
                o = pp_take(("zb", i, t))
                nc.scalar.activation(zb_out[:, s, :], o[:, 0:CW], ACT.Silu).then_inc(pp_free_a, 1)
                act.wait_ge(pp_free_a, pp_at[("zb", i, t)] + 1)
                act.dma_start(zb_dram[t * P:(t + 1) * P, i * CW:(i + 1) * CW], zb_out[:, s, :]).then_inc(zb_spilled[s], 16)
            qi_split_hi(FREE_BLOCKS)
            for t in range(NT + 1):
                for key in Q_EXTRA.get(t, []):
                    if key[0] == "qi":
                        qi_copies(FREE_BLOCKS, [key[2]])
                    else:
                        key_copy(*key)
                    if key == ("ki", 0, 0):
                        act.wait_ge(var_ready, 1)
                        nc.scalar.activation(rk[:], ssk[:], ACT.Sqrt).then_inc(sqrt_done, 1)
                if t < NT:
                    q_tile(1, t)
            split_chunk_hi(act, name_of[("q", 1)] + 2)
            step = 0
            for b in range(FREE_BLOCKS, NT):
                for h in range(H):
                    n = (b - FREE_BLOCKS) * H + h
                    if h == 0 and b + 1 < NT:
                        qi_split_hi(b + 1)
                    act.wait_ge(ps_full, ps_value(("idx", b, h)))
                    if n >= 2:
                        act.wait_ge(rel_used, n - 1)
                    nc.scalar.activation(rel[:, n % 2, 0:keys(b)], ps[ps_at[("idx", b, h)] % 2][:, 0:keys(b)],
                                         ACT.Relu).then_inc(ps_free_a, 1)
                    if (b, h) == (FREE_BLOCKS, 1):
                        act.wait_ge(var_ready, 2)
                        nc.scalar.activation(rq[:], ssq[:], ACT.Sqrt).then_inc(sqrt_done, 1)
                    if h == 5 and b + 1 < NT:
                        qi_copies(b + 1)
                    for _ in range(zb_after[(b, h)]):
                        step += 1
                        if step % KD == 0:
                            zb_tile((step // KD - 1) // NT, (step // KD - 1) % NT)
                            if step == NT * KD:
                                split_chunk_hi(act, name_of[("zb", 0)] + 2)
            split_chunk_hi(act, name_of[("zb", 1)] + 2)

            act.wait_ge(q_spilled, 16 * NT)
            act.wait_ge(rel_used, NSEL * H)
            for s in range(4):
                act.wait_ge(zb_spilled[s], 16 * 4)

            def stage_slot(n):
                if n >= 4:
                    act.wait_ge(sg_out[n % 4], 16 * (n // 4))
                return n % 4

            def gate_unit(kind, i, u):
                m, f = UNITS[u]
                s = stage_slot((16 if kind == "ga" else 0) + 4 * i + u)
                o = pp_take((kind, i, u))
                nc.scalar.activation(stage[:, s, :], o[:], ACT.Sigmoid).then_inc(pp_free_a, 1)
                act.wait_ge(pp_free_a, pp_done[pp_at[(kind, i, u)]][0])
                r = (2 * i + m) * P
                act.dma_start((sga_dram if kind == "ga" else sgb_dram)[r:r + P, f * HALF:(f + 1) * HALF],
                              stage[:, s, :]).then_inc(sg_out[s], 16)
            for kind, i in C_ORDER:
                for u, (m, f) in enumerate(UNITS):
                    if kind == "ua":
                        g = 2 * i + m
                        if g >= 2:
                            act.wait_ge(pooled, g - 1)
                        o = pp_take((kind, i, u))
                        nc.scalar.activation(ua[:, g % 2, f * HALF:(f + 1) * HALF], o[:], ACT.Copy).then_inc(pp_free_a, 1)
                    else:
                        gate_unit(kind, i, u)
                    if (kind, i, u) in POOLED_ROUND:
                        pooled_round(POOLED_ROUND[kind, i, u])
                split_chunk_hi(act, name_of[(kind, i)] + 2)

            def ya_round(n):
                g, f = n // 2, n % 2
                act.wait_ge(ya_done, n + 1)
                nc.scalar.activation(yT_hi[:, g, f * HALF:(f + 1) * HALF], z_silu[:, g % 2, f * HALF:(f + 1) * HALF],
                                     ACT.Copy).then_inc(ya_hi, 1)
            act.wait_ge(pooled, GROUPS)
            for i in range(2):
                for m in range(2):
                    g = 2 * i + m
                    if g >= 2:
                        ya_round(2 * (g - 2))
                        ya_round(2 * (g - 2) + 1)
                        act.wait_ge(ya_lo, 2 * (g - 1))
                        act.wait_ge(ya_hi, 2 * (g - 1))
                    for f in range(2):
                        o = pp_take(("za", i, 2 * m + f))
                        nc.scalar.activation(z_silu[:, g % 2, f * HALF:(f + 1) * HALF], o[:], ACT.Silu).then_inc(pp_free_a, 1)
                    for f in range(2):
                        n = 2 * g + f
                        if n >= 2:
                            act.wait_ge(ya_done, n - 1)
                        o = pp_take(("mix", i, 2 * m + f))
                        nc.scalar.activation(mixed[:, n % 2, :], o[:], ACT.Copy, scale=col[:, 8 + g:9 + g]).then_inc(pp_free_a, 1)
                split_chunk_hi(act, name_of[("za", i)] + 2)
            for n in range(4, 8):
                ya_round(n)

            def tie_copy(b):
                o = pt_take(("eqT", b))[:].bitcast(BF16)
                nc.scalar.activation(eqT[:, 0:keys(b)], o[:, 0:keys(b)], ACT.Copy).then_inc(pt_free_a, 1)
            for i in range(4):
                for u in range(4):
                    gate_unit("ga", i, u)
                    if 4 * i + u in MASK_UNIT:
                        tie_copy(MASK_UNIT[4 * i + u])
                split_chunk_hi(act, name_of[("ga", i)] + 2)

            def load_sga(n):
                i, u = n // 4, n % 4
                m, f = UNITS[u]
                r = (2 * i + m) * P
                if n >= 4:
                    act.wait_ge(ma_out[n % 4], 16 * (n // 4))
                else:
                    act.wait_ge(sg_out[n], 16 * 8)
                act.dma_start(stage[:, n % 4, :], sga_dram[r:r + P, f * HALF:(f + 1) * HALF]).then_inc(sga_in[n % 4], 16)

            def branch_a_copy(n):
                i, u = n // 4, n % 4
                if n >= 2:
                    act.wait_ge(ma_full, n - 1)
                o = pp_take(("wa", i, u))
                nc.scalar.activation(a_out[:, n % 2, :], o[:], ACT.Copy).then_inc(pp_free_a, 1)
                if u == 3:
                    split_chunk_hi(act, name_of[("wa", i)] + 2)
                if 2 <= n < 14:
                    load_sga(n + 2)
            act.wait_ge(ya_lo, 8)
            act.wait_ge(ya_hi, 8)
            branch_a_copy(0)

            def load_q(b):
                if b >= 2:
                    act.wait_ge(stk_lo, b - 1)
                act.dma_start(q_row[:, b % 2, :], q_dram[b * P:(b + 1) * P, :]).then_inc(q_in[b % 2], 16)

            def load_z(b):
                if b >= 2:
                    act.wait_ge(y_done, 2 * (b - 1))
                act.dma_start(z_row[:, b % 2, :], zb_dram[b * P:(b + 1) * P, :]).then_inc(z_in[b % 2], 16)

            def q_split_hi(b):
                act.wait_ge(q_in[b % 2], 16 * (b // 2 + 1))
                if b >= 2:
                    act.wait_ge(pt_full, pt_at[("qT", b - 2, 1)] + 1)
                nc.scalar.activation(q_stk[:, b % 2, :, 0:HD], q_row[:, b % 2, :].rearrange("p (h d) -> p h d", d=HD),
                                     ACT.Copy).then_inc(stk_hi, 1)

            def q_copies(b):
                for g in range(2):
                    o = pt_take(("qT", b, g))
                    nc.scalar.activation(qT[:, b % 2, 4 * g:4 * g + 4, :].rearrange("p h q -> p (h q)"), o[:],
                                         ACT.Copy).then_inc(pt_free_a, 1)

            def load_gate(g):
                if g:
                    act.wait_ge(gate_sum, g)
                act.dma_start(gate_w[:], w_ada.rearrange("(p k) n -> p k n", k=KD)[
                    :, :, 2 * D + g * HALF:2 * D + (g + 1) * HALF]).then_inc(gate_in, 16)
                act.dma_start(gate[0:1, g * HALF:(g + 1) * HALF],
                              b_ada[:, 2 * D + g * HALF:2 * D + (g + 1) * HALF]).then_inc(gate_in, 16)
            act.wait_ge(pp_full, PP_HT)
            for b in range(2):
                load_q(b)
                load_z(b)
            for n in range(4):
                load_sga(n)
            q_split_hi(0)
            for n in range(1, WA_FIRST):
                branch_a_copy(n)
            q_copies(0)
            for i in range(HEADS + 4):
                if i - 1 in MASK_STEP:
                    tie_copy(MASK_STEP[i - 1])
                if 0 <= i - 1 < HEADS:
                    j, b, h = i - 1, (i - 1) // H, (i - 1) % H
                    act.wait_ge(logit_done, j + 1)
                    if j >= 2:
                        act.wait_ge(pt_full, pt_at[("PT", j - 2, (j - 2) // H // 4)] + 1)
                    if h % 4 == 0 and b >= 2:
                        act.wait_ge(o_sum, 2 * (b - 1))
                    r = (b % 2) * H + h
                    nc.scalar.activation(prob[:, j % 2, 0:keys(b)], logit[:, j % 2, 0:keys(b)], ACT.Exp, scale=-1.0,
                                         bias=neg_max[:, j % 2:j % 2 + 1],
                                         accum_out=row_sum[:, r:r + 1]).then_inc(prob_done, 1)
                if 0 <= i - 2 < HEADS:
                    j, b = i - 2, (i - 2) // H
                    if j >= 2:
                        act.wait_ge(pv_done, j - 1)
                    for g in range((b + 4) // 4):
                        t0, t1 = 4 * g, min(4 * g + 4, b + 1)
                        o = pt_take(("PT", j, g))
                        nc.scalar.activation(pT_hi[:, j % 2, t0:t1, :].rearrange("p t q -> p (t q)"), o[:, 0:(t1 - t0) * P],
                                             ACT.Copy).then_inc(pt_free_a, 1)
                if i % H == 2 and i // H + 1 < NT:
                    q_split_hi(i // H + 1)
                if i % H == 4 and i // H + 1 < NT:
                    q_copies(i // H + 1)
                if i % H == 5 and i // H + 2 < NT:
                    load_q(i // H + 2)
                if i in WA_STEP:
                    branch_a_copy(WA_STEP[i])
                if 0 <= i - 3 < HEADS and (i - 3) % 4 == 3:
                    n = (i - 3) // 4
                    if n >= 1:
                        act.wait_ge(o_sum, n)
                    act.wait_ge(pv_done, 4 * (n + 1))
                    o = pp[0][:].rearrange("p (h s d) -> p h s d", s=2, d=HD)
                    nc.scalar.activation(o_lo[:], o[:, :, 1, :], ACT.Copy).then_inc(o_lo_done, 1)
                if i % H == 4 and 2 <= i // H + 1 < NT:
                    load_z(i // H + 1)
                if i in YB_STEP:
                    yb_hi(YB_STEP[i])

            def gate_copy(g):
                o = pt_take(("gate", g))
                nc.scalar.activation(gate[:, g * HALF:(g + 1) * HALF], o[:], ACT.Copy).then_inc(pt_free_a, 1)

            def load_e(n):
                i, u = n // 4, n % 4
                m, f = UNITS[u]
                r = (2 * i + m) * P
                if n >= 4:
                    act.wait_ge(m_raw_done, n - 3)
                act.dma_start(e_in[:, 0, n % 4, :], sgb_dram[r:r + P, f * HALF:(f + 1) * HALF]).then_inc(e_loaded[n % 4], 16)
                act.dma_start(e_in[:, 1, n % 4, :], ma_dram[r:r + P, f * HALF:(f + 1) * HALF]).then_inc(e_loaded[n % 4], 16)
            act.wait_ge(logit_done, HEADS)
            act.wait_ge(ma_full, 16)
            for s in range(4):
                act.wait_ge(ma_out[s], 16 * 4)
            for n in range(4):
                load_e(n)
            act.wait_ge(pt_full, pt_at[("yb", NT - 1)] + 1)
            load_gate(0)
            act.wait_ge(pt_free_v, pt_done[pt_at[("yb", NT - 1)]][1])
            act.wait_ge(y_done, 2 * NT)
            for n in range(16):
                i, u = n // 4, n % 4
                m, f = UNITS[u]
                act.wait_ge(m_raw_done, n + 1)
                nc.scalar.activation(mT_hi[:, 2 * i + m, f * HALF:(f + 1) * HALF], m_raw[:, n % 4, :],
                                     ACT.Copy).then_inc(mT_hi_done, 1)
                if n + 4 < 16:
                    load_e(n + 4)
                if u == 3:
                    split_chunk_hi(act, name_of[("wb", i)] + 2)
            load_gate(1)
            gate_copy(0)

            act.wait_ge(m_raw_done, 16)
            def load_x(n):
                i, t = n // NT, n % NT
                if n >= 4:
                    act.wait_ge(o_row_done, n - 3)
                act.dma_start(x_row[:, n % 4, :], x[t * P:(t + 1) * P, i * CW:(i + 1) * CW]).then_inc(x_row_in[n % 4], 16)
            for n in range(4):
                load_x(n)
            for n in range(4 * NT):
                i, t = n // NT, n % NT
                act.wait_ge(o_row_done, n + 1)
                act.dma_start(out[t * P:(t + 1) * P, i * CW:(i + 1) * CW], o_row[:, n % 4, :]).then_inc(stored[n % 4], 16)
                if n + 4 < 4 * NT:
                    load_x(n + 4)
                if n == GATE_UNIT:
                    gate_copy(1)
                if t == NT - 1:
                    split_chunk_hi(act, name_of[("wo", i)] + 2)
            for s in range(4):
                act.wait_ge(stored[s], 16 * NT)

        @block.gpsimd
        def _(pool):
            gp = nc.gpsimd
            gp.memset(ident[:], 0.0)
            gp.memset(ident_b[:], 0.0)
            gp.memset(prefix[:], 1.0)
            gp.memset(diag_bias[:], 0.0)
            gp.memset(ones[:], 1.0)
            for n in range(16):
                gp.memset(recip_n[:, n:n + 1], 1.0 / (n + 1))
            pool.drain()
            for m in (ident, ident_b):
                gp.affine_select(out=m[:], in_=m[:], compare_op=ALU.not_equal, fill=1.0, base=0,
                                 pattern=[[-1, P]], channel_multiplier=1)
            gp.affine_select(out=prefix[:, 0:P], in_=prefix[:, 0:P], compare_op=ALU.is_ge, fill=0.0, base=0,
                             pattern=[[1, P]], channel_multiplier=-1)
            gp.affine_select(out=diag_bias[:], in_=diag_bias[:], compare_op=ALU.is_ge, fill=NEG_BIAS, base=0,
                             pattern=[[-1, P]], channel_multiplier=1)
            pool.drain()
            gp.memset(rope_a[:], 0.0).then_inc(consts, 1)

            def ht_lo(n):
                f, k = 1 - n // KD, n % KD
                pool.wait_ge(hT_hi_done, n + 1)
                tok = slice(f * HALF, (f + 1) * HALF)
                gp.tensor_tensor(hT_lo[:, k, tok], h_raw[:, n % 4, :], hT_hi[:, k, tok].bitcast(F32),
                                 ALU.subtract).then_inc(hT_lo_p, 1)
            split_chunk_lo(pool, 0)
            for n in range(1, KD, 2):
                ht_lo(n)
            for n in range(KD + 1, 2 * KD, 2):
                ht_lo(n)
            split_chunk_lo(pool, 1)
            pool.wait_ge(wg_hi_done, 1)
            gp.tensor_tensor(wg_lo[:], wg_raw[:], wg_hi[:].bitcast(F32), ALU.subtract).then_inc(wg_lo_done, 1)

            def rope(v, t):
                cc = rot_c[:, t, :].unsqueeze(1).to_broadcast([P, H, ROT])
                ss = rot_s[:, t, :].unsqueeze(1).to_broadcast([P, H, ROT])
                gp.tensor_tensor(rope_a[:], v[:, :, 0:ROT], cc, ALU.mult)
                gp.tensor_tensor(rope_b[:, :, 0:NF], v[:, :, NF:ROT], ss[:, :, 0:NF], ALU.mult)
                gp.tensor_tensor(rope_b[:, :, NF:ROT], v[:, :, 0:NF], ss[:, :, NF:ROT], ALU.mult)
                pool.drain()
                return gp.tensor_tensor(v[:, :, 0:ROT], rope_a[:], rope_b[:], ALU.add)

            def qi_split_lo(b):
                n = b - FREE_BLOCKS
                pool.wait_ge(qi_hi, n + 1)
                nc.gpsimd.tensor_tensor(qi_stk[:, :, HD:2 * HD], qi[:, n, :].rearrange("p (h d) -> p h d", d=HD),
                                        qi_stk[:, :, 0:HD].bitcast(F32), ALU.subtract).then_inc(qi_lo, 1)

            def ya_rest(n):
                g, f = n // 2, n % 2
                tok = slice(f * HALF, (f + 1) * HALF)
                pool.wait_ge(ya_hi, n + 1)
                nc.gpsimd.tensor_tensor(yT_lo[:, g, tok], z_silu[:, g % 2, tok], yT_hi[:, g, tok].bitcast(F32),
                                        ALU.subtract).then_inc(ya_lo, 1)

            pool.wait_ge(pp_free_a, pp_at[("qi", 0, QI_TILES[-1])] + 1)
            split_chunk_lo(pool, 2)
            pool.wait_ge(trig_done, 2)
            for n in range(NSEL):
                t = n + FREE_BLOCKS
                pool.wait_ge(pp_free_a, pp_at[("qi", 1, 3)] + 1)
                rope(qi[:, n, :].rearrange("p (h d) -> p h d", d=HD), t).then_inc(qi_roped, 1)
                pool.wait_ge(qi_roped, n + 1)
                if n == 0:
                    split_chunk_lo(pool, 3)
            split_chunk_lo(pool, 4)
            split_chunk_lo(pool, 5)
            qi_split_lo(FREE_BLOCKS)

            def finish_query(t):
                pool.wait_ge(q_scaled, t + 1)
                rope(q_all[:, t, :].rearrange("p (h d) -> p h d", d=HD), t).then_inc(q_roped, 1)
                pool.wait_ge(q_roped, t + 1)
                pool.dma_start(q_dram[t * P:(t + 1) * P, :], q_all[:, t, :]).then_inc(q_spilled, 16)

            def causal_scores(b):
                pool.wait_ge(block_scored, b - FREE_BLOCKS + 1)
                own = slice(score_at(b) + b * P, score_at(b) + (b + 1) * P)
                gp.affine_select(out=score[:, own], in_=score[:, own], compare_op=ALU.is_ge, fill=MASKED, base=0,
                                 pattern=[[-1, P]], channel_multiplier=1).then_inc(masked, 1)
            for b in range(FREE_BLOCKS, NT):
                if b + 1 < NT:
                    qi_split_lo(b + 1)
                if b == FREE_BLOCKS + 1:
                    split_chunk_lo(pool, 6)
                for t in SCALED[b].values():
                    finish_query(t)
                if b > FREE_BLOCKS:
                    causal_scores(b - 1)
                if b == 5:
                    split_chunk_lo(pool, 7)
            causal_scores(NT - 1)
            split_chunk_lo(pool, 8)

            pool.wait_ge(q_spilled, 16 * NT)
            for s in range(4):
                pool.wait_ge(zb_spilled[s], 16 * 4)

            def window_mean(g):
                w = 2 << g
                pool.wait_ge(pp_free_a, pp_at[("ua", g // 2, 2 * (g % 2) + 1)] + 1)
                if g:
                    pool.wait_ge(pooled, g)
                cur, s, side = ua[:, g % 2, :], 1, 0
                while s < w:
                    nxt = win[:, side, :]
                    gp.tensor_copy(nxt[:, 0:s], cur[:, 0:s])
                    gp.tensor_tensor(nxt[:, s:L], cur[:, s:L], cur[:, 0:L - s], ALU.add)
                    pool.drain()
                    cur, s, side = nxt, 2 * s, 1 - side
                other = win[:, side, :]
                gp.tensor_scalar(other[:, w:L], cur[:, w:L], 1.0 / w, None, ALU.mult)
                gp.tensor_tensor(other[:, 0:w], cur[:, 0:w], recip_n[:, 0:w], ALU.mult)
                pool.drain()
                gp.tensor_tensor(win[:, 0, :], other, ua[:, g % 2, :], ALU.subtract).then_inc(ua_used, 1)

            def pooled_low(g):
                pool.wait_ge(pooled_hi, g + 1)
                gp.tensor_tensor(yT_lo[:, g, :], win[:, 0, :], yT_hi[:, g, :].bitcast(F32), ALU.subtract).then_inc(pooled, 1)
            split_chunk_lo(pool, name_of["ua", 0] + 2)
            window_mean(0)
            split_chunk_lo(pool, name_of["gb", 0] + 2)
            pooled_low(0)
            window_mean(1)
            split_chunk_lo(pool, name_of["gb", 1] + 2)
            pooled_low(1)
            window_mean(2)
            split_chunk_lo(pool, name_of["ua", 1] + 2)
            pooled_low(2)
            window_mean(3)
            split_chunk_lo(pool, name_of["gb", 2] + 2)
            pooled_low(3)
            split_chunk_lo(pool, name_of["gb", 3] + 2)
            for n in range(2 * GROUPS):
                g, f = n // 2, n % 2
                tok = slice(f * HALF, (f + 1) * HALF)
                pool.wait_ge(pp_free_a, pp_at[("mix", g // 2, 2 * (g % 2) + f)] + 1)
                gp.tensor_tensor(z_silu[:, g % 2, tok], mixed[:, n % 2, :], z_silu[:, g % 2, tok], ALU.mult).then_inc(ya_done, 1)
                if n >= 2:
                    ya_rest(n - 2)
                if n % 4 == 3:
                    split_chunk_lo(pool, name_of[("za", n // 4)] + 2)
            ya_rest(2 * GROUPS - 2)
            ya_rest(2 * GROUPS - 1)
            for i in range(4):
                split_chunk_lo(pool, name_of[("ga", i)] + 2)

            def q_split_lo(b):
                pool.wait_ge(stk_hi, b + 1)
                gp.tensor_tensor(q_stk[:, b % 2, :, HD:2 * HD], q_row[:, b % 2, :].rearrange("p (h d) -> p h d", d=HD),
                                 q_stk[:, b % 2, :, 0:HD].bitcast(F32), ALU.subtract).then_inc(stk_lo, 1)

            def gated_a(n):
                i, u = n // 4, n % 4
                m, f = UNITS[u]
                r = (2 * i + m) * P
                pool.wait_ge(pp_free_a, pp_done[pp_at[("wa", i, u)]][0])
                pool.wait_ge(sga_in[n % 4], 16 * (n // 4 + 1))
                gp.tensor_tensor(stage[:, n % 4, :], a_out[:, n % 2, :], stage[:, n % 4, :], ALU.mult).then_inc(ma_full, 1)
                pool.wait_ge(ma_full, n + 1)
                pool.dma_start(ma_dram[r:r + P, f * HALF:(f + 1) * HALF], stage[:, n % 4, :]).then_inc(ma_out[n % 4], 16)
                if u == 3:
                    split_chunk_lo(pool, name_of[("wa", i)] + 2)
            q_split_lo(0)
            for n in range(WA_FIRST):
                gated_a(n)
            for i in range(HEADS + 4):
                if i % H == 2 and i // H + 1 < NT:
                    q_split_lo(i // H + 1)
                if i in WA_STEP:
                    gated_a(WA_STEP[i])
                if 0 <= i - 3 < HEADS and (i - 3) % 4 == 3:
                    n = (i - 3) // 4
                    b, f = n // 2, n % 2
                    pool.wait_ge(o_sum, n + 1)
                    pool.wait_ge(z_in[b % 2], 16 * (b // 2 + 1))
                    y = y_row[:, b, 4 * f * HD:4 * (f + 1) * HD]
                    gp.tensor_tensor(y, y, z_row[:, b % 2, 4 * f * HD:4 * (f + 1) * HD], ALU.mult).then_inc(y_done, 1)
            pool.wait_ge(pt_full, pt_at[("yb", NT - 1)] + 1)
            pool.wait_ge(pt_free_v, pt_done[pt_at[("yb", NT - 1)]][1])
            for n in range(16):
                i, u = n // 4, n % 4
                m, f = UNITS[u]
                tok = slice(f * HALF, (f + 1) * HALF)
                pool.wait_ge(mT_hi_done, n + 1)
                gp.tensor_tensor(mT_lo[:, 2 * i + m, tok], m_raw[:, n % 4, :], mT_hi[:, 2 * i + m, tok].bitcast(F32),
                                 ALU.subtract).then_inc(mT_lo_done, 1)
                if u == 3:
                    split_chunk_lo(pool, name_of[("wb", i)] + 2)
            for i in range(4):
                split_chunk_lo(pool, name_of[("wo", i)] + 2)

        @block.vector
        def _(dve):
            v = nc.vector
            for k in range(31):
                v.memset(bit_i[:, k:k + 1], 1 << (30 - k))
                v.memset(bit_f[:, k:k + 1], float(1 << (30 - k)))
            v.memset(bit_i[:, 31:32], 0)
            v.memset(bit_f[:, 31:32], 0.0)
            dve.wait_ge(cols_in, 64)
            v.tensor_copy(pos_f[:], pos_i[:]).then_inc(dve_ready, 1)
            dve.wait_ge(pt_full, pt_at["cols"] + 1)
            v.tensor_copy(col[:], pt[0][:, 0:28])
            v.tensor_copy(pos_col[:], pt[0][:, 32:32 + NT]).then_inc(pt_free_v, 1)
            dve.wait_ge(pt_full, pt_at["gains"] + 1)
            v.tensor_copy(gains[:], pt[1][:, 0:2 * HD]).then_inc(pt_free_v, 1)
            dve.drain()
            v.tensor_scalar(nx[:], pos_col[:], 0.0, None, ALU.add).then_inc(dve_ready, 1)
            for k in range(NF):
                v.tensor_scalar(angle[:, :, k], pos_col[:], float(np.float32(THETA ** (-2.0 * k / ROT))), None, ALU.mult)
            dve.drain()
            ang = angle[:].rearrange("p t f -> p (t f)")
            v.tensor_scalar(turns[:, 0, :], ang, float(1 / (2 * np.pi)), MAGIC, ALU.mult, ALU.add)
            v.tensor_scalar(turns[:, 1, :], ang, float(1 / (2 * np.pi)), 0.25, ALU.mult, ALU.add)
            dve.drain()
            v.tensor_scalar(turns[:, 1, :], turns[:, 1, :], MAGIC, None, ALU.add)
            dve.drain()
            v.tensor_scalar(turns[:], turns[:], MAGIC, None, ALU.subtract)
            dve.drain()
            for s in range(2):
                v.scalar_tensor_tensor(reduced[:, s, :], turns[:, s, :], -TWO_PI[0], ang, ALU.mult, ALU.add)
            for part in TWO_PI[1:]:
                dve.drain()
                v.scalar_tensor_tensor(reduced[:], turns[:], -part, reduced[:], ALU.mult, ALU.add)
            dve.drain()
            v.tensor_scalar(reduced[:, 1, :], reduced[:, 1, :], float(np.pi / 2), None, ALU.add)
            dve.drain()
            v.tensor_scalar(reduced[:], reduced[:], 3.1415925, -3.1415925, ALU.min, ALU.max).then_inc(dve_ready, 1)

            def rsqrt_step(y, mean, tmp):
                v.reciprocal(y, y)
                dve.drain()
                v.tensor_tensor(tmp, y, y, ALU.mult)
                dve.drain()
                v.tensor_tensor(tmp, tmp, mean, ALU.mult)
                dve.drain()
                v.tensor_scalar(tmp, tmp, -0.5, 1.5, ALU.mult, ALU.add)
                dve.drain()
                v.tensor_tensor(y, y, tmp, ALU.mult)
                dve.drain()

            def ada_products(i):
                for k in range(KD):
                    if k % (KD // 2) == 0:
                        dve.wait_ge(ada_in[2 * i + 2 * k // KD], 16)
                    c = c_silu[:, k:k + 1]
                    if k == 0:
                        v.tensor_scalar(ada_acc[:, i, :], ada_w[:, i, k, :], c, None, ALU.mult)
                    else:
                        dve.drain()
                        ins = v.scalar_tensor_tensor(ada_acc[:, i, :], ada_w[:, i, k, :], c, ada_acc[:, i, :],
                                                     ALU.mult, ALU.add)
                ins.then_inc(ada_sum, 1)
            dve.wait_ge(c_silu_done, 1)
            ada_products(0)
            dve.wait_ge(ssx_done, NT)
            v.tensor_scalar(ssx[:], ssx[:], 1.0 / D, EPS, ALU.mult, ALU.add).then_inc(dve_ready, 1)
            dve.wait_ge(sqrt_done, 1)
            rsqrt_step(rx[:], ssx[:], nx[:])
            v.tensor_copy(nx[:], rx[:]).then_inc(dve_ready, 1)
            ada_products(1)
            ada_products(2)
            ada_products(3)
            dve.wait_ge(trig_done, 1)
            sin, cos = (trig[:, s, :].rearrange("p (t f) -> p t f", f=NF) for s in range(2))
            v.tensor_copy(rot_c[:, :, 0:NF], cos)
            v.tensor_copy(rot_c[:, :, NF:ROT], cos)
            v.tensor_scalar(rot_s[:, :, 0:NF], sin, -1.0, None, ALU.mult)
            v.tensor_copy(rot_s[:, :, NF:ROT], sin)
            dve.drain()
            v.tensor_copy(nq[:, 0:1], rx[:, 0:1]).then_inc(trig_done, 1)
            dve.wait_ge(ps_full, 4)
            v.tensor_tensor(shift[:], ps[0][:, 0:2 * KD], col[:, 12:28], ALU.add).then_inc(ps_free_v, 1)
            dve.drain()
            v.tensor_scalar(gmul[:], shift[:, KD:2 * KD], 1.0, None, ALU.add)
            dve.drain()
            v.tensor_tensor(gmul[:], gmul[:], col[:, 0:KD], ALU.mult)
            dve.drain()
            def ht_lo(j):
                f, k = 1 - j // KD, j % KD
                tok = slice(f * HALF, (f + 1) * HALF)
                dve.wait_ge(hT_hi_done, j + 1)
                v.tensor_tensor(hT_lo[:, k, tok], h_raw[:, j % 4, :], hT_hi[:, k, tok].bitcast(F32),
                                ALU.subtract).then_inc(hT_lo_v, 1)
            for n in range(2 * KD + 2):
                if n == KD:
                    ht_lo(n - 2)
                if n < 2 * KD:
                    k = n % KD
                    dve.wait_ge(pt_full, pt_at[("h", n)] + 1)
                    if n >= 4:
                        if n % 2 == 0:
                            dve.wait_ge(hT_lo_v, (n - 4) // 2 + 1)
                        else:
                            dve.wait_ge(hT_lo_p, (n - 5) // 2 + 1)
                    v.tensor_scalar(h_raw[:, n % 4, :], pt[pt_at[("h", n)] % 2][:], gmul[:, k:k + 1], shift[:, k:k + 1],
                                    ALU.mult, ALU.add).then_inc(h_raw_done, 1)
                    dve.wait_ge(h_raw_done, n + 1)
                    dve.sem_inc(pt_free_v, 1)
                if n >= 2 and n % 2 == 0 and n != KD:
                    ht_lo(n - 2)

            dve.wait_ge(wg_lo_done, 1)
            dve.wait_ge(pp_free_a, pp_at[("kv", 0, 3)] + 1)
            ki, kk, vv = kr[:, :, KR_KI:KR_KI + HD], kr[:, :, KR_K:KR_K + HD], kr[:, :, KR_V:KR_V + HD]
            tmp_a = score[:, 0:NT * ROT].rearrange("p (t r) -> p t r", r=ROT)
            tmp_b = score[:, NT * ROT:2 * NT * ROT].rearrange("p (t r) -> p t r", r=ROT)

            def rope_keys(u):
                v.tensor_tensor(tmp_a, u[:, :, 0:ROT], rot_c[:], ALU.mult)
                v.tensor_tensor(tmp_b[:, :, 0:NF], u[:, :, NF:ROT], rot_s[:, :, 0:NF], ALU.mult)
                v.tensor_tensor(tmp_b[:, :, NF:ROT], u[:, :, 0:NF], rot_s[:, :, NF:ROT], ALU.mult)
                dve.drain()
                v.tensor_tensor(u[:, :, 0:ROT], tmp_a, tmp_b, ALU.add)
                dve.drain()

            def stack_keys(u):
                for s in range(2):
                    v.tensor_copy(kst[:, 0, :, s * HD:(s + 1) * HD], u)
                dve.drain()
                v.tensor_tensor(kst[:, 1, :, 0:HD], u, kst[:, 0, :, 0:HD].bitcast(F32), ALU.subtract)
                v.tensor_tensor(kst[:, 1, :, HD:2 * HD], u, kst[:, 0, :, HD:2 * HD].bitcast(F32),
                                ALU.subtract).then_inc(kst_ready, 1)
            rope_keys(ki)
            stack_keys(ki)
            v.tensor_scalar(w_idx[:], kr[:, :, KR_WI:KR_WI + H], IDX_SCALE, None, ALU.mult)
            v.tensor_copy(v2[:, :, 0:HD], vv)
            dve.drain()
            v.tensor_tensor(v2[:, :, HD:2 * HD], vv, v2[:, :, 0:HD].bitcast(F32), ALU.subtract)
            sq = score[:, 512:512 + NT * HD].rearrange("p (t d) -> p t d", d=HD)
            v.tensor_tensor(sq, kk, kk, ALU.mult)
            dve.drain()
            v.tensor_reduce(ssk[:], sq, AX.X, ALU.add)
            dve.drain()
            v.tensor_scalar(ssk[:], ssk[:], 1.0 / HD, EPS, ALU.mult, ALU.add).then_inc(var_ready, 1)
            dve.wait_ge(sqrt_done, 2)
            rsqrt_step(rk[:], ssk[:], nk[:])
            v.tensor_tensor(kk, kk, rk[:].unsqueeze(2).to_broadcast([P, NT, HD]), ALU.mult)
            dve.drain()
            v.tensor_tensor(kk, kk, gains[:, HD:2 * HD].unsqueeze(1).to_broadcast([P, NT, HD]), ALU.mult)
            dve.drain()
            rope_keys(kk)
            dve.wait_ge(pt_full, pt_at[("ki", 1, 1)] + 1)
            stack_keys(kk)
            for t in range(NT):
                dve.wait_ge(pp_free_a, pp_at[("q", 1, t)] + 1)
                sq = score[:, 512 * (1 + t % 2):512 * (2 + t % 2)]
                v.tensor_tensor(sq, q_all[:, t, :], q_all[:, t, :], ALU.mult)
                dve.drain()
                v.tensor_reduce(ssq[:, t * H:(t + 1) * H], sq.rearrange("p (h d) -> p h d", d=HD), AX.X, ALU.add)
            dve.drain()
            v.tensor_scalar(ssq[:], ssq[:], 1.0 / HD, EPS, ALU.mult, ALU.add).then_inc(var_ready, 1)

            def scale_query(t):
                qv = q_all[:, t, :].rearrange("p (h d) -> p h d", d=HD)
                v.tensor_tensor(qv, qv, rq[:, t * H:(t + 1) * H].unsqueeze(2).to_broadcast([P, H, HD]), ALU.mult)
                dve.drain()
                v.tensor_tensor(qv, qv, gains[:, 0:HD].unsqueeze(1).to_broadcast([P, H, HD]), ALU.mult).then_inc(q_scaled, 1)
            for b in range(FREE_BLOCKS, NT):
                s = score[:, score_at(b):score_at(b + 1)]
                for h in range(H):
                    n = (b - FREE_BLOCKS) * H + h
                    dve.wait_ge(ps_free_a, n + 1)
                    w = w_idx[:, b, h:h + 1]
                    if h == 0:
                        ins = v.tensor_scalar(s, rel[:, n % 2, 0:keys(b)], w, None, ALU.mult)
                    else:
                        dve.wait_ge(rel_used, n)
                        ins = v.scalar_tensor_tensor(s, rel[:, n % 2, 0:keys(b)], w, s, ALU.mult, ALU.add)
                    ins.then_inc(rel_used, 1)
                    if (b, h) == (FREE_BLOCKS, 2):
                        dve.wait_ge(sqrt_done, 3)
                        rsqrt_step(rq[:], ssq[:], nq[:])
                    if h in SCALED[b]:
                        scale_query(SCALED[b][h])
                dve.wait_ge(rel_used, (b - FREE_BLOCKS + 1) * H)
                dve.sem_inc(block_scored, 1)

            dve.wait_ge(masked, NSEL)
            dve.wait_ge(pt_free_a, pt_done[pt_at[("qi", NT - 1, 1)]][0])
            for s in range(4):
                dve.wait_ge(zb_spilled[s], 16 * 4)

            def count(at_least):
                for n in range(NSEL):
                    b = n + FREE_BLOCKS
                    least = at_least if at_least is not None else cand[:, n:n + 1].bitcast(F32)
                    if n and n % 2 == 0:
                        dve.drain()
                    v.tensor_scalar(junk[:, n % 2, 0:keys(b)], score[:, score_at(b):score_at(b + 1)], least, None,
                                    ALU.is_ge, ALU.add, accum_out=cnt[:, n:n + 1])
                dve.drain()
            count(0.0)
            v.tensor_scalar(thr[:], cnt[:], TOPK - 0.5, -1.0, ALU.is_lt, ALU.mult)
            dve.drain()
            v.tensor_scalar(cand[:], thr[:], bit_i[:, 0:1], None, ALU.bitwise_xor)
            dve.drain()
            with dve.Fori(0, 31) as k:
                count(None)
                v.tensor_scalar(accept[:], cnt[:], TOPK - 0.5, bit_f[:, bass.ds(k, 1)], ALU.is_ge, ALU.mult)
                dve.drain()
                v.scalar_tensor_tensor(cand[:], accept[:], bit_i[:, bass.ds(k + 1, 1)], thr[:],
                                       ALU.bitwise_xor, ALU.bitwise_xor)
                v.tensor_tensor(thr[:], thr[:], accept[:], ALU.bitwise_xor)
                dve.drain()

            dve.wait_ge(ya_hi, 2 * GROUPS)
            dve.wait_ge(ya_lo, 2 * GROUPS)
            for b in range(FREE_BLOCKS):
                if b:
                    v.memset(bias[:, bias_at(b):bias_at(b) + b * P], 0.0)
                v.tensor_copy(bias[:, bias_at(b) + b * P:bias_at(b + 1)], diag_bias[:])
            dve.drain()
            dve.sem_inc(bias_ready, 1)

            def mask_begin(b):
                n = b - FREE_BLOCKS
                t = thr[:, n:n + 1].bitcast(F32)
                s = score[:, score_at(b):score_at(b + 1)]
                v.tensor_scalar(gt[:, 0:keys(b)], s, t, None, ALU.is_gt, ALU.add, accum_out=cnt[:, n:n + 1])
                v.tensor_scalar(eq[:, 0:keys(b)], s, t, None, ALU.is_equal).then_inc(eq_ready, 1)
                dve.drain()
                v.tensor_scalar(need[:], cnt[:, n:n + 1], -1.0, float(TOPK), ALU.mult, ALU.add)
                dve.drain()

            def mask_end(b):
                dve.wait_ge(ps_full, ps_value(("cum", b)))
                o = ps[ps_at[("cum", b)] % 2]
                v.scalar_tensor_tensor(eq[:, 0:keys(b)], o[:, 0:keys(b)], need[:], eq[:, 0:keys(b)],
                                       ALU.is_le, ALU.mult).then_inc(ps_free_v, 1)
                dve.drain()
                v.tensor_tensor(gt[:, 0:keys(b)], gt[:, 0:keys(b)], eq[:, 0:keys(b)], ALU.add)
                dve.drain()
                v.tensor_scalar(bias[:, bias_at(b):bias_at(b + 1)], gt[:, 0:keys(b)], 1.0, -NEG_BIAS,
                                ALU.subtract, ALU.mult).then_inc(bias_ready, 1)
                dve.drain()

            def pT_low(j):
                b = j // H
                if j >= 2:
                    dve.wait_ge(pv_done, j - 1)
                for g in range((b + 4) // 4):
                    t0, t1 = 4 * g, min(4 * g + 4, b + 1)
                    n = pt_at[("PT", j, g)]
                    dve.wait_ge(pt_free_a, pt_done[n][0])
                    v.tensor_tensor(pT_lo[:, j % 2, t0:t1, :].rearrange("p t q -> p (t q)"), pt[n % 2][:, 0:(t1 - t0) * P],
                                    pT_hi[:, j % 2, t0:t1, :].rearrange("p t q -> p (t q)").bitcast(F32),
                                    ALU.subtract).then_inc(pt_free_v, 1)

            def outputs(n):
                b, f = n // 2, n % 2
                r = (b % 2) * H + 4 * f
                v.reciprocal(row_inv[:], row_sum[:, r:r + 4])
                dve.wait_ge(o_lo_done, n + 1)
                y = y_row[:, b, 4 * f * HD:4 * (f + 1) * HD].rearrange("p (h d) -> p h d", d=HD)
                o = pp[0][:].rearrange("p (h s d) -> p h s d", s=2, d=HD)
                v.tensor_tensor(y, o[:, :, 0, :], o_lo[:], ALU.add).then_inc(pp_free_v, 1)
                dve.drain()
                v.tensor_tensor(y, y, row_inv[:].unsqueeze(2).to_broadcast([P, 4, HD]), ALU.mult).then_inc(o_sum, 1)

            def yb_low(b):
                n = pt_at[("yb", b)]
                dve.wait_ge(pt_free_a, pt_done[n][0])
                v.tensor_tensor(yT_lo[:, :, b * P:(b + 1) * P], pt[n % 2][:].rearrange("p (k q) -> p k q", q=P),
                                yT_hi[:, :, b * P:(b + 1) * P].bitcast(F32), ALU.subtract).then_inc(pt_free_v, 1)
            for b in MASK_UNIT.values():
                mask_begin(b)
                mask_end(b)
            dve.wait_ge(pp_full, PP_HT)
            for i in range(HEADS + 4):
                if i - 2 in MASK_STEP:
                    mask_end(MASK_STEP[i - 2])
                if i in MASK_STEP:
                    mask_begin(MASK_STEP[i])
                if i < HEADS:
                    b = i // H
                    dve.wait_ge(ps_full, ps_value(("S", i)))
                    if i >= 2:
                        dve.wait_ge(prob_done, i - 1)
                    v.tensor_tensor_reduce(logit[:, i % 2, 0:keys(b)], ps[ps_at[("S", i)] % 2][:, 0:keys(b)],
                                           bias[:, bias_at(b):bias_at(b + 1)], -ATT_SCALE, 3.0e38, ALU.add, ALU.min,
                                           neg_max[:, i % 2:i % 2 + 1]).then_inc(logit_done, 1)
                    dve.wait_ge(logit_done, i + 1)
                    dve.sem_inc(ps_free_v, 1)
                if 0 <= i - 2 < HEADS:
                    pT_low(i - 2)
                if 0 <= i - 3 < HEADS and (i - 3) % 4 == 3:
                    outputs((i - 3) // 4)
                if i in YB_STEP:
                    yb_low(YB_STEP[i])
            for s in range(4):
                dve.wait_ge(ma_out[s], 16 * 4)


            def gate_add(g, k):
                c = c_silu[:, k:k + 1]
                if k == 0:
                    dve.wait_ge(gate_in, 32 * (g + 1))
                    if g:
                        dve.wait_ge(pt_full, pt_at[("gate", g - 1)] + 1)
                    ins = v.tensor_scalar(gate_acc[:], gate_w[:, k, :], c, None, ALU.mult)
                else:
                    ins = v.scalar_tensor_tensor(gate_acc[:], gate_w[:, k, :], c, gate_acc[:], ALU.mult, ALU.add)
                if k == KD - 1:
                    ins.then_inc(gate_sum, 1)
                else:
                    dve.drain()
            for n in range(16):
                u = pp_at[("wb", n // 4, n % 4)]
                dve.wait_ge(pp_full, pp_sig[u])
                dve.wait_ge(e_loaded[n % 4], 32 * (n // 4 + 1))
                if n >= 4:
                    dve.wait_ge(mT_lo_done, n - 3)
                v.tensor_tensor(m_raw[:, n % 4, :], pp[pp_bank[u]][:], e_in[:, 0, n % 4, :], ALU.mult).then_inc(pp_free_v, 1)
                dve.drain()
                v.tensor_tensor(m_raw[:, n % 4, :], m_raw[:, n % 4, :], e_in[:, 1, n % 4, :], ALU.add).then_inc(m_raw_done, 1)
                if 0 <= n - 7 < KD:
                    gate_add(0, n - 7)
            for n in range(4 * NT):
                i = n // NT
                u = pp_at[("wo", i, n % NT)]
                if n % (2 * NT) == 0:
                    dve.wait_ge(pt_free_a, pt_done[pt_at[("gate", n // (2 * NT))]][0])
                dve.wait_ge(pp_full, pp_sig[u])
                dve.wait_ge(x_row_in[n % 4], 16 * (n // 4 + 1))
                if n >= 4:
                    dve.wait_ge(stored[n % 4], 16 * (n // 4))
                v.tensor_tensor(o_row[:, n % 4, :], pp[pp_bank[u]][:, 0:CW], gate[:, i * CW:(i + 1) * CW],
                                ALU.mult).then_inc(pp_free_v, 1)
                dve.drain()
                v.tensor_tensor(o_row[:, n % 4, :], o_row[:, n % 4, :], x_row[:, n % 4, :], ALU.add).then_inc(o_row_done, 1)
                if 0 <= n - 1 < KD:
                    gate_add(1, n - 1)


_INS = ["x", "c", "positions", "w_ada", "b_ada", "norm_gain", "w_in", "w_pool_group", "pool_scale",
        "q_norm_gain", "k_norm_gain", "w_branch_a", "w_branch_b", "w_out"]


def kernel(**inputs):
    import concourse.bacc as bacc
    from concourse.bass_utils import run_bass_kernel_spmd

    nc = bacc.Bacc("TRN2", target_bir_lowering=False, num_devices=1)
    arrays, args = {}, []
    for name in _INS:
        a = np.ascontiguousarray(inputs[name])
        arrays[f"in_{name}"] = a
        args.append(nc.dram_tensor(f"in_{name}", a.shape, mybir.dt.from_np(a.dtype), kind="ExternalInput").ap())
    args.append(nc.dram_tensor("out", (1, L, D), F32, kind="ExternalOutput").ap())
    hybrid_layer(nc, *args)
    r = run_bass_kernel_spmd(nc, [arrays], core_ids=[0])
    return r.results[0]["out"]
```

```python
from contextlib import ExitStack

import numpy as np
import concourse.bass as bass
from concourse import mybir

F32, F32R, BF16, I32, U8 = (mybir.dt.float32, mybir.dt.float32r, mybir.dt.bfloat16, mybir.dt.int32, mybir.dt.uint8)
ACT, ALU, AX = mybir.ActivationFunctionType, mybir.AluOpType, mybir.AxisListType

P = 128
D = 1024
L = 1024
NT = L // P
KD = D // P
HALF = 512
H, HD = 8, 64
ROT = HD // 4
NF = ROT // 2
THETA = 500000.0
TOPK = min(256, L // 4)
FREE_BLOCKS = TOPK // P
NSEL = NT - FREE_BLOCKS
EPS = 1e-6
GROUPS = 4
KA = 512 // P
CW = 256
IDX_SCALE = float(H ** -0.5 * HD ** -0.5)
ATT_SCALE = float(HD ** -0.5)
MAGIC = 12582912.0
TWO_PI = (6.28125, 0.0019340515136718750, 1.2556416e-06)
MASKED = -3.0e38
NEG_BIAS = -1.0e30

O_UA, O_ZA, O_Q, O_K, O_V, O_ZB, O_QI, O_KI, O_WI, O_GA, O_GB = (
    0, 512, 1024, 1536, 1600, 1664, 2176, 2688, 2752, 2760, 3784)
KR_KI, KR_WI, KR_K, KR_V, KR_W = 0, 64, 72, 136, 200


def keys(b):
    return (b + 1) * P


def score_at(b):
    return P * sum(j + 1 for j in range(FREE_BLOCKS, b))


def bias_at(b):
    return P * sum(j + 1 for j in range(b))


def hybrid_layer(nc, x, c, positions, w_ada, b_ada, norm_gain, w_in, w_pool_group, pool_scale,
                 q_norm_gain, k_norm_gain, w_branch_a, w_branch_b, w_out, out):
    x, out = x[0], out[0]
    w_ada, w_in, w_group = w_ada[0], w_in[0], w_pool_group[0]
    w_branch_a, w_branch_b, w_out = w_branch_a[0], w_branch_b[0], w_out[0]

    def cols(src, first, kt=KD):
        return (kt, [(src, first, CW, 0)])
    chunks, name_of = [], {}

    def add(name, chunk):
        name_of[name] = len(chunks)
        chunks.append(chunk)
    for i in range(2):
        add(("qi", i), cols(w_in, O_QI + CW * i))
    add("kv", (KD, [(w_in, O_KI, KR_K, 0), (w_in, O_K, 2 * HD, KR_K)]))
    for i in range(2):
        add(("q", i), cols(w_in, O_Q + CW * i))
    for i in range(2):
        add(("zb", i), cols(w_in, O_ZB + CW * i))
    C_ORDER = [("ua", 0), ("gb", 0), ("gb", 1), ("ua", 1), ("gb", 2), ("gb", 3)]
    for kind, i in C_ORDER:
        add((kind, i), cols(w_in, (O_UA if kind == "ua" else O_GB) + CW * i))
    for i in range(2):
        add(("za", i), cols(w_in, O_ZA + CW * i))
    for i in range(4):
        add(("ga", i), cols(w_in, O_GA + CW * i))
    for i in range(4):
        add(("wa", i), cols(w_branch_a, CW * i, KA))
    for i in range(4):
        add(("wb", i), cols(w_branch_b, CW * i, KA))
    for i in range(4):
        add(("wo", i), cols(w_out, CW * i))
    pieces = [(ci, p) for ci, (kt, _) in enumerate(chunks) for p in range(kt // 4)]
    pieces_through = [sum(k // 4 for k, _ in chunks[:ci + 1]) for ci in range(len(chunks))]
    RAW = 2
    raw_ready, got = [], [0] * RAW
    for n, (ci, _) in enumerate(pieces):
        got[n % RAW] += 16 * len(chunks[ci][1])
        raw_ready.append(got[n % RAW])

    WA_FIRST = 4
    WA_STEP = {4 * (n - WA_FIRST) + 3: n for n in range(WA_FIRST, 16)}
    MASK_UNIT = {11 + n: FREE_BLOCKS + n for n in range(NSEL)}
    assert max(MASK_UNIT) + 1 < 16 + WA_FIRST
    YB_STEP = dict(zip([48, 50, 52, 54, 56, 58, 61, 69], range(NT)))
    assert all(i >= max(H * b + 13, max(WA_STEP) + 1) for i, b in YB_STEP.items())
    assert len(YB_STEP) == NT and max(WA_STEP) < min(YB_STEP)

    pp_uses = []
    QI_ORDER = [(0, 4), (0, 5), (0, 6), (0, 7), (1, 4), (1, 5), (1, 6), (1, 7), (0, 2), (0, 3), (1, 2), (1, 3)]
    ALL_TILES = [4, 5, 6, 7, 0, 1, 2, 3]
    pp_uses += [("qi", i, t) for i, t in QI_ORDER]
    pp_uses += [("kv", 0, t) for t in ALL_TILES]
    for i in range(2):
        pp_uses += [("q", i, t) for t in range(NT)]
    for i in range(2):
        pp_uses += [("zb", i, t) for t in range(NT)]
    UNITS = [(m, f) for m in range(2) for f in range(2)]
    UNITS_B = [(i, m, f) for f in range(2) for i in range(2) for m in range(2)]
    UNITS_B += [(i, m, f) for i in range(2, 4) for f in range(2) for m in range(2)]
    WB_LAST = {max(n for n, unit in enumerate(UNITS_B) if unit[0] == i): i for i in range(4)}
    for kind, i in C_ORDER:
        pp_uses += [(kind, i, u) for u in range(4)]
    for i in range(2):
        for m in range(2):
            pp_uses += [("za", i, 2 * m), ("za", i, 2 * m + 1), ("mix", i, 2 * m), ("mix", i, 2 * m + 1)]
    for i in range(4):
        pp_uses += [("ga", i, u) for u in range(4)]
    PP_HT = len(pp_uses)
    pp_bank = [n % 2 for n in range(PP_HT)]
    pp_uses += [("wa", i, u) for i in range(4) for u in range(4)]
    pp_bank += [n % 2 if n < WA_FIRST else 1 for n in range(16)]
    HEADS = NT * H
    for i in range(HEADS + 6):
        if 0 <= i - 4 < HEADS:
            pp_uses.append(("pv", i - 4))
            pp_bank.append(0)
        if YB_STEP.get(i, NT - 1) < NT - 1:
            pp_uses.append(("yb", YB_STEP[i]))
            pp_bank.append(1)
    pp_uses += [("wb", i, (m, f)) for i, m, f in UNITS_B]
    for i in range(4):
        pp_uses += [("wo", i, t) for t in range(NT)]
    pp_bank += [(n + 1) % 2 for n in range(len(pp_uses) - len(pp_bank))]
    pp_at = {use: n for n, use in enumerate(pp_uses)}
    pp_prev, pp_done, pp_sig = [], [], []
    last_in, na, nv, full = {}, 0, 0, 0
    for n, use in enumerate(pp_uses):
        pp_prev.append(last_in.get(pp_bank[n]))
        last_in[pp_bank[n]] = n
        by_act = n < PP_HT or use[0] in ("wa", "yb")
        by_dve = not by_act or use[0] == "yb"
        na, nv, full = na + by_act, nv + by_dve, full + (use[0] != "pv")
        pp_done.append((na if by_act else 0, nv if by_dve else 0))
        pp_sig.append(full)

    def chunk_done(ci):
        name = [k for k, v in name_of.items() if v == ci][0]
        kind, i = name if isinstance(name, tuple) else (name, 0)
        return max(pp_sig[n] for n, use in enumerate(pp_uses)
                   if use[:2] == (kind, i) or (kind == "za" and use[:2] == ("mix", i)))

    pt_uses = [("cols", "v"), ("gains", "v")]
    pt_uses += [(("h", n), "v") for n in range(2 * KD)]
    Q_EXTRA = {0: [("ki", 0, 0)], 1: [("ki", 0, 1)], 2: [("ki", 1, 0)], 3: [("ki", 1, 1)],
               4: [("qi", FREE_BLOCKS, 0)], 5: [("qi", FREE_BLOCKS, 1)],
               7: [("k", 0, 0)], 8: [("k", 0, 1), ("k", 1, 0), ("k", 1, 1)]}
    for t in Q_EXTRA:
        pt_uses += [(key, "a") for key in Q_EXTRA[t]]
    pt_uses += [(("qi", b, g), "a") for b in range(FREE_BLOCKS + 1, NT) for g in range(2)]
    pt_uses += [(("eqT", b), "a") for b in MASK_UNIT.values()]
    pt_uses += [(("qT", 0, g), "a") for g in range(2)]
    for i in range(HEADS + 6):
        if 0 <= i - 2 < HEADS:
            for g in range((keys((i - 2) // H) // P + 3) // 4):
                pt_uses.append((("PT", i - 2, g), "av"))
        if i % H == 4 and i // H + 1 < NT:
            pt_uses += [(("qT", i // H + 1, g), "a") for g in range(2)]
        if 0 <= i - 4 < HEADS and (i - 4) % 4 == 3:
            pt_uses.append((("out", (i - 4) // 4), "v"))
        if YB_STEP.get(i) == NT - 1:
            pt_uses.append((("yb", NT - 1), "av"))
    pt_uses += [(("gate", g), "a") for g in range(2)]
    pt_at, pt_done, na, nv = {}, [], 0, 0
    for n, (key, who) in enumerate(pt_uses):
        pt_at[key] = n
        na += "a" in who
        nv += "v" in who
        pt_done.append((na if "a" in who else 0, nv if "v" in who else 0))

    ps_uses = [("ada", "v")]
    ps_uses += [(("idx", b, h), "a") for b in range(FREE_BLOCKS, NT) for h in range(H)]
    ps_uses += [(("cum", b), "v") for b in MASK_UNIT.values()]
    ps_uses += [(("S", i), "v") for i in range(HEADS)]
    ps_at, ps_done, na, nv = {}, [], 0, 0
    for n, (key, who) in enumerate(ps_uses):
        ps_at[key] = n
        na += who == "a"
        nv += who == "v"
        ps_done.append((na if who == "a" else 0, nv if who == "v" else 0))

    def ps_value(key):
        return ps_at[key] + 4

    with ExitStack() as ctx:
        def alloc(stack, name, shape, dt=F32):
            return stack.enter_context(nc.sbuf_tensor(name, shape, dt))

        def sb(name, shape, dt=F32):
            return alloc(ctx, name, shape, dt)

        def sem(name):
            return ctx.enter_context(nc.semaphore(name))

        ident = sb("ident", [P, P])
        fold = sb("fold", [P, HD])
        ident_b = sb("ident_b", [P, P], BF16)
        prefix = sb("prefix", [P, L], BF16)
        diag_bias = sb("diag_bias", [P, P], BF16)
        ident_r = sb("ident_r", [P, P], F32R)
        ones = sb("ones", [P, P])
        col = sb("col", [P, 28])
        pos_col = sb("pos_col", [P, NT])
        gains = sb("gains", [P, 2 * HD])
        c_col = sb("c_col", [P, KD])
        c_silu = sb("c_silu", [P, KD])
        shift = sb("shift", [P, 2 * KD])
        gmul = sb("gmul", [P, KD])
        rot_c = sb("rot_c", [P, NT, ROT])
        rot_s = sb("rot_s", [P, NT, ROT])
        ssx, rx, nx = sb("ssx", [P, NT]), sb("rx", [P, NT]), sb("nx", [P, NT])
        ssq, rq, nq = sb("ssq", [P, NT * H]), sb("rq", [P, NT * H]), sb("nq", [P, NT * H])
        ssk, rk, nk = sb("ssk", [P, NT]), sb("rk", [P, NT]), sb("nk", [P, NT])
        w_idx = sb("w_idx", [P, NT, H])
        rope_a, rope_b = sb("rope_a", [P, H, ROT]), sb("rope_b", [P, H, ROT])
        recip_n = sb("recip_n", [P, 16])
        wg_hi, wg_lo = sb("wg_hi", [P, GROUPS, P], F32R), sb("wg_lo", [P, GROUPS, P], F32R)
        cnt, thr = sb("cnt", [P, NSEL]), sb("thr", [P, NSEL], I32)
        cand, accept = sb("cand", [P, NSEL], I32), sb("accept", [P, NSEL], I32)
        bit_i, bit_f = sb("bit_i", [P, 32], I32), sb("bit_f", [P, 32])
        need = sb("need", [P, 2])
        neg_max, row_sum, row_inv = sb("neg_max", [P, 2]), sb("row_sum", [P, 2 * H]), sb("row_inv", [P, 4])
        kT = sb("kT", [P, 2, L], F32R)
        v2 = sb("v2", [P, NT, 2 * HD], F32R)
        w_raw = sb("w_raw", [P, RAW, 4, CW])
        w_hi, w_lo = sb("w_hi", [P, 2, KD, CW], F32R), sb("w_lo", [P, 2, KD, CW], F32R)

        def zone(kib, *tenants):
            got = []
            for tenant in tenants:
                with ExitStack() as s:
                    got.append(tenant(s))
            sb(f"zone_{kib}".replace(".", "_"), [P, int(kib * 256)])
            return got

        ada_w, (hT_hi, hT_lo), att, (mT_hi, mT_lo) = zone(
            64,
            lambda s: alloc(s, "ada_w", [P, 4, KD, HALF]),
            lambda s: (alloc(s, "hT_hi", [P, KD, L], F32R), alloc(s, "hT_lo", [P, KD, L], F32R)),
            lambda s: dict(
                q_row=alloc(s, "q_row", [P, 2, H * HD]), z_row=alloc(s, "z_row", [P, 2, H * HD]),
                q_stk=alloc(s, "q_stk", [P, 2, H, 2 * HD], F32R), qT=alloc(s, "qT", [P, 2, H, P], F32R),
                logit=alloc(s, "logit", [P, 2, L]), prob=alloc(s, "prob", [P, 2, L]),
                pT=alloc(s, "pT", [P, 2, NT, 2, P], F32R), oT=alloc(s, "oT", [P, 8, P])),
            lambda s: (alloc(s, "mT_hi", [P, KD, L], F32R), alloc(s, "mT_lo", [P, KD, L], F32R)))
        def tenants_start(s):
            return (alloc(s, "h_raw", [P, 4, HALF]), alloc(s, "wg_raw", [P, GROUPS, P]),
                    alloc(s, "col_rows", [28, P]),
                    alloc(s, "pos_i", [NT, P], I32), alloc(s, "pos_f", [NT, P]), alloc(s, "gain_row", [1, 2 * HD]),
                    alloc(s, "angle", [P, NT, NF]), alloc(s, "turns", [P, 2, NT * NF]),
                    alloc(s, "reduced", [P, 2, NT * NF]), alloc(s, "trig", [P, 2, NT * NF]))
        (h_raw, wg_raw, col_rows, pos_i, pos_f, gain_row, angle, turns, reduced, trig), score, y_row, gate_w = zone(
            16.5, tenants_start,
            lambda s: alloc(s, "score", [P, score_at(NT)]),
            lambda s: alloc(s, "y_row", [P, NT, H * HD]),
            lambda s: alloc(s, "gate_w", [P, KD, HALF]))

        def tenants_first(s):
            return alloc(s, "x_in", [P, NT, D]), alloc(s, "ada_acc", [P, 4, HALF])

        def tenants_a(s):
            q = alloc(s, "q_all", [P, NT, H * HD])
            kiT = alloc(s, "kiT", [P, 2, L], F32R)
            qi_stk = alloc(s, "qi_stk", [P, H, 2 * HD], F32R)
            qiT = alloc(s, "qiT", [P, 2, H, P], F32R)
            qi = alloc(s, "qi", [P, NSEL, H * HD])
            with ExitStack() as k:
                kr, kst = alloc(k, "kr", [P, NT, KR_W]), alloc(k, "kst", [P, 2, NT, P], F32R)
            with ExitStack() as k:
                rel, zb_out = alloc(k, "rel", [P, 2, L]), alloc(k, "zb_out", [P, 4, CW])
            return q, qi, kiT, qi_stk, qiT, kr, kst, rel, zb_out

        def tenants_c(s):
            yT_hi, yT_lo = alloc(s, "yT_hi", [P, KA, L], F32R), alloc(s, "yT_lo", [P, KA, L], F32R)
            with ExitStack() as k:
                ua, win = alloc(k, "ua", [P, 2, L]), alloc(k, "win", [P, 2, L])
            with ExitStack() as k:
                z_silu, mixed = alloc(k, "z_silu", [P, 2, L]), alloc(k, "mixed", [P, 2, HALF])
            with ExitStack() as k:
                bias, a_out = alloc(k, "bias", [P, bias_at(NT)], BF16), alloc(k, "a_out", [P, 2, HALF])
                eqT1 = alloc(k, "eqT1", [P, L], BF16)
            with ExitStack() as k:
                e_in = alloc(k, "e_in", [P, 2, 4, HALF])
            with ExitStack() as k:
                x_row, o_row = alloc(k, "x_row", [P, 4, CW]), alloc(k, "o_row", [P, 4, CW])
            alloc(s, "zone_c", [P, 16 * 256])
            with ExitStack() as k:
                stage = alloc(k, "stage", [P, 4, HALF])
            with ExitStack() as k:
                m_raw = alloc(k, "m_raw", [P, 4, HALF])
            alloc(s, "zone_s", [P, 8 * 256])
            with ExitStack() as k:
                junk = alloc(k, "junk", [P, 2, L], U8)
            with ExitStack() as k:
                eq, eqT0 = alloc(k, "eq", [P, 2, L], BF16), alloc(k, "eqT0", [P, L], BF16)
            with ExitStack() as k:
                gate, gate_acc = alloc(k, "gate", [P, D]), alloc(k, "gate_acc", [P, HALF])
            alloc(s, "zone_m", [P, 6 * 256])
            return (yT_hi, yT_lo, ua, win, z_silu, mixed, bias, a_out, e_in, stage, eq, (eqT0, eqT1), m_raw, junk,
                    gate, gate_acc, x_row, o_row)

        (x_in, ada_acc), ta, tc = zone(62.5, tenants_first, tenants_a, tenants_c)
        q_all, qi, kiT, qi_stk, qiT, kr, kst, rel, zb_out = ta
        (yT_hi, yT_lo, ua, win, z_silu, mixed, bias, a_out, e_in, stage, eq, eqT, m_raw, junk,
         gate, gate_acc, x_row, o_row) = tc
        q_row, z_row, q_stk, qT = att["q_row"], att["z_row"], att["q_stk"], att["qT"]
        logit, prob, pT, oT = att["logit"], att["prob"], att["pT"], att["oT"]

        pp = [ctx.enter_context(nc.psum_tensor(f"pp{i}", [P, 512], F32)) for i in range(2)]
        pt = [ctx.enter_context(nc.psum_tensor(f"pt{i}", [P, 512], F32)) for i in range(2)]
        ps = [ctx.enter_context(nc.psum_tensor(f"ps{i}", [P, 1024], F32)) for i in range(2)]

        q_dram = nc.dram_tensor("q_spill", [L, H * HD], F32).ap()
        zb_dram = nc.dram_tensor("zb_spill", [L, H * HD], F32).ap()
        sga_dram = nc.dram_tensor("sga_spill", [D, L], F32).ap()
        sgb_dram = nc.dram_tensor("sgb_spill", [D, L], F32).ap()
        ma_dram = nc.dram_tensor("ma_spill", [D, L], F32).ap()

        c_in, cols_in, rows_in, group_in = sem("c_in"), sem("cols_in"), sem("rows_in"), sem("group_in")
        x_tile_in = [sem(f"x_tile_in{t}") for t in range(NT)]
        ada_in = [sem(f"ada_in{i}") for i in range(8)]
        raw_in = [sem(f"raw_in{i}") for i in range(RAW)]
        consts = sem("consts")
        dve_ready = sem("dve_ready")
        w_hi_done, w_lo_done = sem("w_hi_done"), sem("w_lo_done")
        pp_full, pp_free_a, pp_free_v = sem("pp_full"), sem("pp_free_a"), sem("pp_free_v")
        pt_full, pt_free_a, pt_free_v = sem("pt_full"), sem("pt_free_a"), sem("pt_free_v")
        ps_full, ps_free_a, ps_free_v = sem("ps_full"), sem("ps_free_a"), sem("ps_free_v")
        ada_sum_p, ada_sum = sem("ada_sum_p"), sem("ada_sum")
        c_silu_done, ssx_done, sqrt_done, trig_done = sem("c_silu_done"), sem("ssx_done"), sem("sqrt_done"), sem("trig_done")
        xn_done, h_raw_done = sem("xn_done"), sem("h_raw_done")
        hT_hi_done, hT_lo_v, hT_lo_p = sem("hT_hi_done"), sem("hT_lo_v"), sem("hT_lo_p")
        wg_hi_done, wg_lo_done = sem("wg_hi_done"), sem("wg_lo_done")
        qi_roped, kst_ready = sem("qi_roped"), sem("kst_ready")
        var_ready = sem("var_ready")
        q_scaled, q_roped = sem("q_scaled"), sem("q_roped")
        q_spilled, zb_spilled = sem("q_spilled"), [sem(f"zb_spilled{i}") for i in range(4)]
        qi_hi, qi_lo = sem("qi_hi"), sem("qi_lo")
        rel_used, block_scored, masked = sem("rel_used"), sem("block_scored"), sem("masked")
        silu_b = sem("silu_b")
        sel_done, bisected = sem("sel_done"), sem("bisected")
        pooled, pooled_hi, ua_used, mixed_used = sem("pooled"), sem("pooled_hi"), sem("ua_used"), sem("mixed_used")
        ya_hi, ya_lo, ya_done = sem("ya_hi"), sem("ya_lo"), sem("ya_done")
        stage_full, ma_full = sem("stage_full"), sem("ma_full")
        sg_out, sga_in = [sem(f"sg_out{i}") for i in range(4)], [sem(f"sga_in{i}") for i in range(4)]
        ma_out = [sem(f"ma_out{i}") for i in range(4)]
        q_in, z_in = [sem(f"q_in{i}") for i in range(2)], [sem(f"z_in{i}") for i in range(2)]
        stk_hi, stk_lo = sem("stk_hi"), sem("stk_lo")
        gate_sum, gate_in = sem("gate_sum"), sem("gate_in")
        eq_ready, bias_ready = sem("eq_ready"), sem("bias_ready")
        logit_done, prob_done = sem("logit_done"), sem("prob_done")
        pT_read, pv_done = sem("pT_read"), sem("pv_done")
        o_sum, y_done = sem("o_sum"), sem("y_done")
        e_loaded = [sem(f"e_loaded{i}") for i in range(4)]
        m_raw_done, mT_hi_done, mT_lo_done = sem("m_raw_done"), sem("mT_hi_done"), sem("mT_lo_done")
        x_row_in, o_row_done = [sem(f"x_row_in{i}") for i in range(4)], sem("o_row_done")
        stored = [sem(f"stored{i}") for i in range(4)]
        block = ctx.enter_context(nc.Block())

        def wait_done(eng, done, sem_a, sem_v):
            if done[0]:
                eng.wait_ge(sem_a, done[0])
            if done[1]:
                eng.wait_ge(sem_v, done[1])

        V_POS, V_COL, V_SIN = 1, 2, 3
        V_MEAN, V_RSQRT = {1: 4, 0: 6}, {1: 5, 0: 7}

        @block.sync
        def _(sp):
            sp.dma_start(c_col[:], c.rearrange("a (p k) -> p (a k)", k=KD)).then_inc(c_in, 16)
            sp.dma_start(col_rows[0:8, :], norm_gain.rearrange("a (r p) -> (a r) p", p=P)).then_inc(cols_in, 16)
            sp.dma_start(col_rows[8:12, :], pool_scale.rearrange("a (r p) -> (a r) p", p=P)).then_inc(cols_in, 16)
            sp.dma_start(col_rows[12:28, :], b_ada[:, 0:2 * D].rearrange("a (r p) -> (a r) p", p=P)).then_inc(cols_in, 16)
            sp.dma_start(pos_i[:], positions.rearrange("a (r p) -> (a r) p", p=P)).then_inc(cols_in, 16)
            sp.dma_start(gain_row[:, 0:HD], q_norm_gain).then_inc(rows_in, 16)
            sp.dma_start(gain_row[:, HD:2 * HD], k_norm_gain).then_inc(rows_in, 16)
            ada = w_ada.rearrange("(p k) n -> p k n", k=KD)
            for i in range(4):
                for j in range(2):
                    ks = slice(j * KD // 2, (j + 1) * KD // 2)
                    sp.dma_start(ada_w[:, i, ks], ada[:, ks, i * HALF:(i + 1) * HALF]).then_inc(ada_in[2 * i + j], 16)
            for t in range(NT // 2):
                sp.dma_start(x_in[:, t, :], x[t * P:(t + 1) * P, :]).then_inc(x_tile_in[t], 16)
            sp.dma_start(wg_raw[:], w_group.rearrange("g c d -> c g d")).then_inc(group_in, 16)
            for n, (ci, p) in enumerate(pieces):
                if n >= RAW:
                    sp.wait_ge(w_lo_done, n - RAW + 1)
                for src, first, width, to in chunks[ci][1]:
                    view = src.rearrange("(k p) n -> p k n", p=P)
                    sp.dma_start(w_raw[:, n % RAW, :, to:to + width],
                                 view[:, 4 * p:4 * p + 4, first:first + width]).then_inc(raw_in[n % RAW], 16)

        def split_chunk_hi(act, ci):
            if ci >= len(chunks):
                return
            if ci >= 2:
                act.wait_ge(pp_full, chunk_done(ci - 2))
            for n, (cj, p) in enumerate(pieces):
                if cj == ci:
                    width = sum(w for _, _, w, _ in chunks[ci][1])
                    act.wait_ge(raw_in[n % RAW], raw_ready[n])
                    nc.scalar.activation(w_hi[:, ci % 2, 4 * p:4 * p + 4, 0:width], w_raw[:, n % RAW, :, 0:width],
                                         ACT.Copy).then_inc(w_hi_done, 1)

        def split_chunk_lo(pool, ci):
            if ci >= len(chunks):
                return
            for n, (cj, p) in enumerate(pieces):
                if cj == ci:
                    width = sum(w for _, _, w, _ in chunks[ci][1])
                    pool.wait_ge(w_hi_done, n + 1)
                    nc.gpsimd.tensor_tensor(w_lo[:, ci % 2, 4 * p:4 * p + 4, 0:width], w_raw[:, n % RAW, :, 0:width],
                                            w_hi[:, ci % 2, 4 * p:4 * p + 4, 0:width].bitcast(F32),
                                            ALU.subtract).then_inc(w_lo_done, 1)

        SCALED = {b: {3: 2 * n, 6: 2 * n + 1} if n < 2 else {1: 2 + n} for n, b in enumerate(range(FREE_BLOCKS, NT))}

        POOLED_ROUND = {("gb", 1, 0): 0, ("ua", 1, 1): 1, ("gb", 2, 1): 2, ("gb", 3, 1): 3}

        WB_AFTER = {HEADS + i: n for i, n in enumerate([1, 3, 0, 1, 3])}
        assert sum(WB_AFTER.values()) == 2 * KA
        H_AFTER = {n: KD + 2 * (n - 1) for n in range(1, 5)}
        GATE_LOADS = 5
        GATE_UNIT = NT + 5

        zb_after = {(b, h): 2 if b in (FREE_BLOCKS, NT - 1) else 3 for b in range(FREE_BLOCKS, NT) for h in range(H)}
        assert sum(zb_after.values()) == 2 * NT * KD

        @block.tensor
        def _(pe):
            def pp_claim(use):
                n = pp_at[use]
                if pp_prev[n] is not None:
                    wait_done(pe, pp_done[pp_prev[n]], pp_free_a, pp_free_v)
                return pp[pp_bank[n]]

            def pt_claim(key):
                n = pt_at[key]
                if n >= 2:
                    wait_done(pe, pt_done[n - 2], pt_free_a, pt_free_v)
                return pt[n % 2]

            def ps_claim(key):
                n = ps_at[key]
                if n >= 2:
                    wait_done(pe, ps_done[n - 2], ps_free_a, ps_free_v)
                return ps[n % 2]

            def product(o, a_hi, a_lo, b_hi, b_lo, first, last):
                nc.tensor.matmul(o, a_hi, b_hi, start=first, stop=False)
                nc.tensor.matmul(o, a_hi, b_lo, start=False, stop=False)
                return nc.tensor.matmul(o, a_lo, b_hi, start=False, stop=last)

            def rows_step(o, t, ci, k, width):
                s, tok = ci % 2, slice(t * P, (t + 1) * P)
                return product(o[:, 0:width], hT_hi[:, k, tok], hT_lo[:, k, tok],
                               w_hi[:, s, k, 0:width], w_lo[:, s, k, 0:width], k == 0, k == KD - 1)

            def channels(use, ci, m, f, act_hi, act_lo, kt):
                o = pp_claim(use)
                s, tok, ch = ci % 2, slice(f * HALF, (f + 1) * HALF), slice(m * P, (m + 1) * P)
                for k in range(kt):
                    last = product(o[:], w_hi[:, s, k, ch], w_lo[:, s, k, ch], act_hi[:, k, tok], act_lo[:, k, tok],
                                   k == 0, k == kt - 1)
                last.then_inc(pp_full, 1)

            def yb_transposes(b):
                pe.wait_ge(y_done, 2 * b + 2)
                o = pt_claim(("yb", b)) if b == NT - 1 else pp_claim(("yb", b))
                for j in range(4):
                    last = nc.tensor.transpose(o[:, j * P:(j + 1) * P], y_row[:, b, j * P:(j + 1) * P], ident[:])
                last.then_inc(pt_full if b == NT - 1 else pp_full, 1)

            pe.wait_ge(consts, 1)
            pe.wait_ge(dve_ready, V_POS)
            o = pt_claim("cols")
            nc.tensor.transpose(o[:, 0:28], col_rows[:], ident[0:28, 0:28])
            nc.tensor.transpose(o[:, 32:32 + NT], pos_f[:], ident[0:NT, 0:NT]).then_inc(pt_full, 1)
            pe.wait_ge(rows_in, 32)
            o = pt_claim("gains")
            nc.tensor.matmul(o[:, 0:2 * HD], ones[0:1, :], gain_row[:], start=True, stop=True).then_inc(pt_full, 1)
            def h_transposes(n):
                f, k = 1 - n // KD, n % KD
                if k == 0:
                    pe.wait_ge(xn_done, NT if f == 0 else NT // 2)
                o = pt_claim(("h", n))
                for j in range(4):
                    last = nc.tensor.transpose(o[:, j * P:(j + 1) * P], x_in[:, 4 * f + j, k * P:(k + 1) * P], ident[:])
                last.then_inc(pt_full, 1)
            for n in range(2):
                h_transposes(n)
            o = ps_claim("ada")
            for i in range(4):
                if i == 0:
                    pe.wait_ge(ada_sum_p, 1)
                else:
                    pe.wait_ge(ada_sum, i)
                summed = ada_acc[:, i] if i else ada_w[:, 0, 0]
                for j in range(4):
                    last = nc.tensor.matmul(o[:, 4 * i + j:4 * i + j + 1], summed[:, j * P:(j + 1) * P],
                                            ones[:, 0:1], start=True, stop=True)
                last.then_inc(ps_full, 1)
            for n in range(2, KD):
                h_transposes(n)

            def rows_chunk(kind, i, tiles, width):
                ci = name_of[(kind, i)] if kind != "kv" else name_of["kv"]
                pe.wait_ge(w_lo_done, pieces_through[ci])
                for t in tiles:
                    o = pp_claim((kind, i, t))
                    for k in range(KD):
                        last = rows_step(o, t, ci, k, width)
                    last.then_inc(pp_full, 1)
            for n, (i, t) in enumerate(QI_ORDER):
                ci = name_of[("qi", i)]
                if t == 4:
                    pe.wait_ge(w_lo_done, pieces_through[ci])
                if n == NT:
                    pe.wait_ge(hT_hi_done, 2 * KD)
                    pe.wait_ge(hT_lo_v, KD)
                    pe.wait_ge(hT_lo_p, KD)
                o = pp_claim(("qi", i, t))
                for k in range(KD):
                    if n == 0:
                        pe.wait_ge(hT_hi_done, k + 1)
                        pe.wait_ge(hT_lo_v, k // 2 + 1)
                        if k:
                            pe.wait_ge(hT_lo_p, (k + 1) // 2)
                    last = rows_step(o, t, ci, k, CW)
                last.then_inc(pp_full, 1)
                if n in H_AFTER:
                    h_transposes(H_AFTER[n])
                    h_transposes(H_AFTER[n] + 1)
            rows_chunk("kv", 0, ALL_TILES, KR_W)

            def key_transposes(kind, s, f):
                pe.wait_ge(kst_ready, 1 if kind == "ki" else 2)
                o = pt_claim((kind, s, f))
                for j in range(4):
                    last = nc.tensor.transpose(o[:, j * P:(j + 1) * P].bitcast(F32R), kst[:, s, 4 * f + j, :],
                                               ident_r[:])
                last.then_inc(pt_full, 1)
            rows_chunk("q", 0, range(NT), CW)

            def qi_transposes(b, groups=range(2)):
                n = b - FREE_BLOCKS
                pe.wait_ge(qi_hi, n + 1)
                pe.wait_ge(qi_lo, n + 1)
                for g in groups:
                    o = pt_claim(("qi", b, g))
                    for j in range(4):
                        last = nc.tensor.transpose(o[:, j * P:(j + 1) * P].bitcast(F32R), qi_stk[:, 4 * g + j, :],
                                                   ident_r[:])
                    last.then_inc(pt_full, 1)

            def two_pass(o, q, kt_, n):
                for a in range(0, n, 512):
                    z = min(a + 512, n)
                    nc.tensor.matmul(o[:, a:z], q, kt_[:, 0, a:z], start=True, stop=False)
                    last = nc.tensor.matmul(o[:, a:z], q, kt_[:, 1, a:z], start=False, stop=True)
                return last

            def zb_step(n):
                i, t, k = n // (NT * KD), n // KD % NT, n % KD
                ci = name_of[("zb", i)]
                if t == 0 and k == 0:
                    pe.wait_ge(w_lo_done, pieces_through[ci])
                o = pp_claim(("zb", i, t)) if k == 0 else pp[pp_bank[pp_at[("zb", i, t)]]]
                last = rows_step(o, t, ci, k, CW)
                if k == KD - 1:
                    last.then_inc(pp_full, 1)
            ci = name_of[("q", 1)]
            pe.wait_ge(w_lo_done, pieces_through[ci])
            for t in range(NT + 1):
                for key in Q_EXTRA.get(t, []):
                    if key[0] == "qi":
                        qi_transposes(FREE_BLOCKS, [key[2]])
                    else:
                        key_transposes(*key)
                if t < NT:
                    o = pp_claim(("q", 1, t))
                    for k in range(KD):
                        last = rows_step(o, t, ci, k, CW)
                    last.then_inc(pp_full, 1)
            step = 0
            for b in range(FREE_BLOCKS, NT):
                pe.wait_ge(pt_free_a, pt_done[pt_at[("qi", b, 1)]][0])
                for h in range(H):
                    o = ps_claim(("idx", b, h))
                    two_pass(o, qiT[:, b % 2, h, :], kiT, keys(b)).then_inc(ps_full, 1)
                    if h == 5 and b + 1 < NT:
                        qi_transposes(b + 1)
                    for _ in range(zb_after[(b, h)]):
                        zb_step(step)
                        step += 1

            def channel_chunk(kind, i):
                ci = name_of[(kind, i)]
                pe.wait_ge(w_lo_done, pieces_through[ci])
                for u, (m, f) in enumerate(UNITS):
                    channels((kind, i, u), ci, m, f, hT_hi, hT_lo, KD)
            for kind, i in C_ORDER:
                channel_chunk(kind, i)
            pe.wait_ge(wg_lo_done, 1)
            for i in range(2):
                ci = name_of[("za", i)]
                pe.wait_ge(w_lo_done, pieces_through[ci])
                for m in range(2):
                    g = 2 * i + m
                    for f in range(2):
                        channels(("za", i, 2 * m + f), ci, m, f, hT_hi, hT_lo, KD)
                    pe.wait_ge(pooled_hi, g + 1)
                    pe.wait_ge(pooled, g + 1)
                    for f in range(2):
                        tok = slice(f * HALF, (f + 1) * HALF)
                        o = pp_claim(("mix", i, 2 * m + f))
                        product(o[:], wg_hi[:, g, :], wg_lo[:, g, :], yT_hi[:, g, tok], yT_lo[:, g, tok],
                                True, True).then_inc(pp_full, 1)

            def tie_transposes(b):
                pe.wait_ge(eq_ready, b - FREE_BLOCKS + 1)
                o = pt_claim(("eqT", b))[:].bitcast(BF16)
                for j in range(b + 1):
                    last = nc.tensor.transpose(o[:, j * P:(j + 1) * P], eq[:, b % 2, j * P:(j + 1) * P], ident_b[:])
                last.then_inc(pt_full, 1)

            def tie_counts(b):
                pe.wait_ge(pt_free_a, pt_done[pt_at[("eqT", b)]][0])
                o = ps_claim(("cum", b))
                n = keys(b)
                for j in range(b + 1):
                    for a in range(0, n, 512):
                        z, lo = min(a + 512, n), max(a, j * P)
                        if lo < z:
                            last = nc.tensor.matmul(o[:, lo:z], eqT[b % 2][:, j * P:(j + 1) * P],
                                                    prefix[:, lo - j * P:z - j * P], start=(j == 0),
                                                    stop=(j == min(b, z // P - 1)))
                last.then_inc(ps_full, 1)

            def mask_products(u):
                if u in MASK_UNIT:
                    tie_transposes(MASK_UNIT[u])
                if u - 1 in MASK_UNIT:
                    tie_counts(MASK_UNIT[u - 1])
            for i in range(4):
                ci = name_of[("ga", i)]
                pe.wait_ge(w_lo_done, pieces_through[ci])
                for u, (m, f) in enumerate(UNITS):
                    channels(("ga", i, u), ci, m, f, hT_hi, hT_lo, KD)
                    mask_products(4 * i + u)

            def q_transposes(b):
                pe.wait_ge(stk_hi, b + 1)
                pe.wait_ge(stk_lo, b + 1)
                for g in range(2):
                    o = pt_claim(("qT", b, g))
                    for j in range(4):
                        last = nc.tensor.transpose(o[:, j * P:(j + 1) * P].bitcast(F32R), q_stk[:, b % 2, 4 * g + j, :],
                                                   ident_r[:])
                    last.then_inc(pt_full, 1)

            def branch_a(q):
                n, k = q // KA, q % KA
                i, u = n // 4, n % 4
                m, f = UNITS[u]
                ci = name_of[("wa", i)]
                if u == 0 and k == 0:
                    pe.wait_ge(w_lo_done, pieces_through[ci])
                o = pp_claim(("wa", i, u)) if k == 0 else pp[pp_bank[pp_at[("wa", i, u)]]]
                s, tok, ch = ci % 2, slice(f * HALF, (f + 1) * HALF), slice(m * P, (m + 1) * P)
                last = product(o[:], w_hi[:, s, k, ch], w_lo[:, s, k, ch], yT_hi[:, k, tok], yT_lo[:, k, tok],
                               k == 0, k == KA - 1)
                if k == KA - 1:
                    last.then_inc(pp_full, 1)
            pe.wait_ge(ya_hi, 2 * GROUPS)
            pe.wait_ge(ya_lo, 2 * GROUPS)
            for q in range(KA * WA_FIRST):
                branch_a(q)
                if q % KA == KA - 1:
                    mask_products(16 + q // KA)
                    if q // KA == WA_FIRST - 2:
                        q_transposes(0)

            def branch_b(q):
                n, k = q // KA, q % KA
                i, m, f = UNITS_B[n]
                ci = name_of[("wb", i)]
                if q == 0:
                    wait_done(pe, pp_done[pp_at[("yb", NT // 2 - 1)]], pp_free_a, pp_free_v)
                if k == 0 and f == 1:
                    wait_done(pe, pt_done[pt_at[("yb", NT - 1)]], pt_free_a, pt_free_v)
                if (m, f) == (0, 0) and k == 0:
                    pe.wait_ge(w_lo_done, pieces_through[ci])
                o = pp_claim(("wb", i, (m, f))) if k == 0 else pp[pp_bank[pp_at[("wb", i, (m, f))]]]
                s, tok, ch = ci % 2, slice(f * HALF, (f + 1) * HALF), slice(m * P, (m + 1) * P)
                last = product(o[:], w_hi[:, s, k, ch], w_lo[:, s, k, ch], yT_hi[:, k, tok], yT_lo[:, k, tok],
                               k == 0, k == KA - 1)
                if k == KA - 1:
                    last.then_inc(pp_full, 1)
            q_b = 0
            for i in range(HEADS + 6):
                if 0 <= i - 2 < HEADS:
                    j, b = i - 2, (i - 2) // H
                    pe.wait_ge(prob_done, j + 1)
                    for g in range((b + 4) // 4):
                        o = pt_claim(("PT", j, g))
                        for t in range(4 * g, min(4 * g + 4, b + 1)):
                            last = nc.tensor.transpose(o[:, (t % 4) * P:(t % 4 + 1) * P], prob[:, j % 2, t * P:(t + 1) * P],
                                                       ident[:])
                        last.then_inc(pt_full, 1)
                if i < HEADS:
                    b, h = i // H, i % H
                    if h == 0:
                        pe.wait_ge(pt_free_a, pt_done[pt_at[("qT", b, 1)]][0])
                    o = ps_claim(("S", i))
                    two_pass(o, qT[:, b % 2, h, :], kT, keys(b)).then_inc(ps_full, 1)
                if i < KA * (16 - WA_FIRST):
                    branch_a(KA * WA_FIRST + i)
                if 0 <= i - 3 < HEADS:
                    j, b = i - 3, (i - 3) // H
                    wait_done(pe, pt_done[pt_at[("PT", j, b // 4)]], pt_free_a, pt_free_v)
                    pp_claim(("pv", j))
                    for t in range(b + 1):
                        last = nc.tensor.matmul(pp[0][:, 0:2 * P], v2[:, t, :],
                                                pT[:, j % 2, t, :, :].rearrange("p s q -> p (s q)"),
                                                start=(t == 0), stop=(t == b))
                    last.then_inc(pv_done, 1)
                if i % H == 4 and i // H + 1 < NT:
                    q_transposes(i // H + 1)
                if 0 <= i - 4 < HEADS and (i - 4) % 4 == 3:
                    n = (i - 4) // 4
                    pe.wait_ge(pp_free_v, pp_done[pp_at[("pv", 4 * n + 3)]][1])
                    o = pt_claim(("out", n))
                    for h in range(4):
                        last = nc.tensor.matmul(o[:, h * HD:(h + 1) * HD], oT[:, (4 * n + h) % 8, :], fold[:],
                                                start=True, stop=True)
                    last.then_inc(pt_full, 1)
                for _ in range(WB_AFTER.get(i, 0)):
                    branch_b(q_b)
                    q_b += 1
                if i in YB_STEP:
                    yb_transposes(YB_STEP[i])

            def gate_rows(g):
                pe.wait_ge(gate_sum, g + 1)
                o = pt_claim(("gate", g))
                nc.tensor.matmul(o[:], ones[:], gate_acc[:], start=True, stop=True).then_inc(pt_full, 1)

            while q_b < 16 * KA:
                branch_b(q_b)
                q_b += 1
            gate_rows(0)
            pe.wait_ge(mT_hi_done, 14)
            pe.wait_ge(mT_lo_done, 14)
            for i in range(4):
                ci = name_of[("wo", i)]
                pe.wait_ge(w_lo_done, pieces_through[ci])
                for t in range(NT):
                    if i == 0 and t == NT // 2:
                        pe.wait_ge(mT_hi_done, 16)
                        pe.wait_ge(mT_lo_done, 16)
                    o = pp_claim(("wo", i, t))
                    tok = slice(t * P, (t + 1) * P)
                    for k in range(KD):
                        last = product(o[:, 0:CW], mT_hi[:, k, tok], mT_lo[:, k, tok], w_hi[:, ci % 2, k, :],
                                       w_lo[:, ci % 2, k, :], k == 0, k == KD - 1)
                    last.then_inc(pp_full, 1)
                    if NT * i + t == GATE_UNIT:
                        gate_rows(1)

        @block.scalar
        def _(act):
            for t in range(NT // 2, NT):
                act.dma_start(x_in[:, t, :], x[t * P:(t + 1) * P, :]).then_inc(x_tile_in[t], 16)
            act.wait_ge(consts, 1)
            nc.scalar.activation(ident_r[:], ident[:], ACT.Copy)
            act.wait_ge(c_in, 16)
            nc.scalar.activation(c_silu[:], c_col[:], ACT.Silu).then_inc(c_silu_done, 1)

            def square_half(f):
                for t in range(4 * f, 4 * f + 4):
                    act.wait_ge(x_tile_in[t], 16)
                    nc.scalar.activation(ps[1][:], x_in[:, t, :], ACT.Square, accum_out=ssx[:, t:t + 1]).then_inc(ssx_done, 1)
                    act.drain()

            def sqrt_half(f):
                act.wait_ge(dve_ready, V_MEAN[f])
                nc.scalar.activation(rx[:, 4 * f:4 * f + 4], ssx[:, 4 * f:4 * f + 4], ACT.Sqrt).then_inc(sqrt_done, 1)

            def scale_half(f):
                act.wait_ge(dve_ready, V_RSQRT[f])
                for t in range(4 * f, 4 * f + 4):
                    nc.scalar.activation(x_in[:, t, :], x_in[:, t, :], ACT.Copy, scale=rx[:, t:t + 1]).then_inc(xn_done, 1)
            square_half(1)
            sqrt_half(1)
            scale_half(1)
            nc.scalar.activation(trig[:], reduced[:], ACT.Sin).then_inc(trig_done, 1)
            square_half(0)
            split_chunk_hi(act, 0)

            def ht_hi(n):
                f, k = 1 - n // KD, n % KD
                act.wait_ge(h_raw_done, n + 1)
                nc.scalar.activation(hT_hi[:, k, f * HALF:(f + 1) * HALF], h_raw[:, n % 4, :],
                                     ACT.Copy).then_inc(hT_hi_done, 1)
            for n in range(KD):
                ht_hi(n)
                if n == 1:
                    sqrt_half(0)
            split_chunk_hi(act, 1)
            scale_half(0)

            def pp_take(use):
                act.wait_ge(pp_full, pp_sig[pp_at[use]])
                return pp[pp_bank[pp_at[use]]]

            def pt_take(key):
                act.wait_ge(pt_full, pt_at[key] + 1)
                return pt[pt_at[key] % 2]

            def pooled_round(g):
                act.wait_ge(ua_used, g + 1)
                nc.scalar.activation(yT_hi[:, g, :], win[:, 0, :], ACT.Copy).then_inc(pooled_hi, 1)

            def yb_hi(b):
                o = pt_take(("yb", b)) if b == NT - 1 else pp_take(("yb", b))
                nc.scalar.activation(yT_hi[:, :, b * P:(b + 1) * P], o[:].rearrange("p (k q) -> p k q", q=P),
                                     ACT.Copy).then_inc(pt_free_a if b == NT - 1 else pp_free_a, 1)

            for n, (i, t) in enumerate(QI_ORDER):
                o = pp_take(("qi", i, t))
                nc.scalar.activation(qi[:, t - FREE_BLOCKS, i * CW:(i + 1) * CW], o[:, 0:CW],
                                     ACT.Copy).then_inc(pp_free_a, 1)
                if n in H_AFTER:
                    ht_hi(H_AFTER[n])
                    ht_hi(H_AFTER[n] + 1)
                if n == 6:
                    act.wait_ge(group_in, 16)
                    nc.scalar.activation(wg_hi[:], wg_raw[:], ACT.Copy).then_inc(wg_hi_done, 1)
                if t == 3:
                    split_chunk_hi(act, name_of[("qi", i)] + 2)
            for t in ALL_TILES:
                o = pp_take(("kv", 0, t))
                nc.scalar.activation(kr[:, t, :], o[:, 0:KR_W], ACT.Copy).then_inc(pp_free_a, 1)
            split_chunk_hi(act, name_of["kv"] + 2)

            def q_tile(i, t):
                o = pp_take(("q", i, t))
                nc.scalar.activation(q_all[:, t, i * CW:(i + 1) * CW], o[:, 0:CW], ACT.Copy).then_inc(pp_free_a, 1)

            def key_copy(kind, s, f):
                to = kiT if kind == "ki" else kT
                o = pt_take((kind, s, f))
                nc.scalar.activation(to[:, s, f * HALF:(f + 1) * HALF], o[:], ACT.Copy).then_inc(pt_free_a, 1)
            for t in range(NT):
                q_tile(0, t)
            split_chunk_hi(act, name_of[("q", 0)] + 2)

            def qi_split_hi(b):
                n = b - FREE_BLOCKS
                act.wait_ge(qi_roped, n + 1)
                if n:
                    act.wait_ge(pt_full, pt_at[("qi", b - 1, 1)] + 1)
                nc.scalar.activation(qi_stk[:, :, 0:HD], qi[:, n, :].rearrange("p (h d) -> p h d", d=HD),
                                     ACT.Copy).then_inc(qi_hi, 1)

            def qi_copies(b, groups=range(2)):
                for g in groups:
                    o = pt_take(("qi", b, g))
                    nc.scalar.activation(qiT[:, b % 2, 4 * g:4 * g + 4, :].rearrange("p h q -> p (h q)"), o[:],
                                         ACT.Copy).then_inc(pt_free_a, 1)

            def zb_tile(i, t):
                s = (i * NT + t) % 4
                if i * NT + t >= 4:
                    act.wait_ge(zb_spilled[s], 16 * ((i * NT + t) // 4))
                o = pp_take(("zb", i, t))
                nc.scalar.activation(zb_out[:, s, :], o[:, 0:CW], ACT.Silu).then_inc(pp_free_a, 1)
                act.wait_ge(pp_free_a, pp_at[("zb", i, t)] + 1)
                act.dma_start(zb_dram[t * P:(t + 1) * P, i * CW:(i + 1) * CW], zb_out[:, s, :]).then_inc(zb_spilled[s], 16)
            qi_split_hi(FREE_BLOCKS)
            for t in range(NT + 1):
                for key in Q_EXTRA.get(t, []):
                    if key[0] == "qi":
                        qi_copies(FREE_BLOCKS, [key[2]])
                    else:
                        key_copy(*key)
                    if key == ("ki", 0, 0):
                        act.wait_ge(var_ready, 1)
                        nc.scalar.activation(rk[:], ssk[:], ACT.Sqrt).then_inc(sqrt_done, 1)
                if t < NT:
                    q_tile(1, t)
            split_chunk_hi(act, name_of[("q", 1)] + 2)
            step = 0
            for b in range(FREE_BLOCKS, NT):
                for h in range(H):
                    n = (b - FREE_BLOCKS) * H + h
                    if h == 0 and b + 1 < NT:
                        qi_split_hi(b + 1)
                    act.wait_ge(ps_full, ps_value(("idx", b, h)))
                    if n >= 2:
                        act.wait_ge(rel_used, n - 1)
                    nc.scalar.activation(rel[:, n % 2, 0:keys(b)], ps[ps_at[("idx", b, h)] % 2][:, 0:keys(b)],
                                         ACT.Relu).then_inc(ps_free_a, 1)
                    if (b, h) == (FREE_BLOCKS, 1):
                        act.wait_ge(var_ready, 2)
                        nc.scalar.activation(rq[:], ssq[:], ACT.Sqrt).then_inc(sqrt_done, 1)
                    if h == 5 and b + 1 < NT:
                        qi_copies(b + 1)
                    for _ in range(zb_after[(b, h)]):
                        step += 1
                        if step % KD == 0:
                            zb_tile((step // KD - 1) // NT, (step // KD - 1) % NT)
                            if step == NT * KD:
                                split_chunk_hi(act, name_of[("zb", 0)] + 2)
            split_chunk_hi(act, name_of[("zb", 1)] + 2)

            act.wait_ge(q_spilled, 16 * NT)
            act.wait_ge(rel_used, NSEL * H)
            for s in range(4):
                act.wait_ge(zb_spilled[s], 16 * 4)

            def stage_slot(n):
                if n >= 4:
                    act.wait_ge(sg_out[n % 4], 16 * (n // 4))
                return n % 4

            def gate_unit(kind, i, u):
                m, f = UNITS[u]
                s = stage_slot((16 if kind == "ga" else 0) + 4 * i + u)
                o = pp_take((kind, i, u))
                nc.scalar.activation(stage[:, s, :], o[:], ACT.Sigmoid).then_inc(pp_free_a, 1)
                act.wait_ge(pp_free_a, pp_done[pp_at[(kind, i, u)]][0])
                r = (2 * i + m) * P
                act.dma_start((sga_dram if kind == "ga" else sgb_dram)[r:r + P, f * HALF:(f + 1) * HALF],
                              stage[:, s, :]).then_inc(sg_out[s], 16)
            for kind, i in C_ORDER:
                for u, (m, f) in enumerate(UNITS):
                    if kind == "ua":
                        g = 2 * i + m
                        if g >= 2:
                            act.wait_ge(pooled, g - 1)
                        o = pp_take((kind, i, u))
                        nc.scalar.activation(ua[:, g % 2, f * HALF:(f + 1) * HALF], o[:], ACT.Copy).then_inc(pp_free_a, 1)
                    else:
                        gate_unit(kind, i, u)
                    if (kind, i, u) in POOLED_ROUND:
                        pooled_round(POOLED_ROUND[kind, i, u])
                split_chunk_hi(act, name_of[(kind, i)] + 2)

            def ya_round(n):
                g, f = n // 2, n % 2
                act.wait_ge(ya_done, n + 1)
                nc.scalar.activation(yT_hi[:, g, f * HALF:(f + 1) * HALF], z_silu[:, g % 2, f * HALF:(f + 1) * HALF],
                                     ACT.Copy).then_inc(ya_hi, 1)
            act.wait_ge(pooled, GROUPS)
            for i in range(2):
                for m in range(2):
                    g = 2 * i + m
                    if g >= 2:
                        ya_round(2 * (g - 2))
                        ya_round(2 * (g - 2) + 1)
                        act.wait_ge(ya_lo, 2 * (g - 1))
                        act.wait_ge(ya_hi, 2 * (g - 1))
                    for f in range(2):
                        o = pp_take(("za", i, 2 * m + f))
                        nc.scalar.activation(z_silu[:, g % 2, f * HALF:(f + 1) * HALF], o[:], ACT.Silu).then_inc(pp_free_a, 1)
                    for f in range(2):
                        n = 2 * g + f
                        if n >= 2:
                            act.wait_ge(ya_done, n - 1)
                        o = pp_take(("mix", i, 2 * m + f))
                        nc.scalar.activation(mixed[:, n % 2, :], o[:], ACT.Copy, scale=col[:, 8 + g:9 + g]).then_inc(pp_free_a, 1)
                split_chunk_hi(act, name_of[("za", i)] + 2)
            for n in range(4, 8):
                ya_round(n)

            def tie_copy(b):
                if b >= FREE_BLOCKS + 2:
                    act.wait_ge(ps_full, ps_value(("cum", b - 2)))
                o = pt_take(("eqT", b))[:].bitcast(BF16)
                nc.scalar.activation(eqT[b % 2][:, 0:keys(b)], o[:, 0:keys(b)], ACT.Copy).then_inc(pt_free_a, 1)
            for i in range(4):
                for u in range(4):
                    gate_unit("ga", i, u)
                    if 4 * i + u in MASK_UNIT:
                        tie_copy(MASK_UNIT[4 * i + u])
                split_chunk_hi(act, name_of[("ga", i)] + 2)

            def load_sga(n):
                i, u = n // 4, n % 4
                m, f = UNITS[u]
                r = (2 * i + m) * P
                if n >= 4:
                    act.wait_ge(ma_out[n % 4], 16 * (n // 4))
                else:
                    act.wait_ge(sg_out[n], 16 * 8)
                act.dma_start(stage[:, n % 4, :], sga_dram[r:r + P, f * HALF:(f + 1) * HALF]).then_inc(sga_in[n % 4], 16)

            def branch_a_copy(n):
                i, u = n // 4, n % 4
                if n >= 2:
                    act.wait_ge(ma_full, n - 1)
                o = pp_take(("wa", i, u))
                nc.scalar.activation(a_out[:, n % 2, :], o[:], ACT.Copy).then_inc(pp_free_a, 1)
                if 16 + n in MASK_UNIT:
                    tie_copy(MASK_UNIT[16 + n])
                if u == 3:
                    split_chunk_hi(act, name_of[("wa", i)] + 2)
                if 2 <= n < 14:
                    load_sga(n + 2)
            act.wait_ge(ya_lo, 8)
            act.wait_ge(ya_hi, 8)
            branch_a_copy(0)

            def load_e(n):
                i, m, f = UNITS_B[n]
                r = (2 * i + m) * P
                if n >= 4:
                    act.wait_ge(m_raw_done, n - 3)
                act.dma_start(e_in[:, 0, n % 4, :], sgb_dram[r:r + P, f * HALF:(f + 1) * HALF]).then_inc(e_loaded[n % 4], 16)
                act.dma_start(e_in[:, 1, n % 4, :], ma_dram[r:r + P, f * HALF:(f + 1) * HALF]).then_inc(e_loaded[n % 4], 16)

            def load_q(b):
                if b >= 2:
                    act.wait_ge(stk_lo, b - 1)
                act.dma_start(q_row[:, b % 2, :], q_dram[b * P:(b + 1) * P, :]).then_inc(q_in[b % 2], 16)

            def load_z(b):
                if b >= 2:
                    act.wait_ge(y_done, 2 * (b - 1))
                act.dma_start(z_row[:, b % 2, :], zb_dram[b * P:(b + 1) * P, :]).then_inc(z_in[b % 2], 16)

            def q_split_hi(b):
                act.wait_ge(q_in[b % 2], 16 * (b // 2 + 1))
                if b >= 2:
                    act.wait_ge(pt_full, pt_at[("qT", b - 2, 1)] + 1)
                nc.scalar.activation(q_stk[:, b % 2, :, 0:HD], q_row[:, b % 2, :].rearrange("p (h d) -> p h d", d=HD),
                                     ACT.Copy).then_inc(stk_hi, 1)

            def q_copies(b):
                for g in range(2):
                    o = pt_take(("qT", b, g))
                    nc.scalar.activation(qT[:, b % 2, 4 * g:4 * g + 4, :].rearrange("p h q -> p (h q)"), o[:],
                                         ACT.Copy).then_inc(pt_free_a, 1)

            def load_gate(g, j):
                if g and j == 0:
                    act.wait_ge(gate_sum, g)
                act.dma_start(gate_w[:, 2 * j:2 * j + 2], w_ada.rearrange("(p k) n -> p k n", k=KD)[
                    :, 2 * j:2 * j + 2, 2 * D + g * HALF:2 * D + (g + 1) * HALF]).then_inc(gate_in, 16)
                if j == 3:
                    act.dma_start(gate[0:1, g * HALF:(g + 1) * HALF],
                                  b_ada[:, 2 * D + g * HALF:2 * D + (g + 1) * HALF]).then_inc(gate_in, 16)
            act.wait_ge(pp_full, PP_HT)
            for b in range(2):
                load_q(b)
                load_z(b)
            for n in range(4):
                load_sga(n)
            q_split_hi(0)
            for n in range(1, WA_FIRST):
                branch_a_copy(n)
                if n == WA_FIRST - 2:
                    q_copies(0)
            for i in range(HEADS + 6):
                if 0 <= i - 2 < HEADS:
                    j, b = i - 2, (i - 2) // H
                    if j >= 2:
                        act.wait_ge(pv_done, j - 1)
                    for g in range((b + 4) // 4):
                        t0, t1 = 4 * g, min(4 * g + 4, b + 1)
                        o = pt_take(("PT", j, g))
                        nc.scalar.activation(pT[:, j % 2, t0:t1, 0, :], o[:, 0:(t1 - t0) * P].rearrange(
                            "p (t q) -> p t q", q=P), ACT.Copy).then_inc(pt_free_a, 1)
                if 0 <= i - 1 < HEADS:
                    j, b, h = i - 1, (i - 1) // H, (i - 1) % H
                    act.wait_ge(logit_done, j + 1)
                    if j >= 2:
                        act.wait_ge(pt_full, pt_at[("PT", j - 2, (j - 2) // H // 4)] + 1)
                    if h % 4 == 0 and b >= 2:
                        act.wait_ge(o_sum, 2 * (b - 1))
                    r = (b % 2) * H + h
                    nc.scalar.activation(prob[:, j % 2, 0:keys(b)], logit[:, j % 2, 0:keys(b)], ACT.Exp, scale=-1.0,
                                         bias=neg_max[:, j % 2:j % 2 + 1],
                                         accum_out=row_sum[:, r:r + 1]).then_inc(prob_done, 1)
                if i % H == 2 and i // H + 1 < NT:
                    q_split_hi(i // H + 1)
                if i % H == 4 and i // H + 1 < NT:
                    q_copies(i // H + 1)
                if i % H == 5 and i // H + 2 < NT:
                    load_q(i // H + 2)
                if i in WA_STEP:
                    branch_a_copy(WA_STEP[i])
                if i % H == 6 and 2 <= i // H + 1 < NT:
                    load_z(i // H + 1)
                if i in YB_STEP:
                    yb_hi(YB_STEP[i])
                if i == HEADS:
                    act.wait_ge(logit_done, HEADS)
                    act.wait_ge(ma_full, 16)
                    for s in range(4):
                        act.wait_ge(ma_out[s], 16 * 4)
                    for n in range(4):
                        load_e(n)

            def gate_copy(g):
                o = pt_take(("gate", g))
                nc.scalar.activation(gate[:, g * HALF:(g + 1) * HALF], o[:], ACT.Copy).then_inc(pt_free_a, 1)

            act.wait_ge(pt_full, pt_at[("yb", NT - 1)] + 1)
            act.wait_ge(pt_free_v, pt_done[pt_at[("yb", NT - 1)]][1])
            act.wait_ge(y_done, 2 * NT)
            for n in range(16):
                i, m, f = UNITS_B[n]
                if n in WB_LAST:
                    split_chunk_hi(act, name_of[("wb", WB_LAST[n])] + 2)
                act.wait_ge(m_raw_done, n + 1)
                nc.scalar.activation(mT_hi[:, 2 * i + m, f * HALF:(f + 1) * HALF], m_raw[:, n % 4, :],
                                     ACT.Copy).then_inc(mT_hi_done, 1)
                if n + 4 < 16:
                    load_e(n + 4)
                if n < 4:
                    load_gate(0, n)

            act.wait_ge(m_raw_done, 16)
            def load_x(n):
                i, t = n // NT, n % NT
                if n >= 4:
                    act.wait_ge(o_row_done, n - 3)
                act.dma_start(x_row[:, n % 4, :], x[t * P:(t + 1) * P, i * CW:(i + 1) * CW]).then_inc(x_row_in[n % 4], 16)
            for n in range(4):
                load_x(n)
            gate_copy(0)
            for n in range(4 * NT):
                i, t = n // NT, n % NT
                act.wait_ge(o_row_done, n + 1)
                act.dma_start(out[t * P:(t + 1) * P, i * CW:(i + 1) * CW], o_row[:, n % 4, :]).then_inc(stored[n % 4], 16)
                if n + 4 < 4 * NT:
                    load_x(n + 4)
                if n < 4:
                    load_gate(1, n)
                if n == GATE_UNIT:
                    gate_copy(1)
                if t == NT - 1:
                    split_chunk_hi(act, name_of[("wo", i)] + 2)
            for s in range(4):
                act.wait_ge(stored[s], 16 * NT)

        @block.gpsimd
        def _(pool):
            gp = nc.gpsimd
            gp.memset(ident[:], 0.0)
            gp.memset(ident_b[:], 0.0)
            gp.memset(fold[:], 0.0)
            gp.memset(prefix[:], 1.0)
            gp.memset(diag_bias[:], 0.0)
            gp.memset(ones[:], 1.0)
            for n in range(16):
                gp.memset(recip_n[:, n:n + 1], 1.0 / (n + 1))
            pool.drain()
            for m in (ident, ident_b):
                gp.affine_select(out=m[:], in_=m[:], compare_op=ALU.not_equal, fill=1.0, base=0,
                                 pattern=[[-1, P]], channel_multiplier=1)
            for base in (0, -HD):
                gp.affine_select(out=fold[:], in_=fold[:], compare_op=ALU.not_equal, fill=1.0, base=base,
                                 pattern=[[-1, HD]], channel_multiplier=1)
                pool.drain()
            gp.affine_select(out=prefix[:, 0:P], in_=prefix[:, 0:P], compare_op=ALU.is_ge, fill=0.0, base=0,
                             pattern=[[1, P]], channel_multiplier=-1)
            gp.affine_select(out=diag_bias[:], in_=diag_bias[:], compare_op=ALU.is_ge, fill=NEG_BIAS, base=0,
                             pattern=[[-1, P]], channel_multiplier=1)
            pool.drain()
            gp.memset(rope_a[:], 0.0).then_inc(consts, 1)

            pool.wait_ge(c_silu_done, 1)
            for j in range(2):
                pool.wait_ge(ada_in[j], 16)
                ks = slice(j * KD // 2, (j + 1) * KD // 2)
                gp.tensor_tensor(ada_w[:, 0, ks], ada_w[:, 0, ks],
                                 c_silu[:, ks].unsqueeze(2).to_broadcast([P, KD // 2, HALF]), ALU.mult)
            k = KD // 2
            while k:
                pool.drain()
                ins = gp.tensor_tensor(ada_w[:, 0, 0:k], ada_w[:, 0, 0:k], ada_w[:, 0, k:2 * k], ALU.add)
                k //= 2
            ins.then_inc(ada_sum_p, 1)

            def ht_lo(n):
                f, k = 1 - n // KD, n % KD
                pool.wait_ge(hT_hi_done, n + 1)
                tok = slice(f * HALF, (f + 1) * HALF)
                gp.tensor_tensor(hT_lo[:, k, tok], h_raw[:, n % 4, :], hT_hi[:, k, tok].bitcast(F32),
                                 ALU.subtract).then_inc(hT_lo_p, 1)
            split_chunk_lo(pool, 0)
            for n in range(1, KD, 2):
                ht_lo(n)
            split_chunk_lo(pool, 1)
            for n in range(KD + 1, 2 * KD, 2):
                ht_lo(n)
            pool.wait_ge(wg_hi_done, 1)
            gp.tensor_tensor(wg_lo[:], wg_raw[:], wg_hi[:].bitcast(F32), ALU.subtract).then_inc(wg_lo_done, 1)

            def rope(v, t):
                cc = rot_c[:, t, :].unsqueeze(1).to_broadcast([P, H, ROT])
                ss = rot_s[:, t, :].unsqueeze(1).to_broadcast([P, H, ROT])
                gp.tensor_tensor(rope_a[:], v[:, :, 0:ROT], cc, ALU.mult)
                gp.tensor_tensor(rope_b[:, :, 0:NF], v[:, :, NF:ROT], ss[:, :, 0:NF], ALU.mult)
                gp.tensor_tensor(rope_b[:, :, NF:ROT], v[:, :, 0:NF], ss[:, :, NF:ROT], ALU.mult)
                pool.drain()
                return gp.tensor_tensor(v[:, :, 0:ROT], rope_a[:], rope_b[:], ALU.add)

            def qi_split_lo(b):
                n = b - FREE_BLOCKS
                pool.wait_ge(qi_hi, n + 1)
                nc.gpsimd.tensor_tensor(qi_stk[:, :, HD:2 * HD], qi[:, n, :].rearrange("p (h d) -> p h d", d=HD),
                                        qi_stk[:, :, 0:HD].bitcast(F32), ALU.subtract).then_inc(qi_lo, 1)

            def ya_rest(n):
                g, f = n // 2, n % 2
                tok = slice(f * HALF, (f + 1) * HALF)
                pool.wait_ge(ya_hi, n + 1)
                nc.gpsimd.tensor_tensor(yT_lo[:, g, tok], z_silu[:, g % 2, tok], yT_hi[:, g, tok].bitcast(F32),
                                        ALU.subtract).then_inc(ya_lo, 1)

            pool.wait_ge(pp_free_a, pp_at[("qi", 0, 3)] + 1)
            split_chunk_lo(pool, 2)
            pool.wait_ge(trig_done, 2)
            for n in range(NSEL):
                t = n + FREE_BLOCKS
                pool.wait_ge(pp_free_a, pp_at[("qi", 1, 3)] + 1)
                rope(qi[:, n, :].rearrange("p (h d) -> p h d", d=HD), t).then_inc(qi_roped, 1)
                pool.wait_ge(qi_roped, n + 1)
                if n == 0:
                    split_chunk_lo(pool, 3)
            split_chunk_lo(pool, 4)
            split_chunk_lo(pool, 5)
            qi_split_lo(FREE_BLOCKS)

            def finish_query(t):
                pool.wait_ge(q_scaled, t + 1)
                rope(q_all[:, t, :].rearrange("p (h d) -> p h d", d=HD), t).then_inc(q_roped, 1)
                pool.wait_ge(q_roped, t + 1)
                pool.dma_start(q_dram[t * P:(t + 1) * P, :], q_all[:, t, :]).then_inc(q_spilled, 16)

            def causal_scores(b):
                pool.wait_ge(block_scored, b - FREE_BLOCKS + 1)
                own = slice(score_at(b) + b * P, score_at(b) + (b + 1) * P)
                gp.affine_select(out=score[:, own], in_=score[:, own], compare_op=ALU.is_ge, fill=MASKED, base=0,
                                 pattern=[[-1, P]], channel_multiplier=1).then_inc(masked, 1)
            for b in range(FREE_BLOCKS, NT):
                if b + 1 < NT:
                    qi_split_lo(b + 1)
                if b == FREE_BLOCKS + 1:
                    split_chunk_lo(pool, 6)
                for t in SCALED[b].values():
                    finish_query(t)
                if b > FREE_BLOCKS:
                    causal_scores(b - 1)
                if b == 5:
                    split_chunk_lo(pool, 7)
            causal_scores(NT - 1)
            split_chunk_lo(pool, 8)

            pool.wait_ge(q_spilled, 16 * NT)
            for s in range(4):
                pool.wait_ge(zb_spilled[s], 16 * 4)

            def window_mean(g):
                w = 2 << g
                pool.wait_ge(pp_free_a, pp_at[("ua", g // 2, 2 * (g % 2) + 1)] + 1)
                if g:
                    pool.wait_ge(pooled, g)
                cur, s, side = ua[:, g % 2, :], 1, 0
                while s < w:
                    nxt = win[:, side, :]
                    gp.tensor_copy(nxt[:, 0:s], cur[:, 0:s])
                    gp.tensor_tensor(nxt[:, s:L], cur[:, s:L], cur[:, 0:L - s], ALU.add)
                    pool.drain()
                    cur, s, side = nxt, 2 * s, 1 - side
                other = win[:, side, :]
                gp.tensor_scalar(other[:, w:L], cur[:, w:L], 1.0 / w, None, ALU.mult)
                gp.tensor_tensor(other[:, 0:w], cur[:, 0:w], recip_n[:, 0:w], ALU.mult)
                pool.drain()
                gp.tensor_tensor(win[:, 0, :], other, ua[:, g % 2, :], ALU.subtract).then_inc(ua_used, 1)

            def pooled_low(g):
                pool.wait_ge(pooled_hi, g + 1)
                gp.tensor_tensor(yT_lo[:, g, :], win[:, 0, :], yT_hi[:, g, :].bitcast(F32), ALU.subtract).then_inc(pooled, 1)
            split_chunk_lo(pool, name_of["ua", 0] + 2)
            window_mean(0)
            split_chunk_lo(pool, name_of["gb", 0] + 2)
            pooled_low(0)
            window_mean(1)
            split_chunk_lo(pool, name_of["gb", 1] + 2)
            pooled_low(1)
            window_mean(2)
            split_chunk_lo(pool, name_of["ua", 1] + 2)
            pooled_low(2)
            window_mean(3)
            split_chunk_lo(pool, name_of["gb", 2] + 2)
            pooled_low(3)
            split_chunk_lo(pool, name_of["gb", 3] + 2)
            for n in range(2 * GROUPS):
                g, f = n // 2, n % 2
                tok = slice(f * HALF, (f + 1) * HALF)
                pool.wait_ge(pp_free_a, pp_at[("mix", g // 2, 2 * (g % 2) + f)] + 1)
                gp.tensor_tensor(z_silu[:, g % 2, tok], mixed[:, n % 2, :], z_silu[:, g % 2, tok], ALU.mult).then_inc(ya_done, 1)
                if n >= 2:
                    ya_rest(n - 2)
                if n % 4 == 3:
                    split_chunk_lo(pool, name_of[("za", n // 4)] + 2)
            ya_rest(2 * GROUPS - 2)
            ya_rest(2 * GROUPS - 1)
            for i in range(4):
                split_chunk_lo(pool, name_of[("ga", i)] + 2)

            def q_split_lo(b):
                pool.wait_ge(stk_hi, b + 1)
                gp.tensor_tensor(q_stk[:, b % 2, :, HD:2 * HD], q_row[:, b % 2, :].rearrange("p (h d) -> p h d", d=HD),
                                 q_stk[:, b % 2, :, 0:HD].bitcast(F32), ALU.subtract).then_inc(stk_lo, 1)

            def gated_a(n):
                i, u = n // 4, n % 4
                m, f = UNITS[u]
                r = (2 * i + m) * P
                pool.wait_ge(pp_free_a, pp_done[pp_at[("wa", i, u)]][0])
                pool.wait_ge(sga_in[n % 4], 16 * (n // 4 + 1))
                gp.tensor_tensor(stage[:, n % 4, :], a_out[:, n % 2, :], stage[:, n % 4, :], ALU.mult).then_inc(ma_full, 1)
                pool.wait_ge(ma_full, n + 1)
                pool.dma_start(ma_dram[r:r + P, f * HALF:(f + 1) * HALF], stage[:, n % 4, :]).then_inc(ma_out[n % 4], 16)
                if u == 3:
                    split_chunk_lo(pool, name_of[("wa", i)] + 2)
            q_split_lo(0)
            for n in range(WA_FIRST):
                gated_a(n)
            for i in range(HEADS + 6):
                if i % H == 2 and i // H + 1 < NT:
                    q_split_lo(i // H + 1)
                if i in WA_STEP:
                    gated_a(WA_STEP[i])
                if 0 <= i - 5 < HEADS and (i - 5) % 4 == 3:
                    n = (i - 5) // 4
                    b, f = n // 2, n % 2
                    pool.wait_ge(o_sum, n + 1)
                    pool.wait_ge(z_in[b % 2], 16 * (b // 2 + 1))
                    y = y_row[:, b, 4 * f * HD:4 * (f + 1) * HD]
                    gp.tensor_tensor(y, y, z_row[:, b % 2, 4 * f * HD:4 * (f + 1) * HD], ALU.mult).then_inc(y_done, 1)
            pool.wait_ge(pt_full, pt_at[("yb", NT - 1)] + 1)
            pool.wait_ge(pt_free_v, pt_done[pt_at[("yb", NT - 1)]][1])
            for n in range(16):
                i, m, f = UNITS_B[n]
                tok = slice(f * HALF, (f + 1) * HALF)
                if n in WB_LAST:
                    split_chunk_lo(pool, name_of[("wb", WB_LAST[n])] + 2)
                pool.wait_ge(mT_hi_done, n + 1)
                gp.tensor_tensor(mT_lo[:, 2 * i + m, tok], m_raw[:, n % 4, :], mT_hi[:, 2 * i + m, tok].bitcast(F32),
                                 ALU.subtract).then_inc(mT_lo_done, 1)
            for i in range(4):
                split_chunk_lo(pool, name_of[("wo", i)] + 2)

        @block.vector
        def _(dve):
            v = nc.vector
            for k in range(31):
                v.memset(bit_i[:, k:k + 1], 1 << (30 - k))
                v.memset(bit_f[:, k:k + 1], float(1 << (30 - k)))
            v.memset(bit_i[:, 31:32], 0)
            v.memset(bit_f[:, 31:32], 0.0)
            dve.wait_ge(cols_in, 64)
            v.tensor_copy(pos_f[:], pos_i[:]).then_inc(dve_ready, 1)
            dve.wait_ge(pt_full, pt_at["cols"] + 1)
            v.tensor_copy(col[:], pt[0][:, 0:28])
            v.tensor_copy(pos_col[:], pt[0][:, 32:32 + NT]).then_inc(pt_free_v, 1)
            dve.wait_ge(pt_full, pt_at["gains"] + 1)
            v.tensor_copy(gains[:], pt[1][:, 0:2 * HD]).then_inc(pt_free_v, 1)
            dve.drain()
            v.tensor_scalar(nx[:], pos_col[:], 0.0, None, ALU.add).then_inc(dve_ready, 1)
            for k in range(NF):
                v.tensor_scalar(angle[:, :, k], pos_col[:], float(np.float32(THETA ** (-2.0 * k / ROT))), None, ALU.mult)
            dve.drain()
            ang = angle[:].rearrange("p t f -> p (t f)")
            v.tensor_scalar(turns[:, 0, :], ang, float(1 / (2 * np.pi)), MAGIC, ALU.mult, ALU.add)
            v.tensor_scalar(turns[:, 1, :], ang, float(1 / (2 * np.pi)), 0.25, ALU.mult, ALU.add)
            dve.drain()
            v.tensor_scalar(turns[:, 1, :], turns[:, 1, :], MAGIC, None, ALU.add)
            dve.drain()
            v.tensor_scalar(turns[:], turns[:], MAGIC, None, ALU.subtract)
            dve.drain()
            for s in range(2):
                v.scalar_tensor_tensor(reduced[:, s, :], turns[:, s, :], -TWO_PI[0], ang, ALU.mult, ALU.add)
            for part in TWO_PI[1:]:
                dve.drain()
                v.scalar_tensor_tensor(reduced[:], turns[:], -part, reduced[:], ALU.mult, ALU.add)
            dve.drain()
            v.tensor_scalar(reduced[:, 1, :], reduced[:, 1, :], float(np.pi / 2), None, ALU.add)
            dve.drain()
            v.tensor_scalar(reduced[:], reduced[:], 3.1415925, -3.1415925, ALU.min, ALU.max).then_inc(dve_ready, 1)

            def rsqrt_step(y, mean, tmp):
                v.reciprocal(y, y)
                dve.drain()
                v.tensor_tensor(tmp, y, y, ALU.mult)
                dve.drain()
                v.tensor_tensor(tmp, tmp, mean, ALU.mult)
                dve.drain()
                v.tensor_scalar(tmp, tmp, -0.5, 1.5, ALU.mult, ALU.add)
                dve.drain()
                v.tensor_tensor(y, y, tmp, ALU.mult)
                dve.drain()

            def ada_products(i):
                for k in range(KD):
                    if k % (KD // 2) == 0:
                        dve.wait_ge(ada_in[2 * i + 2 * k // KD], 16)
                    c = c_silu[:, k:k + 1]
                    if k == 0:
                        v.tensor_scalar(ada_acc[:, i, :], ada_w[:, i, k, :], c, None, ALU.mult)
                    else:
                        dve.drain()
                        ins = v.scalar_tensor_tensor(ada_acc[:, i, :], ada_w[:, i, k, :], c, ada_acc[:, i, :],
                                                     ALU.mult, ALU.add)
                ins.then_inc(ada_sum, 1)
            dve.wait_ge(c_silu_done, 1)

            def mean_half(f):
                ts = slice(4 * f, 4 * f + 4)
                dve.wait_ge(ssx_done, NT // 2 if f else NT)
                v.tensor_scalar(ssx[:, ts], ssx[:, ts], 1.0 / D, EPS, ALU.mult, ALU.add).then_inc(dve_ready, 1)

            def rsqrt_half(f):
                ts = slice(4 * f, 4 * f + 4)
                dve.wait_ge(sqrt_done, 1 if f else 2)
                rsqrt_step(rx[:, ts], ssx[:, ts], nx[:, ts])
                v.tensor_copy(nx[:, ts], rx[:, ts]).then_inc(dve_ready, 1)
            mean_half(1)
            rsqrt_half(1)
            for i in range(1, 4):
                ada_products(i)
            dve.wait_ge(ps_full, 4)
            v.tensor_tensor(shift[:], ps[0][:, 0:2 * KD], col[:, 12:28], ALU.add).then_inc(ps_free_v, 1)
            dve.drain()
            v.tensor_scalar(gmul[:], shift[:, KD:2 * KD], 1.0, None, ALU.add)
            dve.drain()
            v.tensor_tensor(gmul[:], gmul[:], col[:, 0:KD], ALU.mult)
            dve.drain()
            def ht_lo(j):
                f, k = 1 - j // KD, j % KD
                tok = slice(f * HALF, (f + 1) * HALF)
                dve.wait_ge(hT_hi_done, j + 1)
                v.tensor_tensor(hT_lo[:, k, tok], h_raw[:, j % 4, :], hT_hi[:, k, tok].bitcast(F32),
                                ALU.subtract).then_inc(hT_lo_v, 1)
            for n in range(2 * KD + 2):
                if n == 2:
                    mean_half(0)
                if n == 4:
                    rsqrt_half(0)
                if n == KD:
                    ht_lo(n - 2)
                if n < 2 * KD:
                    k = n % KD
                    dve.wait_ge(pt_full, pt_at[("h", n)] + 1)
                    if n >= 4:
                        if n % 2 == 0:
                            dve.wait_ge(hT_lo_v, (n - 4) // 2 + 1)
                        else:
                            dve.wait_ge(hT_lo_p, (n - 5) // 2 + 1)
                    v.tensor_scalar(h_raw[:, n % 4, :], pt[pt_at[("h", n)] % 2][:], gmul[:, k:k + 1], shift[:, k:k + 1],
                                    ALU.mult, ALU.add).then_inc(h_raw_done, 1)
                    dve.wait_ge(h_raw_done, n + 1)
                    dve.sem_inc(pt_free_v, 1)
                if n >= 2 and n % 2 == 0 and n != KD:
                    ht_lo(n - 2)

            dve.wait_ge(trig_done, 1)
            sin, cos = (trig[:, s, :].rearrange("p (t f) -> p t f", f=NF) for s in range(2))
            v.tensor_copy(rot_c[:, :, 0:NF], cos)
            v.tensor_copy(rot_c[:, :, NF:ROT], cos)
            v.tensor_scalar(rot_s[:, :, 0:NF], sin, -1.0, None, ALU.mult)
            v.tensor_copy(rot_s[:, :, NF:ROT], sin)
            dve.drain()
            v.tensor_copy(nq[:, 0:1], rx[:, 0:1]).then_inc(trig_done, 1)
            dve.wait_ge(wg_lo_done, 1)
            dve.wait_ge(pp_free_a, pp_at[("kv", 0, 3)] + 1)
            ki, kk, vv = kr[:, :, KR_KI:KR_KI + HD], kr[:, :, KR_K:KR_K + HD], kr[:, :, KR_V:KR_V + HD]
            tmp_a = score[:, 0:NT * ROT].rearrange("p (t r) -> p t r", r=ROT)
            tmp_b = score[:, NT * ROT:2 * NT * ROT].rearrange("p (t r) -> p t r", r=ROT)

            def rope_keys(u):
                v.tensor_tensor(tmp_a, u[:, :, 0:ROT], rot_c[:], ALU.mult)
                v.tensor_tensor(tmp_b[:, :, 0:NF], u[:, :, NF:ROT], rot_s[:, :, 0:NF], ALU.mult)
                v.tensor_tensor(tmp_b[:, :, NF:ROT], u[:, :, 0:NF], rot_s[:, :, NF:ROT], ALU.mult)
                dve.drain()
                v.tensor_tensor(u[:, :, 0:ROT], tmp_a, tmp_b, ALU.add)
                dve.drain()

            def stack_keys(u):
                for s in range(2):
                    v.tensor_copy(kst[:, 0, :, s * HD:(s + 1) * HD], u)
                dve.drain()
                v.tensor_tensor(kst[:, 1, :, 0:HD], u, kst[:, 0, :, 0:HD].bitcast(F32), ALU.subtract)
                v.tensor_tensor(kst[:, 1, :, HD:2 * HD], u, kst[:, 0, :, HD:2 * HD].bitcast(F32),
                                ALU.subtract).then_inc(kst_ready, 1)
            rope_keys(ki)
            stack_keys(ki)
            v.tensor_scalar(w_idx[:], kr[:, :, KR_WI:KR_WI + H], IDX_SCALE, None, ALU.mult)
            v.tensor_copy(v2[:, :, 0:HD], vv)
            dve.drain()
            v.tensor_tensor(v2[:, :, HD:2 * HD], vv, v2[:, :, 0:HD].bitcast(F32), ALU.subtract)
            sq = score[:, 512:512 + NT * HD].rearrange("p (t d) -> p t d", d=HD)
            v.tensor_tensor(sq, kk, kk, ALU.mult)
            dve.drain()
            v.tensor_reduce(ssk[:], sq, AX.X, ALU.add)
            dve.drain()
            v.tensor_scalar(ssk[:], ssk[:], 1.0 / HD, EPS, ALU.mult, ALU.add).then_inc(var_ready, 1)
            dve.wait_ge(sqrt_done, 3)
            rsqrt_step(rk[:], ssk[:], nk[:])
            v.tensor_tensor(kk, kk, rk[:].unsqueeze(2).to_broadcast([P, NT, HD]), ALU.mult)
            dve.drain()
            v.tensor_tensor(kk, kk, gains[:, HD:2 * HD].unsqueeze(1).to_broadcast([P, NT, HD]), ALU.mult)
            dve.drain()
            rope_keys(kk)
            dve.wait_ge(pt_full, pt_at[("ki", 1, 1)] + 1)
            stack_keys(kk)
            for t in range(NT):
                dve.wait_ge(pp_free_a, pp_at[("q", 1, t)] + 1)
                sq = score[:, 512 * (1 + t % 2):512 * (2 + t % 2)]
                v.tensor_tensor(sq, q_all[:, t, :], q_all[:, t, :], ALU.mult)
                dve.drain()
                v.tensor_reduce(ssq[:, t * H:(t + 1) * H], sq.rearrange("p (h d) -> p h d", d=HD), AX.X, ALU.add)
            dve.drain()
            v.tensor_scalar(ssq[:], ssq[:], 1.0 / HD, EPS, ALU.mult, ALU.add).then_inc(var_ready, 1)

            def scale_query(t):
                qv = q_all[:, t, :].rearrange("p (h d) -> p h d", d=HD)
                v.tensor_tensor(qv, qv, rq[:, t * H:(t + 1) * H].unsqueeze(2).to_broadcast([P, H, HD]), ALU.mult)
                dve.drain()
                v.tensor_tensor(qv, qv, gains[:, 0:HD].unsqueeze(1).to_broadcast([P, H, HD]), ALU.mult).then_inc(q_scaled, 1)
            for b in range(FREE_BLOCKS, NT):
                s = score[:, score_at(b):score_at(b + 1)]
                for h in range(H):
                    n = (b - FREE_BLOCKS) * H + h
                    dve.wait_ge(ps_free_a, n + 1)
                    w = w_idx[:, b, h:h + 1]
                    if h == 0:
                        ins = v.tensor_scalar(s, rel[:, n % 2, 0:keys(b)], w, None, ALU.mult)
                    else:
                        dve.wait_ge(rel_used, n)
                        ins = v.scalar_tensor_tensor(s, rel[:, n % 2, 0:keys(b)], w, s, ALU.mult, ALU.add)
                    ins.then_inc(rel_used, 1)
                    if (b, h) == (FREE_BLOCKS, 2):
                        dve.wait_ge(sqrt_done, 4)
                        rsqrt_step(rq[:], ssq[:], nq[:])
                    if h in SCALED[b]:
                        scale_query(SCALED[b][h])
                dve.wait_ge(rel_used, (b - FREE_BLOCKS + 1) * H)
                dve.sem_inc(block_scored, 1)

            dve.wait_ge(masked, NSEL)
            dve.wait_ge(pt_free_a, pt_done[pt_at[("qi", NT - 1, 1)]][0])
            for s in range(4):
                dve.wait_ge(zb_spilled[s], 16 * 4)

            def count(at_least):
                for n in range(NSEL):
                    b = n + FREE_BLOCKS
                    least = at_least if at_least is not None else cand[:, n:n + 1].bitcast(F32)
                    if n and n % 2 == 0:
                        dve.drain()
                    v.tensor_scalar(junk[:, n % 2, 0:keys(b)], score[:, score_at(b):score_at(b + 1)], least, None,
                                    ALU.is_ge, ALU.add, accum_out=cnt[:, n:n + 1])
                dve.drain()
            count(0.0)
            v.tensor_scalar(thr[:], cnt[:], TOPK - 0.5, -1.0, ALU.is_lt, ALU.mult)
            dve.drain()
            v.tensor_scalar(cand[:], thr[:], bit_i[:, 0:1], None, ALU.bitwise_xor)
            dve.drain()
            with dve.Fori(0, 31) as k:
                count(None)
                v.tensor_scalar(accept[:], cnt[:], TOPK - 0.5, bit_f[:, bass.ds(k, 1)], ALU.is_ge, ALU.mult)
                dve.drain()
                v.scalar_tensor_tensor(cand[:], accept[:], bit_i[:, bass.ds(k + 1, 1)], thr[:],
                                       ALU.bitwise_xor, ALU.bitwise_xor)
                v.tensor_tensor(thr[:], thr[:], accept[:], ALU.bitwise_xor)
                dve.drain()

            dve.wait_ge(ya_hi, 2 * GROUPS)
            dve.wait_ge(ya_lo, 2 * GROUPS)
            for b in range(FREE_BLOCKS):
                if b:
                    v.memset(bias[:, bias_at(b):bias_at(b) + b * P], 0.0)
                v.tensor_copy(bias[:, bias_at(b) + b * P:bias_at(b + 1)], diag_bias[:])
            dve.drain()
            dve.sem_inc(bias_ready, 1)

            def mask_begin(b):
                n = b - FREE_BLOCKS
                t = thr[:, n:n + 1].bitcast(F32)
                s = score[:, score_at(b):score_at(b + 1)]
                own = bias[:, bias_at(b):bias_at(b + 1)]
                v.tensor_scalar(own, s, t, None, ALU.is_gt, ALU.add, accum_out=cnt[:, n:n + 1])
                v.tensor_scalar(eq[:, b % 2, 0:keys(b)], s, t, None, ALU.is_equal).then_inc(eq_ready, 1)
                dve.drain()
                v.tensor_scalar(need[:, b % 2:b % 2 + 1], cnt[:, n:n + 1], -1.0, float(TOPK), ALU.mult, ALU.add)
                dve.drain()

            def mask_end(b):
                n = b - FREE_BLOCKS
                dve.wait_ge(ps_full, ps_value(("cum", b)))
                o = ps[ps_at[("cum", b)] % 2]
                ties, own = eq[:, b % 2, 0:keys(b)], bias[:, bias_at(b):bias_at(b + 1)]
                v.scalar_tensor_tensor(ties, o[:, 0:keys(b)], need[:, b % 2:b % 2 + 1], ties,
                                       ALU.is_le, ALU.mult).then_inc(ps_free_v, 1)
                dve.drain()
                v.scalar_tensor_tensor(own, score[:, score_at(b):score_at(b + 1)], thr[:, n:n + 1].bitcast(F32), ties,
                                       ALU.is_gt, ALU.add)
                dve.drain()
                v.tensor_scalar(own, own, 1.0, -NEG_BIAS, ALU.subtract, ALU.mult).then_inc(bias_ready, 1)
                dve.drain()

            def pT_low(j):
                b = j // H
                if j >= 2:
                    dve.wait_ge(pv_done, j - 1)
                for g in range((b + 4) // 4):
                    t0, t1 = 4 * g, min(4 * g + 4, b + 1)
                    n = pt_at[("PT", j, g)]
                    dve.wait_ge(pt_free_a, pt_done[n][0])
                    v.tensor_tensor(pT[:, j % 2, t0:t1, 1, :], pt[n % 2][:, 0:(t1 - t0) * P].rearrange(
                        "p (t q) -> p t q", q=P), pT[:, j % 2, t0:t1, 0, :].bitcast(F32),
                        ALU.subtract).then_inc(pt_free_v, 1)

            def output_parts(j):
                dve.wait_ge(pv_done, j + 1)
                if j % 4 == 0 and j >= 8:
                    dve.wait_ge(pt_full, pt_at[("out", j // 4 - 2)] + 1)
                v.tensor_reduce(oT[:, j % 8, :], pp[0][:, 0:2 * P].rearrange("p (s q) -> p q s", q=P), AX.X,
                                ALU.add).then_inc(pp_free_v, 1)

            def outputs(n):
                b, f = n // 2, n % 2
                r = (b % 2) * H + 4 * f
                v.reciprocal(row_inv[:], row_sum[:, r:r + 4])
                dve.drain()
                dve.wait_ge(pt_full, pt_at[("out", n)] + 1)
                y = y_row[:, b, 4 * f * HD:4 * (f + 1) * HD].rearrange("p (h d) -> p h d", d=HD)
                v.tensor_tensor(y, pt[pt_at[("out", n)] % 2][:, 0:4 * HD].rearrange("p (h d) -> p h d", d=HD),
                                row_inv[:].unsqueeze(2).to_broadcast([P, 4, HD]), ALU.mult).then_inc(o_sum, 1)
                dve.wait_ge(o_sum, n + 1)
                dve.sem_inc(pt_free_v, 1)

            def yb_low(b):
                if b == NT - 1:
                    n = pt_at[("yb", b)]
                    dve.wait_ge(pt_free_a, pt_done[n][0])
                    o, freed = pt[n % 2], pt_free_v
                else:
                    n = pp_at[("yb", b)]
                    dve.wait_ge(pp_free_a, pp_done[n][0])
                    o, freed = pp[pp_bank[n]], pp_free_v
                v.tensor_tensor(yT_lo[:, :, b * P:(b + 1) * P], o[:].rearrange("p (k q) -> p k q", q=P),
                                yT_hi[:, :, b * P:(b + 1) * P].bitcast(F32), ALU.subtract).then_inc(freed, 1)

            for b in range(FREE_BLOCKS, NT + 1):
                if b < NT:
                    mask_begin(b)
                if b > FREE_BLOCKS:
                    mask_end(b - 1)
            dve.wait_ge(pp_full, PP_HT)
            def gate_add(g, k):
                c = c_silu[:, k:k + 1]
                if k == 0:
                    dve.wait_ge(gate_in, 16 * GATE_LOADS * (g + 1))
                    if g:
                        dve.wait_ge(pt_full, pt_at[("gate", g - 1)] + 1)
                    v.tensor_scalar(gate_acc[:], gate_w[:, k, :], c, None, ALU.mult)
                else:
                    v.scalar_tensor_tensor(gate_acc[:], gate_w[:, k, :], c, gate_acc[:], ALU.mult, ALU.add)
                dve.drain()
                if k == KD - 1:
                    v.tensor_tensor(gate_acc[0:1, :], gate_acc[0:1, :], gate[0:1, g * HALF:(g + 1) * HALF],
                                    ALU.add).then_inc(gate_sum, 1)

            def merge(n):
                i, m, f = UNITS_B[n]
                u = pp_at[("wb", i, (m, f))]
                dve.wait_ge(pp_full, pp_sig[u])
                dve.wait_ge(e_loaded[n % 4], 32 * (n // 4 + 1))
                if n >= 4:
                    dve.wait_ge(mT_lo_done, n - 3)
                v.tensor_tensor(m_raw[:, n % 4, :], pp[pp_bank[u]][:], e_in[:, 0, n % 4, :], ALU.mult).then_inc(pp_free_v, 1)
                dve.drain()
                v.tensor_tensor(m_raw[:, n % 4, :], m_raw[:, n % 4, :], e_in[:, 1, n % 4, :], ALU.add).then_inc(m_raw_done, 1)
                if 0 <= n - 7 < KD:
                    gate_add(0, n - 7)
            for i in range(HEADS + 6):
                if 0 <= i - 5 < HEADS and (i - 5) % 4 == 3:
                    outputs((i - 5) // 4)
                if 0 <= i - 4 < HEADS:
                    output_parts(i - 4)
                if 0 <= i - 2 < HEADS:
                    pT_low(i - 2)
                if i < HEADS:
                    b = i // H
                    dve.wait_ge(ps_full, ps_value(("S", i)))
                    if i >= 2:
                        dve.wait_ge(prob_done, i - 1)
                    v.tensor_tensor_reduce(logit[:, i % 2, 0:keys(b)], ps[ps_at[("S", i)] % 2][:, 0:keys(b)],
                                           bias[:, bias_at(b):bias_at(b + 1)], -ATT_SCALE, 3.0e38, ALU.add, ALU.min,
                                           neg_max[:, i % 2:i % 2 + 1]).then_inc(logit_done, 1)
                    dve.wait_ge(logit_done, i + 1)
                    dve.sem_inc(ps_free_v, 1)
                if i == HEADS + 5:
                    for s in range(4):
                        dve.wait_ge(ma_out[s], 16 * 4)
                    merge(0)
                if i in YB_STEP:
                    yb_low(YB_STEP[i])

            for n in range(1, 16):
                merge(n)
            for n in range(4 * NT):
                i = n // NT
                u = pp_at[("wo", i, n % NT)]
                if n % (2 * NT) == 0:
                    dve.wait_ge(pt_free_a, pt_done[pt_at[("gate", n // (2 * NT))]][0])
                dve.wait_ge(pp_full, pp_sig[u])
                dve.wait_ge(x_row_in[n % 4], 16 * (n // 4 + 1))
                if n >= 4:
                    dve.wait_ge(stored[n % 4], 16 * (n // 4))
                v.tensor_tensor(o_row[:, n % 4, :], pp[pp_bank[u]][:, 0:CW], gate[:, i * CW:(i + 1) * CW],
                                ALU.mult).then_inc(pp_free_v, 1)
                dve.drain()
                v.tensor_tensor(o_row[:, n % 4, :], o_row[:, n % 4, :], x_row[:, n % 4, :], ALU.add).then_inc(o_row_done, 1)
                if 0 <= n - 5 < KD:
                    gate_add(1, n - 5)


_INS = ["x", "c", "positions", "w_ada", "b_ada", "norm_gain", "w_in", "w_pool_group", "pool_scale",
        "q_norm_gain", "k_norm_gain", "w_branch_a", "w_branch_b", "w_out"]


def kernel(**inputs):
    import concourse.bacc as bacc
    from concourse.bass_utils import run_bass_kernel_spmd

    nc = bacc.Bacc("TRN2", target_bir_lowering=False, num_devices=1)
    arrays, args = {}, []
    for name in _INS:
        a = np.ascontiguousarray(inputs[name])
        arrays[f"in_{name}"] = a
        args.append(nc.dram_tensor(f"in_{name}", a.shape, mybir.dt.from_np(a.dtype), kind="ExternalInput").ap())
    args.append(nc.dram_tensor("out", (1, L, D), F32, kind="ExternalOutput").ap())
    hybrid_layer(nc, *args)
    r = run_bass_kernel_spmd(nc, [arrays], core_ids=[0])
    return r.results[0]["out"]
```
